# Optimizing a Trainium2 kernel written in Bass

```python
import math
import jax, jax.numpy as jnp
from jax import lax
import numpy as np

D_MODEL = 1024
BATCH = 1
SEQ = 512
DEPTH = 1
DEC_BATCH = 1
DEC_SEQ = 256
PAST_LEN = 128

D_MIX = D_MODEL
ATTN_WIDTH = D_MIX // 2
POOL_WIDTH = D_MIX - ATTN_WIDTH
V_HEAD_DIM = 128
MLA_HEADS = ATTN_WIDTH // V_HEAD_DIM
QK_NOPE_DIM = 128
QK_ROPE_DIM = 64
QK_DIM = QK_NOPE_DIM + QK_ROPE_DIM
Q_LORA_RANK = 384
KV_LORA_RANK = 256
ROPE_THETA = 10000.0
Q_BLOCK = 128
POOL_WINDOWS = (2, 4, 8, 16)
N_POOL_GROUPS = len(POOL_WINDOWS)
POOL_CH = POOL_WIDTH // N_POOL_GROUPS
IN_WIDTH = Q_LORA_RANK + KV_LORA_RANK + QK_ROPE_DIM + POOL_WIDTH
N_GROUPS = 4
EXPERTS_PER_GROUP = 8
N_EXPERTS = N_GROUPS * EXPERTS_PER_GROUP
TOP_K = 2
EXPERT_HIDDEN = 256
EPS = 1e-6

kernel_name = "hymba_mla_pool_hmoe_encoder"

def rms_norm(x, g):
    xf = x.astype(jnp.float32)
    y = xf * lax.rsqrt(jnp.mean(xf * xf, axis=-1, keepdims=True) + EPS)
    return (y * g.astype(jnp.float32)).astype(x.dtype)

def rope_tables(seq):
    inv_freq = 1.0 / (ROPE_THETA ** (jnp.arange(0, QK_ROPE_DIM, 2, dtype=jnp.float32) / QK_ROPE_DIM))
    ang = jnp.arange(seq, dtype=jnp.float32)[:, None] * inv_freq[None, :]
    emb = jnp.concatenate([ang, ang], axis=-1)
    return jnp.cos(emb)[:, None, :], jnp.sin(emb)[:, None, :]

def apply_rope(x, cos, sin):
    xf = x.astype(jnp.float32)
    x1, x2 = jnp.split(xf, 2, axis=-1)
    rot = jnp.concatenate([-x2, x1], axis=-1)
    return (xf * cos + rot * sin).astype(x.dtype)

def bidirectional_attention(q, k, v):
    B, S, H, Dq = q.shape
    nb = S // Q_BLOCK
    qb = q.reshape(B, nb, Q_BLOCK, H, Dq).transpose(1, 0, 2, 3, 4)
    scale = QK_DIM ** -0.5

    def one_block(qblk):
        s = jnp.einsum('bqhd,bkhd->bhqk', qblk, k).astype(jnp.float32) * scale
        p = jax.nn.softmax(s, axis=-1)
        return jnp.einsum('bhqk,bkhd->bqhd', p.astype(v.dtype), v)

    o = lax.map(one_block, qb)
    return o.transpose(1, 0, 2, 3, 4).reshape(B, S, H * V_HEAD_DIM)

def multi_scale_pool(u, w_pool, pool_scale):
    B, S, _ = u.shape
    ug = u.reshape(B, S, N_POOL_GROUPS, POOL_CH)
    uf = ug.astype(jnp.float32)
    c = jnp.cumsum(uf, axis=1)
    c = jnp.concatenate([jnp.zeros((B, 1, N_POOL_GROUPS, POOL_CH), jnp.float32), c], axis=1)
    wins = np.array(POOL_WINDOWS, dtype=np.int32)
    lo = jnp.asarray(wins // 2)
    hi = jnp.asarray(wins - wins // 2 - 1)
    t = jnp.arange(S, dtype=jnp.int32)
    idx_hi = jnp.clip(t[:, None] + hi[None, :] + 1, 0, S)
    idx_lo = jnp.clip(t[:, None] - lo[None, :], 0, S)
    s_hi = jnp.take_along_axis(c, idx_hi[None, :, :, None], axis=1)
    s_lo = jnp.take_along_axis(c, idx_lo[None, :, :, None], axis=1)
    count = (idx_hi - idx_lo).astype(jnp.float32)[None, :, :, None]
    d = ((s_hi - s_lo) / count - uf).astype(u.dtype)
    mixed = jnp.einsum('bsgc,gcd->bsgd', d, w_pool).reshape(B, S, POOL_WIDTH)
    return mixed * pool_scale

def token_mixer(a, w_in, g_q_lat, g_kv_lat, w_uq, w_ukv, g_q_head, g_k_head, w_pool, pool_scale, w_out):
    B, S, _ = a.shape
    p = a @ w_in
    c_q, c_kv, k_r, u = jnp.split(
        p, [Q_LORA_RANK, Q_LORA_RANK + KV_LORA_RANK, Q_LORA_RANK + KV_LORA_RANK + QK_ROPE_DIM], axis=-1)
    c_q = rms_norm(c_q, g_q_lat)
    c_kv = rms_norm(c_kv, g_kv_lat)
    q = (c_q @ w_uq).reshape(B, S, MLA_HEADS, QK_DIM)
    kv = (c_kv @ w_ukv).reshape(B, S, MLA_HEADS, QK_NOPE_DIM + V_HEAD_DIM)
    k_nope, v = jnp.split(kv, [QK_NOPE_DIM], axis=-1)
    k_rope = jnp.broadcast_to(k_r[:, :, None, :], (B, S, MLA_HEADS, QK_ROPE_DIM))
    k = jnp.concatenate([k_nope, k_rope], axis=-1)
    q = rms_norm(q, g_q_head)
    k = rms_norm(k, g_k_head)
    cos, sin = rope_tables(S)
    q = jnp.concatenate([q[..., :QK_NOPE_DIM], apply_rope(q[..., QK_NOPE_DIM:], cos, sin)], axis=-1)
    k = jnp.concatenate([k[..., :QK_NOPE_DIM], apply_rope(k[..., QK_NOPE_DIM:], cos, sin)], axis=-1)
    attn = bidirectional_attention(q, k, v)
    pool = multi_scale_pool(u, w_pool, pool_scale)
    return jnp.concatenate([attn, pool], axis=-1) @ w_out

def hier_moe(a, w_group_router, b_group_router, w_expert_router, b_expert_router, w_gate, w_up, w_down):
    B, S, D = a.shape
    T = B * S
    x = a.reshape(T, D)
    gp = jax.nn.softmax((x @ w_group_router).astype(jnp.float32) + b_group_router.astype(jnp.float32), axis=-1)
    g_val, g_idx = lax.top_k(gp, 1)
    el = ((x @ w_expert_router).astype(jnp.float32) + b_expert_router.astype(jnp.float32))
    el = el.reshape(T, N_GROUPS, EXPERTS_PER_GROUP)
    el_sel = jnp.take_along_axis(el, g_idx[:, :, None], axis=1)[:, 0]
    ep = jax.nn.softmax(el_sel, axis=-1)
    e_val, e_idx = lax.top_k(ep, TOP_K)
    e_val = e_val / jnp.sum(e_val, axis=-1, keepdims=True)
    gate = g_val * e_val
    expert_id = g_idx * EXPERTS_PER_GROUP + e_idx
    combine = jnp.sum(jax.nn.one_hot(expert_id, N_EXPERTS, dtype=jnp.float32) * gate[..., None], axis=1)
    y = jnp.zeros((T, D), jnp.float32)
    for e in range(N_EXPERTS):
        hdn = jax.nn.silu(x @ w_gate[e]) * (x @ w_up[e])
        y = y + combine[:, e:e + 1] * (hdn @ w_down[e]).astype(jnp.float32)
    return y.astype(a.dtype).reshape(B, S, D)

def encoder(x, g_attn_norm, w_in, g_q_lat, g_kv_lat, w_uq, w_ukv, g_q_head, g_k_head, w_pool, pool_scale,
            w_out, g_ffn_norm, w_group_router, b_group_router, w_expert_router, b_expert_router,
            w_gate, w_up, w_down):
    for l in range(DEPTH):
        h = x + token_mixer(rms_norm(x, g_attn_norm[l]), w_in[l], g_q_lat[l], g_kv_lat[l], w_uq[l], w_ukv[l],
                            g_q_head[l], g_k_head[l], w_pool[l], pool_scale[l], w_out[l])
        x = h + hier_moe(rms_norm(h, g_ffn_norm[l]), w_group_router[l], b_group_router[l],
                         w_expert_router[l], b_expert_router[l], w_gate[l], w_up[l], w_down[l])
    return x

def setup_inputs(seed: int = 0) -> dict:
    key = jax.random.key(seed)
    ks = jax.random.split(key, 22)
    f32 = jnp.float32

    def nrm(k, shape, fan_in):
        return jax.random.normal(k, shape, f32) * (fan_in ** -0.5)

    def gain(k, shape):
        return 1.0 + 0.1 * jax.random.normal(k, shape, f32)

    return {
        "x_prompt": jax.random.normal(ks[0], (BATCH, SEQ, D_MODEL), f32),
        "x_sample": jax.random.normal(ks[1], (DEC_BATCH, DEC_SEQ, D_MODEL), f32),
        "g_attn_norm": gain(ks[2], (DEPTH, D_MODEL)),
        "w_in": nrm(ks[3], (DEPTH, D_MODEL, IN_WIDTH), D_MODEL),
        "g_q_lat": gain(ks[4], (DEPTH, Q_LORA_RANK)),
        "g_kv_lat": gain(ks[5], (DEPTH, KV_LORA_RANK)),
        "w_uq": nrm(ks[6], (DEPTH, Q_LORA_RANK, MLA_HEADS * QK_DIM), Q_LORA_RANK),
        "w_ukv": nrm(ks[7], (DEPTH, KV_LORA_RANK, MLA_HEADS * (QK_NOPE_DIM + V_HEAD_DIM)), KV_LORA_RANK),
        "g_q_head": gain(ks[8], (DEPTH, QK_DIM)),
        "g_k_head": gain(ks[9], (DEPTH, QK_DIM)),
        "w_pool": nrm(ks[10], (DEPTH, N_POOL_GROUPS, POOL_CH, POOL_CH), POOL_CH),
        "pool_scale": gain(ks[11], (DEPTH, POOL_WIDTH)),
        "w_out": nrm(ks[12], (DEPTH, D_MIX, D_MODEL), D_MIX),
        "g_ffn_norm": gain(ks[13], (DEPTH, D_MODEL)),
        "w_group_router": nrm(ks[14], (DEPTH, D_MODEL, N_GROUPS), D_MODEL),
        "b_group_router": 0.01 * jax.random.normal(ks[15], (DEPTH, N_GROUPS), f32),
        "w_expert_router": nrm(ks[16], (DEPTH, D_MODEL, N_EXPERTS), D_MODEL),
        "b_expert_router": 0.01 * jax.random.normal(ks[17], (DEPTH, N_EXPERTS), f32),
        "w_gate": nrm(ks[18], (DEPTH, N_EXPERTS, D_MODEL, EXPERT_HIDDEN), D_MODEL),
        "w_up": nrm(ks[19], (DEPTH, N_EXPERTS, D_MODEL, EXPERT_HIDDEN), D_MODEL),
        "w_down": nrm(ks[20], (DEPTH, N_EXPERTS, EXPERT_HIDDEN, D_MODEL), EXPERT_HIDDEN),
    }

def reference(x_prompt, x_sample, g_attn_norm, w_in, g_q_lat, g_kv_lat, w_uq, w_ukv, g_q_head, g_k_head,
              w_pool, pool_scale, w_out, g_ffn_norm, w_group_router, b_group_router, w_expert_router,
              b_expert_router, w_gate, w_up, w_down):
    y_prompt = encoder(x_prompt, g_attn_norm, w_in, g_q_lat, g_kv_lat, w_uq, w_ukv, g_q_head, g_k_head,
                       w_pool, pool_scale, w_out, g_ffn_norm, w_group_router, b_group_router,
                       w_expert_router, b_expert_router, w_gate, w_up, w_down)
    y_sample = encoder(x_sample, g_attn_norm, w_in, g_q_lat, g_kv_lat, w_uq, w_ukv, g_q_head, g_k_head,
                       w_pool, pool_scale, w_out, g_ffn_norm, w_group_router, b_group_router,
                       w_expert_router, b_expert_router, w_gate, w_up, w_down)
    return (y_prompt, y_sample)


_drawn_inputs = setup_inputs


def setup_inputs(seed=0):
    import zlib

    import numpy as np

    out = dict(_drawn_inputs(seed))
    spreads = {}
    factors = {'g_q_lat': 3.152,
     'g_q_head': 3.731,
     'g_k_head': 3.481,
     'b_group_router': 46.914,
     'b_expert_router': 4.928}
    for name, (base, spread) in spreads.items():
        noise = np.random.default_rng([zlib.crc32(name.encode()), seed]).standard_normal(out[name].shape)
        drawn = base * np.exp(spread * noise) if base else spread * noise
        out[name] = __import__('jax').numpy.asarray(drawn.astype(out[name].dtype))
    for name, factor in factors.items():
        out[name] = (out[name] * factor).astype(out[name].dtype)
    return out
```

```python
from contextlib import ExitStack

import numpy as np

import concourse.bass as bass
from concourse import mybir
from concourse.alu_op_type import AluOpType as ALU

F32 = mybir.dt.float32
BF16 = mybir.dt.bfloat16
I32 = mybir.dt.int32
U32 = mybir.dt.uint32
ACT = mybir.ActivationFunctionType
AX = mybir.AxisListType

P = 128
D = 1024
KD = D // P
SEQS = (512, 256)
T = sum(SEQS)
NT = T // P
FIRST = (0, SEQS[0] // P)
TILES = tuple(s // P for s in SEQS)
H = 4
DN, DR, DV = 128, 64, 128
DQK = DN + DR
RQ, RKV = 384, 256
KQ, KKV = RQ // P, RKV // P
NU = 512
NG, GC = 4, 128
IN_W = RQ + RKV + DR + NU
WINDOWS = (2, 4, 8, 16)
HALO = max(WINDOWS) // 2
BANDW = P + 2 * HALO
EG, EPG = 4, 8
E = EG * EPG
FH = 256
LANE = 64
PAIRS = E // 2
PASSES = T // LANE
BLOCK = 2 * LANE * PAIRS
ROW = D + E
EPS = 1e-6
SCALE = float(DQK) ** -0.5
BIG = 1e30

C_ID, C_LTRI, C_COS, C_SIN = 0, P, 2 * P, 2 * P + 4 * DR
C_IOTA = C_SIN + 4 * DR
C_EBASE = C_IOTA + E
C_W = C_EBASE + E


def host_constants():
    c = np.zeros((P, C_W), np.float32)
    c[:, C_ID:C_ID + P] = np.eye(P)
    c[:, C_LTRI:C_LTRI + P] = np.triu(np.ones((P, P)), 1)
    inv = (1.0 / (np.float32(10000.0) ** (np.arange(0, DR, 2, dtype=np.float32) / np.float32(DR)))).astype(np.float32)
    pos = np.arange(max(SEQS), dtype=np.float32)
    ang = (pos[:, None] * inv[None, :]).astype(np.float32)
    cos = np.concatenate([np.cos(ang)] * 2, -1).reshape(-1, P, DR)
    sin = np.concatenate([-np.sin(ang), np.sin(ang)], -1).reshape(-1, P, DR)
    c[:, C_COS:C_COS + 4 * DR] = cos.transpose(1, 0, 2).reshape(P, -1)
    c[:, C_SIN:C_SIN + 4 * DR] = sin.transpose(1, 0, 2).reshape(P, -1)
    e = np.arange(E)
    c[:, C_IOTA:C_IOTA + E] = e
    c[:, C_EBASE:C_EBASE + E] = (e // PAIRS) * (LANE * PAIRS) + e % PAIRS
    band = np.zeros((P, NG, 3, BANDW), np.float32)
    s = 3 * P
    for g, w in enumerate(WINDOWS):
        full = np.zeros((s, s), np.float64)
        for t in range(s):
            lo, hi = max(t - w // 2, 0), min(t + w - w // 2, s)
            full[lo:hi, t] = 1.0 / (hi - lo)
            full[t, t] -= 1.0
        for kind in range(3):
            for col in range(BANDW):
                t = kind * P - HALO + col
                if 0 <= t < s:
                    band[:, g, kind, col] = full[kind * P:(kind + 1) * P, t]
    tokens = (np.arange(P)[:, None] + P * np.arange(NT)[None, :]).astype(np.int32)
    slots = np.broadcast_to((T + np.arange(2 * LANE))[None, :, None], (PASSES, 2 * LANE, PAIRS))
    slots = np.ascontiguousarray(slots.reshape(-1, 1).astype(np.int32))
    zeros = np.zeros((P, ROW), np.float32)
    return {"consts": c, "band": band.reshape(P, -1), "tokens": tokens, "slots": slots, "zeros": zeros}


def build(nc, a, out):
    table = nc.dram_tensor("token_rows", [T + P, ROW], F32, kind="Internal").ap()
    slot_table = nc.dram_tensor("slot_tokens", [PASSES * BLOCK, 1], I32, kind="Internal").ap()

    ctx = ExitStack()
    with ctx:
        def sem(name):
            return ctx.enter_context(nc.semaphore(name))

        def region(size, *groups):
            got = []
            for group in groups:
                with ExitStack() as one:
                    used = 0
                    for name, shape, dt in group:
                        got.append(one.enter_context(nc.sbuf_tensor(name, shape, dt)))
                        used += (int(np.prod(shape[1:])) * (2 if dt == BF16 else 4) + 31) // 32 * 32
                    assert used <= size, (group[0][0], used, size)
            hold = group[0][0] + "_region"
            ctx.enter_context(nc.sbuf_tensor(hold, [P, size // 4], F32))
            return got

        (consts, bf_consts, g_attn, g_lat, g_nope, g_pool, r_bias, tok_ids, neg_half, idx_pos, counts_i,
         m_sum, w_router) = region(
            6 * 1024,
            [("consts_sb", [P, C_W], F32), ("bf_consts", [P, 2, P], BF16), ("g_attn", [P, KD], F32),
             ("g_lat", [P, KQ + KKV], F32), ("g_nope", [P, 2], F32), ("g_pool", [P, NG], F32),
             ("r_bias", [EG + E, 1], F32), ("tok_ids", [P, NT], I32), ("neg_half", [P, 8], F32),
             ("idx_pos", [P, NT, 2], I32), ("counts_i", [1, 4, PAIRS], I32), ("m_sum", [P, 2, E], BF16),
             ("w_router", [P, KD, EG + E], F32)])
        W_BYTES = 2 * (2 * KD * FH + 2 * D) * 4
        (w0,) = region(W_BYTES, [("expert_w0", [P, 2, 3, 2 * D], F32)])
        qT, kT, g_rows, more_rows = region(
            2 * H * T * 4,
            [("qT", [P, H, T], F32), ("kT", [P, H, T], F32)],
            [("g_rows", [P, 2, ROW], F32), ("ov_rows", [P, ROW], F32)])
        rT, v_sb, u_sb, x_res, h_sb, rows, a2T, g_ffn, route_f, route_u, h_junk = region(
            3 * H * T * 4,
            [("rT", [P, 4, T], F32), ("v_sb", [P, NT, H * DV], F32), ("u_sb", [P, NT, NU], F32)],
            [("x_res", [P, D], F32), ("h_sb", [P, 2, D], F32), ("rows", [P, 2, ROW], F32),
             ("a2T", [P, KD, P], F32), ("g_ffn", [P, D], F32), ("route_f", [P, 420], F32),
             ("route_u", [P, 24], U32), ("h_junk", [P, D], F32)])
        (w_in, w_out, xT, s_act, hid, hT, y_sb, idx_all, idx_now, gate) = region(
            KD * IN_W * 4,
            [("w_in_sb", [P, KD, IN_W], F32)],
            [("w_out_sb", [P, KD, D], F32)],
            [("xT", [P, 2, KD, P], F32), ("s_act", [P, 2, FH], F32), ("hid", [P, 2, 2, P], F32),
             ("hT", [P, 2, 2, P], F32), ("y_sb", [P, 3, D], F32), ("idx_all", [P, PAIRS], I32),
             ("idx_now", [P, 5], I32), ("gate", [P, 3], F32)])
        (w_uq, w_ukv, x_sb, xn, aT, cn, cT, junk, q_n, q_x, q_r, k_n, k_raw, k_r, rope_t, rope_k, rope_tab, stats,
         p_sb, pT, dT, band, w_pool, a_stat, w1) = region(
            56064,
            [("w_uq_sb", [P, KQ, H * DQK], F32), ("w_ukv_sb", [P, KKV, H * (DN + DV)], F32),
             ("x_sb", [P, 2, D], F32), ("xn", [P, KD, P], F32), ("aT", [P, KD, P], F32),
             ("cn", [P, KQ + KKV, P], F32), ("cT", [P, KQ + KKV, P], F32), ("junk", [P, H * DQK], F32),
             ("q_n", [P, H, DN], F32), ("q_x", [P, H, DR], F32), ("q_r", [P, H, DR], F32),
             ("k_n", [P, H, DN], F32), ("k_raw", [P, DR], F32), ("k_r", [P, H, DR], F32),
             ("rope_t", [P, 2, H, DR], F32), ("rope_k", [P, DR], F32), ("rope_tab", [P, 4, 4, DR], F32),
             ("stats", [P, 48], F32)],
            [("p_sb", [P, 4, 512], F32), ("pT", [P, 2, 4, 512], F32), ("dT", [P, 2, T], F32),
             ("band_sb", [P, NG, 3, BANDW], F32), ("w_pool_sb", [P, NG, GC], F32), ("a_stat", [P, 4, 4], F32)],
            [("expert_w1", [P, 2, 3, 2 * D], F32)])
        weights = (w0, w1)
        g_rope = q_x

        ps = ctx.enter_context(nc.psum_tensor("ps", [P, 8, 512], F32))

        ident = consts[:, C_ID:C_ID + P]
        iota = consts[:, C_IOTA:C_IOTA + E]
        ebase = consts[:, C_EBASE:C_EBASE + E]
        ones_bf, ltri_bf = bf_consts[:, 0, :], bf_consts[:, 1, :]

        consts_in, gains_in, setup_dram = sem("consts_in"), sem("gains_in"), sem("setup_dram")
        x_in = (sem("x_in0"), sem("x_in1"))
        w_in_in = [sem(f"w_in_in{n}") for n in range(3)]
        w_up_in, w_out_in, pool_in = sem("w_up_in"), sem("w_out_in"), sem("pool_in")
        x_res_in, g_ffn_in = sem("x_res_in"), sem("g_ffn_in")
        gu_in = (sem("gate_up_in0"), sem("gate_up_in1"))
        dn_in = (sem("down_in0"), sem("down_in1"))
        neg_half_set, tables_set, bf_set = sem("neg_half_set"), sem("tables_set"), sem("bf_set")
        x_sq, x_ms, x_rstd, xn_done = sem("x_sq"), sem("x_ms"), sem("x_rstd"), sem("xn_done")
        x_tr, aT_done = sem("x_tr"), sem("aT_done")
        p1_done, p2_done, p3_done = sem("p1_done"), sem("p2_done"), sem("p3_done")
        c_sq, c_ms, c_rstd, cn_done, k_raw_done = sem("c_sq"), sem("c_ms"), sem("c_rstd"), sem("cn_done"), sem("k_raw_done")
        c_tr, cT_done, u_done = sem("c_tr"), sem("cT_done"), sem("u_done")
        q_mm, kv_mm, q_sq, q_ss, q_ms, q_rstd = (sem(n) for n in ("q_mm", "kv_mm", "q_sq", "q_ss", "q_ms", "q_rstd"))
        k_sq, k_ss, k_ms, k_eps, k_rstd, v_done = (sem(n) for n in ("k_sq", "k_ss", "k_ms", "k_eps", "k_rstd", "v_done"))
        qn_done, qx_done, kn_done, rope_step, qr_done, kr_done = (
            sem(n) for n in ("qn_done", "qx_done", "kn_done", "rope_step", "qr_done", "kr_done"))
        qn_tr, kn_tr, r_tr, qT_done, kT_done, rT_done = (
            sem(n) for n in ("qn_tr", "kn_tr", "r_tr", "qT_done", "kT_done", "rT_done"))
        s_ready, row_max, neg_max, exp_done, recip_done, p_done, p_tr = (
            sem(n) for n in ("s_ready", "row_max", "neg_max", "exp_done", "recip_done", "p_done", "p_tr"))
        pT_act, pT_dve = sem("pT_act"), sem("pT_dve")
        pv_done, o_act, o_dve = sem("pv_done"), sem("o_act"), sem("o_dve")
        d_mm, dT_done, mix_mm, mix_done = sem("d_mm"), sem("dT_done"), sem("mix_mm"), sem("mix_done")
        o_mm, h_done, h_sq, h_ms, h_rstd, a2_done = (sem(n) for n in ("o_mm", "h_done", "h_sq", "h_ms", "h_rstd", "a2_done"))
        a2_tr, a2T_done, lg_mm, lg_bias, lg_tr = (sem(n) for n in ("a2_tr", "a2T_done", "lg_mm", "lg_bias", "lg_tr"))
        route_step, g_exp, e_exp, neg_g, e_diff = (sem(n) for n in ("route_step", "g_exp", "e_exp", "neg_g", "e_diff"))
        mask_done, rank_mm, pos_done, gates_done = (sem(n) for n in ("mask_done", "rank_mm", "pos_done", "gates_done"))
        h_stored, rows_stored, slots_stored = sem("h_stored"), sem("rows_stored"), sem("slots_stored")
        total_mm, counts_done = sem("total_mm"), sem("counts_done")
        idx_in, idx_set = sem("idx_in"), sem("idx_set")

        class PassSignals:

            def __init__(self, prefix, o):
                self.o = o
                self.gathered0, self.gathered1 = sem(prefix + "gathered0"), sem(prefix + "gathered1")
                self.x_tr, self.x_act, self.x_dve = sem(prefix + "x_tr"), sem(prefix + "x_act"), sem(prefix + "x_dve")
                self.gu_mm, self.silu_done = sem(prefix + "gu_mm"), sem(prefix + "silu_done")
                self.gate_done, self.hid_done = sem(prefix + "gate_done"), sem(prefix + "hid_done")
                self.h_tr, self.hT_done, self.y_mm = sem(prefix + "h_tr"), sem(prefix + "hT_done"), sem(prefix + "y_mm")
                self.y_act, self.y_dve, self.added = sem(prefix + "y_act"), sem(prefix + "y_dve"), sem(prefix + "added")

        main, over = PassSignals("main_", 0), PassSignals("more_", 1)
        pair_done = sem("pair_done")
        dma_go = sem("dma_go")
        over_idx_in = sem("more_idx_in")

        def w_gu(b, lane, k):
            return weights[b][:, lane, 0:2, k * FH:(k + 1) * FH]

        def w_dn(b, lane, k, n):
            return weights[b][:, lane, 2, k * D + n * 512:k * D + (n + 1) * 512]

        units = [(s, hp, qt) for s in range(2) for hp in range(2) for qt in range(TILES[s])]
        last_of_head = [m for m, (s, hp, qt) in enumerate(units) if qt == TILES[s] - 1]

        def x_dram(i):
            s = 0 if i < FIRST[1] else 1
            r = (i - FIRST[s]) * P
            return a["x_prompt" if s == 0 else "x_sample"][0, r:r + P, :]

        def load_pair(sp, j, b):
            for lane in range(2):
                e = PAIRS * lane + j
                for n, name in enumerate(("w_gate", "w_up")):
                    src = a[name][0, bass.ds(e, 1)].rearrange("e (p k) f -> p (e k f)", k=KD)
                    sp.dma_start(weights[b][:, lane, n, :], src).then_inc(gu_in[b], 16)
            for lane in range(2):
                e = PAIRS * lane + j
                src = a["w_down"][0, bass.ds(e, 1)].rearrange("e (p k) d -> p (e k d)", k=2)
                sp.dma_start(weights[b][:, lane, 2, :], src).then_inc(dn_in[b], 16)

        def pe_y_free(pe, j):
            if isinstance(j, int) and j == 0:
                return
            pe.wait_ge(main.y_act, j)
            pe.wait_ge(main.y_dve, j)

        def run_pairs(eng, pair):
            pair(0, 0, 0, False)
            pair(1, 0, 1, False)
            with eng.Fori(1, PAIRS // 2 - 1) as i:
                pair(2 * i, i, 0, False)
                pair(2 * i + 1, i, 1, False)
            pair(PAIRS - 2, PAIRS // 2 - 1, 0, False)
            pair(PAIRS - 1, PAIRS // 2 - 1, 1, True)

        def passes_counter(eng):
            before = eng.alloc_register("more_before")
            eng.reg_mov(before, 0)

            def run(j, again):
                todo = eng.value_load(counts_i[0:1, 3, bass.ds(j, 1)], min_val=0, max_val=PASSES - 1)
                with eng.If(todo > 0):
                    with eng.Fori(1, todo + 1) as p:
                        n = eng.snap(before)
                        again(n, p)
                        eng.reg_add(before, before, 1)
            return run

        def y_free(eng, q, n):
            if q is over:
                if not (isinstance(n, int) and n == 0):
                    eng.wait_ge(over.added, 16 * n)
            elif not (isinstance(n, int) and n < 2):
                eng.wait_ge(main.added, 16 * (n - 1))

        def pT_copy(eng, m, u):
            s, hp, qt = units[m]
            eng.wait_ge(p_tr, 2 * m + u + 1)
            g = sum(1 for x in last_of_head if x < m)
            if g >= 1:
                eng.wait_ge(pv_done, 2 * g)
            dst = pT[:, u, 0:TILES[s], qt * P:(qt + 1) * P]
            src = ps[:, 4 + u, 0:SEQS[s]].rearrange("p (c t) -> p c t", c=TILES[s])
            if u == 0:
                eng.activation(dst, src, ACT.Copy).then_inc(pT_act, 1)
            else:
                eng.tensor_copy(dst, src).then_inc(pT_dve, 1)

        def o_copy(eng, m, u):
            s, hp, qt = units[m]
            eng.wait_ge(pv_done, 2 * last_of_head.index(m) + u + 1)
            dst = qT[:, 2 * hp + u, FIRST[s] * P:FIRST[s] * P + SEQS[s]]
            if u == 0:
                eng.activation(dst, ps[:, 6, 0:SEQS[s]], ACT.Copy).then_inc(o_act, 1)
            else:
                eng.tensor_copy(dst, ps[:, 7, 0:SEQS[s]]).then_inc(o_dve, 1)

        N_GAINS = 17
        block = ctx.enter_context(nc.Block())

        @block.sync
        def _(sp):
            sp.dma_start(x_sb[:, 0, :], x_dram(0)).then_inc(x_in[0], 16)
            sp.dma_start(consts[:, :], a["consts"]).then_inc(consts_in, 16)
            w_in_d = a["w_in"][0].rearrange("(p k) n -> p k n", k=KD)
            cuts = (0, RQ, RQ + RKV + DR, IN_W)
            sp.dma_start(w_in[:, :, 0:cuts[1]], w_in_d[:, :, 0:cuts[1]]).then_inc(w_in_in[0], 16)
            gains = [
                (g_attn[:, :], a["g_attn_norm"][0].rearrange("(p k) -> p k", k=KD)),
                (g_lat[:, 0:KQ], a["g_q_lat"][0].rearrange("(p k) -> p k", k=KQ)),
                (g_lat[:, KQ:], a["g_kv_lat"][0].rearrange("(p k) -> p k", k=KKV)),
                (g_nope[:, 0:1], a["g_q_head"][0, 0:DN].rearrange("(p k) -> p k", k=1)),
                (g_nope[:, 1:2], a["g_k_head"][0, 0:DN].rearrange("(p k) -> p k", k=1)),
                (g_pool[:, :], a["pool_scale"][0].rearrange("(g p) -> p g", p=P)),
                (r_bias[0:EG, :], a["b_group_router"][0].rearrange("(p k) -> p k", k=1)),
                (r_bias[EG:, :], a["b_expert_router"][0].rearrange("(p k) -> p k", k=1)),
                (tok_ids[:, :], a["tokens"]),
                (w_router[:, :, 0:EG], a["w_group_router"][0].rearrange("(p k) n -> p k n", k=KD)),
                (w_router[:, :, EG:], a["w_expert_router"][0].rearrange("(p k) n -> p k n", k=KD)),
            ]
            half = DR // 2
            for n, name in enumerate(("g_q_head", "g_k_head")):
                g = a[name][0:1, DN:DQK]
                gains += [(g_rope[:, 2 * n, :], g.partition_broadcast(P)),
                          (g_rope[:, 2 * n + 1, 0:half], g[:, half:DR].partition_broadcast(P)),
                          (g_rope[:, 2 * n + 1, half:DR], g[:, 0:half].partition_broadcast(P))]
            with nc.allow_non_contiguous_dma(reason="a few hundred short rows"):
                for dst, src in gains:
                    sp.dma_start(dst, src).then_inc(gains_in, 16)
            assert len(gains) == N_GAINS
            sp.dma_start(w_in[:, :, cuts[1]:cuts[2]], w_in_d[:, :, cuts[1]:cuts[2]]).then_inc(w_in_in[1], 16)
            sp.dma_start(x_sb[:, 1, :], x_dram(1)).then_inc(x_in[1], 16)
            sp.dma_start(w_in[:, :, cuts[2]:cuts[3]], w_in_d[:, :, cuts[2]:cuts[3]]).then_inc(w_in_in[2], 16)
            sp.dma_start(w_uq[:, :, :], a["w_uq"][0].rearrange("(p k) n -> p k n", k=KQ)).then_inc(w_up_in, 16)
            sp.dma_start(w_ukv[:, :, :], a["w_ukv"][0].rearrange("(p k) n -> p k n", k=KKV)).then_inc(w_up_in, 16)
            sp.dma_start(slot_table.rearrange("(a b) c -> a (b c)", a=P),
                         a["slots"].rearrange("(a b) c -> a (b c)", a=P)).then_inc(setup_dram, 16)
            sp.dma_start(table[T:T + P, :], a["zeros"]).then_inc(setup_dram, 16)
            sp.dma_start(out[T:T + P, :], a["zeros"][:, 0:D]).then_inc(setup_dram, 16)
            load_pair(sp, 0, 0)
            for i in range(2, NT):
                sp.wait_ge(xn_done, i - 1)
                sp.dma_start(x_sb[:, i % 2, :], x_dram(i)).then_inc(x_in[i % 2], 16)
            sp.wait_ge(p3_done, NT)
            sp.dma_start(w_out[:, :, :], a["w_out"][0].rearrange("(k p) n -> p k n", p=P)).then_inc(w_out_in, 16)
            sp.wait_ge(kv_mm, NT)
            sp.wait_ge(r_tr, NT)
            sp.wait_ge(qT_done, NT)
            sp.wait_ge(kT_done, NT)
            sp.wait_ge(rT_done, NT)
            sp.wait_ge(v_done, NT)
            sp.dma_start(band[:, :, :, :], a["band"].rearrange("p (g k c) -> p g k c", g=NG, k=3)).then_inc(pool_in, 16)
            sp.dma_start(w_pool[:, :, :], a["w_pool"][0].rearrange("g c d -> c g d")).then_inc(pool_in, 16)
            sp.wait_ge(d_mm, NG)
            sp.dma_start(x_res[:, :], x_dram(0)).then_inc(x_res_in, 16)
            sp.dma_start(g_ffn[:, :], a["g_ffn_norm"].partition_broadcast(P)).then_inc(g_ffn_in, 16)
            sp.wait_ge(mix_mm, NG)
            sp.wait_ge(dT_done, 2 * NG)
            load_pair(sp, 1, 1)
            for i in range(NT):
                sp.wait_ge(h_done, 2 * (i + 1))
                sp.dma_start(out[i * P:(i + 1) * P, :], h_sb[:, i % 2, :]).then_inc(h_stored, 16)
                if i + 1 < NT:
                    sp.dma_start(x_res[:, :], x_dram(i + 1)).then_inc(x_res_in, 16)
                sp.wait_ge(gates_done, i + 1)
                sp.dma_start(table[i * P:(i + 1) * P, :], rows[:, i % 2, :]).then_inc(rows_stored, 16)
            sp.wait_ge(slots_stored, 2 * NT * 16)
            sp.wait_ge(counts_done, 1)
            sp.dma_start(idx_all[:, :], slot_table[0:BLOCK, :].rearrange("(s j) c -> s (j c)", j=PAIRS)).then_inc(idx_in, 16)
            with sp.Fori(1, PAIRS // 2) as i:
                for b in range(2):
                    sp.wait_ge(main.y_mm, 2 * i + b - 1)
                    sp.wait_ge(pair_done, 2 * i + b - 1)
                    load_pair(sp, 2 * i + b, b)

        @block.tensor
        def _(pe):
            def x_transposes(i):
                pe.wait_ge(xn_done, i + 1)
                if i >= 1:
                    pe.wait_ge(aT_done, 2 * i)
                if i >= 2:
                    pe.wait_ge(cT_done, i - 1)
                if i == 0:
                    pe.wait_ge(consts_in, 16)
                for k in range(KD):
                    mm = pe.transpose(ps[:, k // 4, (k % 4) * P:(k % 4 + 1) * P], xn[:, k, :], ident)
                    if k % 4 == 3:
                        mm.then_inc(x_tr, 1)

            def project(i, n, bank, lo, hi, done):
                pe.wait_ge(w_in_in[n], 16)
                for k in range(KD):
                    mm = pe.matmul(ps[:, bank, 0:hi - lo], aT[:, k, :], w_in[:, k, lo:hi], start=(k == 0), stop=(k == KD - 1))
                mm.then_inc(done, 1)

            def head_transposes(i, src, ready, done):
                pe.wait_ge(ready, i + 1)
                for h in range(H):
                    mm = pe.transpose(ps[:, 7, h * P:(h + 1) * P], src[:, h, :], ident)
                mm.then_inc(done, 1)

            def rope_transposes(i):
                pe.wait_ge(qr_done, i + 1)
                pe.wait_ge(kr_done, i + 1)
                pe.wait_ge(kT_done, i + 1)
                for n, src in enumerate((q_r, k_r)):
                    flat = src[:, :, :].rearrange("t h r -> t (h r)")
                    for hp in range(2):
                        mm = pe.transpose(ps[:, 7, (2 * n + hp) * P:(2 * n + hp + 1) * P], flat[:, hp * P:(hp + 1) * P], ident)
                mm.then_inc(r_tr, 1)

            x_transposes(0)
            for i in range(NT):
                pe.wait_ge(aT_done, 2 * (i + 1))
                if i >= 1:
                    pe.wait_ge(q_sq, i)
                    pe.wait_ge(qn_done, i)
                project(i, 0, 2, 0, RQ, p1_done)
                if i >= 1:
                    if i >= 2:
                        pe.wait_ge(rT_done, i - 1)
                    head_transposes(i - 1, q_n, qn_done, qn_tr)
                project(i, 1, 3, RQ, RQ + RKV + DR, p2_done)
                if i >= 1:
                    pe.wait_ge(qT_done, i)
                    head_transposes(i - 1, k_n, kn_done, kn_tr)
                    pe.wait_ge(u_done, i)
                project(i, 2, 4, RQ + RKV + DR, IN_W, p3_done)
                if i + 1 < NT:
                    x_transposes(i + 1)
                pe.wait_ge(cn_done, 2 * (i + 1))
                if i + 1 < NT:
                    pe.wait_ge(aT_done, 2 * (i + 2))
                for k in range(KQ + KKV):
                    mm = pe.transpose(ps[:, k // 4, (k % 4) * P:(k % 4 + 1) * P], cn[:, k, :], ident)
                mm.then_inc(c_tr, 1)
                if i >= 1:
                    rope_transposes(i - 1)
                pe.wait_ge(cT_done, i + 1)
                pe.wait_ge(k_raw_done, i + 1)
                pe.wait_ge(w_up_in, 32)
                for n in range(2):
                    for k in range(KQ):
                        mm = pe.matmul(ps[:, 2 + n, 0:384], cT[:, k, :], w_uq[:, k, n * 384:(n + 1) * 384],
                                       start=(k == 0), stop=(k == KQ - 1))
                mm.then_inc(q_mm, 1)
                if i >= 1:
                    pe.wait_ge(k_sq, i)
                    pe.wait_ge(kn_done, i)
                    pe.wait_ge(v_done, i)
                for n in range(2):
                    for k in range(KKV):
                        mm = pe.matmul(ps[:, 5 + n, :], cT[:, KQ + k, :], w_ukv[:, k, n * 512:(n + 1) * 512],
                                       start=(k == 0), stop=(k == KKV - 1))
                mm.then_inc(kv_mm, 1)
            pe.wait_ge(rT_done, NT - 1)
            head_transposes(NT - 1, q_n, qn_done, qn_tr)
            pe.wait_ge(qT_done, NT)
            head_transposes(NT - 1, k_n, kn_done, kn_tr)
            rope_transposes(NT - 1)

            pe.wait_ge(rT_done, NT)
            pe.wait_ge(kT_done, NT)
            pe.wait_ge(v_done, NT)
            pe.wait_ge(k_sq, NT)
            pe.wait_ge(kn_done, NT)
            pe.wait_ge(qn_done, NT)
            pe.wait_ge(u_done, NT)

            def scores(m):
                s, hp, qt = units[m]
                keys = slice(FIRST[s] * P, (FIRST[s] + TILES[s]) * P)
                q = slice((FIRST[s] + qt) * P, (FIRST[s] + qt + 1) * P)
                if m >= 2:
                    pe.wait_ge(exp_done, 2 * (m - 1))
                bank = 2 * (m % 2)
                n = SEQS[s]
                for u in range(2):
                    h = 2 * hp + u
                    pe.matmul(ps[:, bank + u, 0:n], qT[:, h, q], kT[:, h, keys], start=True, stop=False)
                for u in range(2):
                    r = slice(u * DR, (u + 1) * DR)
                    pe.matmul(ps[:, bank + u, 0:n], rT[r, hp, q], rT[r, 2 + hp, keys], start=False, stop=True).then_inc(s_ready, 1)

            def p_transposes(m):
                s, hp, qt = units[m]
                if m >= 1:
                    pe.wait_ge(pT_act, m)
                    pe.wait_ge(pT_dve, m)
                for u in range(2):
                    pe.wait_ge(p_done, 2 * m + u + 1)
                    for c in range(TILES[s]):
                        mm = pe.transpose(ps[:, 4 + u, c * P:(c + 1) * P], p_sb[:, (2 * m + u) % 4, c * P:(c + 1) * P], ident)
                    mm.then_inc(p_tr, 1)

            def attend(m):
                s, hp, qt = units[m]
                g = last_of_head.index(m)
                pe.wait_ge(pT_act, m + 1)
                pe.wait_ge(pT_dve, m + 1)
                if g >= 1:
                    pe.wait_ge(o_act, g)
                    pe.wait_ge(o_dve, g)
                for u in range(2):
                    h = 2 * hp + u
                    for c in range(TILES[s]):
                        mm = pe.matmul(ps[:, 6 + u, 0:SEQS[s]], v_sb[:, FIRST[s] + c, h * DV:(h + 1) * DV],
                                       pT[:, u, c, 0:SEQS[s]], start=(c == 0), stop=(c == TILES[s] - 1))
                    mm.then_inc(pv_done, 1)

            scores(0)
            for m in range(len(units)):
                if m + 1 < len(units):
                    scores(m + 1)
                p_transposes(m)
                if m in last_of_head:
                    attend(m)

            pe.wait_ge(pool_in, 32)

            def windows(g):
                if g >= 2:
                    pe.wait_ge(dT_done, 2 * (g - 1))
                for s in range(2):
                    bank = 2 * (g % 2) + s
                    for t in range(TILES[s]):
                        kind = 0 if t == 0 else 2 if t == TILES[s] - 1 else 1
                        lo, hi = max(t * P - HALO, 0), min((t + 1) * P + HALO, SEQS[s])
                        c = lo - (t * P - HALO)
                        mm = pe.matmul(ps[:, bank, lo:hi], u_sb[:, FIRST[s] + t, g * GC:(g + 1) * GC],
                                       band[:, g, kind, c:c + hi - lo], start=(t == 0), stop=(t == TILES[s] - 1),
                                       skip_group_check=True)
                mm.then_inc(d_mm, 1)

            def mix(g):
                pe.wait_ge(dT_done, 2 * (g + 1))
                if g == 0:
                    pe.wait_ge(o_act, len(last_of_head))
                    pe.wait_ge(o_dve, len(last_of_head))
                if g >= 2:
                    pe.wait_ge(mix_done, 2 * (g - 1))
                for s in range(2):
                    mm = pe.matmul(ps[:, 4 + 2 * (g % 2) + s, 0:SEQS[s]], w_pool[:, g, :],
                                   dT[:, g % 2, FIRST[s] * P:FIRST[s] * P + SEQS[s]], start=True, stop=True)
                mm.then_inc(mix_mm, 1)

            windows(0)
            for g in range(NG):
                if g + 1 < NG:
                    windows(g + 1)
                mix(g)

            pe.wait_ge(mix_done, 2 * NG)
            pe.wait_ge(w_out_in, 16)
            pe.wait_ge(bf_set, 2)

            def out_half(i, n):
                if i >= 2:
                    pe.wait_ge(h_done, 2 * (i - 1))
                for c in range(KD):
                    src = qT if c < H else kT
                    mm = pe.matmul(ps[:, 2 * (i % 2) + n, :], src[:, c % H, i * P:(i + 1) * P],
                                   w_out[:, c, n * 512:(n + 1) * 512], start=(c == 0), stop=(c == KD - 1))
                mm.then_inc(o_mm, 1)

            def row_transposes(i):
                pe.wait_ge(a2_done, i + 1)
                if i >= 1:
                    pe.wait_ge(a2T_done, 2 * i)
                for k in range(KD):
                    mm = pe.transpose(ps[:, 4 + k // 4, (k % 4) * P:(k % 4 + 1) * P], rows[:, i % 2, k * P:(k + 1) * P], ident)
                mm.then_inc(a2_tr, 1)

            def logits(i):
                pe.wait_ge(a2T_done, 2 * (i + 1))
                if i >= 1:
                    pe.wait_ge(pos_done, i)
                for k in range(KD):
                    mm = pe.matmul(ps[0:EG + E, 6, 0:P], w_router[:, k, :], a2T[:, k, :], start=(k == 0), stop=(k == KD - 1))
                mm.then_inc(lg_mm, 1)
                pe.wait_ge(lg_bias, i + 1)
                if i >= 1:
                    pe.wait_ge(mask_done, i)
                pe.transpose(ps[:, 7, 0:EG + E], route_f[0:EG + E, 0:P], consts[0:EG + E, C_ID:C_ID + EG + E]).then_inc(lg_tr, 1)

            def ranks(i):
                pe.wait_ge(mask_done, i + 1)
                pe.matmul(ps[:, 6, 128:128 + E], ones_bf, m_sum[:, 0, :], start=True, stop=False)
                pe.matmul(ps[:, 6, 128:128 + E], ltri_bf, m_sum[:, 1, :], start=False, stop=True).then_inc(rank_mm, 1)

            for i in range(NT):
                out_half(i, 0)
                if i >= 1:
                    row_transposes(i - 1)
                if i >= 2:
                    ranks(i - 2)
                out_half(i, 1)
                if i >= 1:
                    logits(i - 1)
            row_transposes(NT - 1)
            ranks(NT - 2)
            logits(NT - 1)
            ranks(NT - 1)
            pe.wait_ge(pos_done, NT)
            pe.matmul(ps[:, 7, 0:E], ones_bf, m_sum[:, 0, :], start=True, stop=True).then_inc(total_mm, 1)

            pe.wait_ge(counts_done, 1)

            def gather_transposes(q, src, b, n, landed, uses):
                pe.wait_ge(landed, 16 * uses)
                banks = 0 if q is main else 6
                for k in range(KD):
                    mm = pe.transpose(ps[:, banks + k // 4, (k % 4) * P:(k % 4 + 1) * P], src[:, k * P:(k + 1) * P], ident)
                mm.then_inc(q.x_tr, 1)

            def gate_up(q, b, n):
                pe.wait_ge(q.x_act, n + 1)
                pe.wait_ge(q.x_dve, n + 1)
                for k in range(KD):
                    for lane in range(2):
                        r = slice(lane * LANE, (lane + 1) * LANE)
                        mm = pe.matmul(ps[r, 2, :].rearrange("p (g f) -> p g f", g=2), xT[:, q.o, k, r], w_gu(b, lane, k),
                                       start=(k == 0), stop=(k == KD - 1))
                mm.then_inc(q.gu_mm, 1)

            def hidden_transposes(q, n):
                pe.wait_ge(q.hid_done, n + 1)
                for k in range(2):
                    mm = pe.transpose(ps[:, 3, k * P:(k + 1) * P], hid[:, q.o, k, :], ident)
                mm.then_inc(q.h_tr, 1)

            def down(q, b, n):
                pe.wait_ge(q.hT_done, n + 1)
                for half in range(2):
                    for k in range(2):
                        for lane in range(2):
                            r = slice(lane * LANE, (lane + 1) * LANE)
                            mm = pe.matmul(ps[r, 4 + half, :], hT[:, q.o, k, r], w_dn(b, lane, k, half),
                                           start=(k == 0), stop=(k == 1))
                mm.then_inc(q.y_mm, 1)

            more_passes = passes_counter(pe)

            def pair(j, i, b, last):
                pe.wait_ge(gu_in[b], 64 * (i + 1))
                gate_up(main, b, j)
                if not last:
                    nb = 1 - b
                    gather_transposes(main, g_rows[:, nb, :], nb, j + 1, (main.gathered0, main.gathered1)[nb], i + 1 if b == 0 else i + 2)
                hidden_transposes(main, j)
                pe.wait_ge(dn_in[b], 32 * (i + 1))
                pe_y_free(pe, j)
                down(main, b, j)

                def again(n, p):
                    gather_transposes(over, more_rows[:, :], b, n, over.gathered0, n + 1)
                    gate_up(over, b, n)
                    hidden_transposes(over, n)
                    pe.wait_ge(main.y_act, j + 1)
                    pe.wait_ge(main.y_dve, j + 1)
                    down(over, b, n)
                    pe.wait_ge(over.y_act, n + 1)
                    pe.wait_ge(over.y_dve, n + 1)

                more_passes(j, again)
                pe.nop().then_inc(pair_done, 1)

            gather_transposes(main, g_rows[:, 0, :], 0, 0, main.gathered0, 1)
            run_pairs(pe, pair)

        @block.scalar
        def _(act):
            def norm_x(i):
                act.wait_ge(x_in[i % 2], 16 * (i // 2 + 1))
                if i >= 1:
                    act.wait_ge(x_tr, 2 * i)
                act.activation(xn[:, :, :].rearrange("t k p -> t (k p)"), x_sb[:, i % 2, :], ACT.Square,
                               accum_out=stats[:, 0:1]).then_inc(x_sq, 1)
                act.wait_ge(x_rstd, i + 1)
                act.activation(xn[:, :, :].rearrange("t k p -> t p k"), x_sb[:, i % 2, :].rearrange("t (p k) -> t p k", k=KD),
                               ACT.Copy, scale=stats[:, 2:3]).then_inc(xn_done, 1)

            def heads_out(i, col, dst, tr, done):
                act.wait_ge(tr, i + 1)
                act.activation(dst[:, :, i * P:(i + 1) * P], ps[:, 7, :].rearrange("p (h t) -> p h t", h=H), ACT.Copy,
                               scale=g_nope[:, col:col + 1]).then_inc(done, 1)

            act.wait_ge(gains_in, 16 * N_GAINS)
            norm_x(0)
            for i in range(NT):
                if i + 1 < NT:
                    norm_x(i + 1)
                act.wait_ge(p1_done, i + 1)
                if i >= 1:
                    act.wait_ge(k_ss, i)
                    act.wait_ge(c_rstd, i)
                act.activation(junk[:, 0:RQ], ps[:, 2, 0:RQ], ACT.Square, accum_out=stats[:, 4:5]).then_inc(c_sq, 1)
                if i >= 1:
                    heads_out(i - 1, 0, qT, qn_tr, qT_done)
                act.wait_ge(p2_done, i + 1)
                act.wait_ge(c_sq, 3 * i + 1)
                act.activation(junk[:, 0:RKV], ps[:, 3, 0:RKV], ACT.Square, accum_out=stats[:, 5:6]).then_inc(c_sq, 1)
                act.wait_ge(c_sq, 3 * i + 2)
                if i >= 1:
                    act.wait_ge(k_ms, i)
                    act.wait_ge(kr_done, i)
                act.activation(junk[:, 0:DR], ps[:, 3, RKV:RKV + DR], ACT.Square, accum_out=stats[:, 6:7]).then_inc(c_sq, 1)
                act.activation(k_raw[:, :], ps[:, 3, RKV:RKV + DR], ACT.Copy).then_inc(k_raw_done, 1)
                if i >= 1:
                    heads_out(i - 1, 1, kT, kn_tr, kT_done)
                act.wait_ge(c_rstd, i + 1)
                if i >= 1:
                    act.wait_ge(c_tr, i)
                act.activation(cn[:, 0:KQ, :].rearrange("t k p -> t p k"), ps[:, 2, 0:RQ].rearrange("t (p k) -> t p k", k=KQ),
                               ACT.Copy, scale=stats[:, 8:9]).then_inc(cn_done, 1)
                act.activation(cn[:, KQ:, :].rearrange("t k p -> t p k"), ps[:, 3, 0:RKV].rearrange("t (p k) -> t p k", k=KKV),
                               ACT.Copy, scale=stats[:, 9:10]).then_inc(cn_done, 1)
                act.wait_ge(p3_done, i + 1)
                act.activation(u_sb[:, i, :], ps[:, 4, :], ACT.Copy).then_inc(u_done, 1)
                act.wait_ge(q_mm, i + 1)
                act.wait_ge(c_sq, 3 * i + 3)
                act.activation(junk[:, 0:H * DQK].rearrange("t (b c) -> t b c", b=2), ps[:, 2:4, 0:384], ACT.Square).then_inc(q_sq, 1)
                act.wait_ge(kv_mm, i + 1)
                act.wait_ge(q_ss, i + 1)
                kv = ps[:, 5:7, :].rearrange("t b (h w) -> t b h w", h=2)
                act.activation(junk[:, 0:H * DN].rearrange("t (b h w) -> t b h w", b=2, h=2), kv[:, :, :, 0:DN], ACT.Square).then_inc(k_sq, 1)
                act.activation(v_sb[:, i, :].rearrange("t (b h w) -> t b h w", b=2, h=2), kv[:, :, :, DN:], ACT.Copy).then_inc(v_done, 1)
            heads_out(NT - 1, 0, qT, qn_tr, qT_done)
            heads_out(NT - 1, 1, kT, kn_tr, kT_done)

            act.wait_ge(r_tr, NT)
            act.wait_ge(rT_done, NT)
            for m, (s, hp, qt) in enumerate(units):
                n = SEQS[s]
                for u in range(2):
                    w = 2 * m + u
                    act.wait_ge(neg_max, w + 1)
                    if w >= 4:
                        act.wait_ge(p_tr, w - 3)
                    act.activation(p_sb[:, w % 4, 0:n], ps[:, 2 * (m % 2) + u, 0:n], ACT.Exp, bias=a_stat[:, w % 4, 1:2],
                                   scale=SCALE, accum_out=a_stat[:, w % 4, 2:3]).then_inc(exp_done, 1)
                if m >= 1:
                    pT_copy(act, m - 1, 0)
                if m - 1 in last_of_head:
                    o_copy(act, m - 1, 0)
            pT_copy(act, len(units) - 1, 0)
            o_copy(act, len(units) - 1, 0)

            for g in range(NG):
                act.wait_ge(d_mm, g + 1)
                if g >= 2:
                    act.wait_ge(mix_mm, g - 1)
                for s in range(2):
                    act.activation(dT[:, g % 2, FIRST[s] * P:FIRST[s] * P + SEQS[s]], ps[:, 2 * (g % 2) + s, 0:SEQS[s]],
                                   ACT.Copy).then_inc(dT_done, 1)

            def route_exps(i):
                act.wait_ge(neg_g, i + 1)
                if i >= 1:
                    act.wait_ge(gates_done, i)
                act.activation(route_f[:, 160:164], route_f[:, 128:132], ACT.Exp, bias=route_f[:, 176:177],
                               accum_out=route_f[:, 177:178]).then_inc(g_exp, 1)
                act.wait_ge(e_diff, i + 1)
                act.activation(route_f[:, 179:180], route_f[:, 178:179], ACT.Exp).then_inc(e_exp, 1)

            for i in range(NT):
                act.wait_ge(h_done, 2 * (i + 1))
                if i >= 1:
                    act.wait_ge(h_rstd, i)
                act.activation(h_junk[:, :], h_sb[:, i % 2, :], ACT.Square, accum_out=route_f[:, 400:401]).then_inc(h_sq, 1)
                if i >= 1:
                    route_exps(i - 1)
                act.wait_ge(a2_tr, i + 1)
                if i >= 1:
                    act.wait_ge(lg_mm, i)
                for half in range(2):
                    act.activation(a2T[:, 4 * half:4 * half + 4, :], ps[:, 4 + half, :].rearrange("p (k t) -> p k t", k=4),
                                   ACT.Copy).then_inc(a2T_done, 1)
            route_exps(NT - 1)

            act.wait_ge(counts_done, 1)

            def x_copy(q, n):
                act.wait_ge(q.x_tr, n + 1)
                bank = 0 if q is main else 6
                act.activation(xT[:, q.o, 0:4, :], ps[:, bank, :].rearrange("p (k t) -> p k t", k=4), ACT.Copy).then_inc(q.x_act, 1)

            def silu(q, n):
                act.wait_ge(q.gu_mm, n + 1)
                act.activation(s_act[:, q.o, :], ps[:, 2, 0:FH], ACT.Silu).then_inc(q.silu_done, 1)

            def y_copy(q, n, buf):
                act.wait_ge(q.y_mm, n + 1)
                y_free(act, q, n)
                act.activation(y_sb[:, buf, 0:512], ps[:, 4, :], ACT.Copy).then_inc(q.y_act, 1)

            more_passes = passes_counter(act)

            def pair(j, i, b, last):
                silu(main, j)
                if not last:
                    x_copy(main, j + 1)
                y_copy(main, j, b)

                def again(n, p):
                    x_copy(over, n)
                    silu(over, n)
                    y_copy(over, n, 2)

                more_passes(j, again)

            x_copy(main, 0)
            run_pairs(act, pair)

        @block.vector
        def _(dve):
            steps = {"rope": 0, "route": 0}

            def link(kind, signal, ins):
                steps[kind] += 1
                ins.then_inc(signal, 1)
                dve.wait_ge(signal, steps[kind])

            dve.wait_ge(consts_in, 16)
            dve.tensor_copy(ltri_bf, consts[:, C_LTRI:C_LTRI + P]).then_inc(bf_set, 1)
            dve.memset(ones_bf, 1.0).then_inc(bf_set, 1)
            dve.memset(m_sum[:, 0, :], 0.0).then_inc(bf_set, 1)
            dve.wait_ge(gains_in, 16 * N_GAINS)
            for n in range(4):
                tab = consts[:, (C_COS, C_SIN)[n % 2]:(C_COS, C_SIN)[n % 2] + 4 * DR].rearrange("p (t r) -> p t r", t=4)
                dve.tensor_tensor(rope_tab[:, n, :, :], tab, g_rope[:, n, :].unsqueeze(1).to_broadcast([P, 4, DR]),
                                  ALU.mult).then_inc(tables_set, 1)
            dve.wait_ge(tables_set, 4)

            def aT_copy(i):
                for half in range(2):
                    dve.wait_ge(x_tr, 2 * i + half + 1)
                    if i >= 1 and half == 0:
                        dve.wait_ge(p3_done, i)
                    dve.tensor_tensor(aT[:, 4 * half:4 * half + 4, :], ps[:, half, :].rearrange("p (k t) -> p k t", k=4),
                                      g_attn[:, 4 * half:4 * half + 4].unsqueeze(2).to_broadcast([P, 4, P]),
                                      ALU.mult).then_inc(aT_done, 1)

            def rotate(x, o, n, pt, heads, done):
                half = DR // 2
                t = rope_t[:, :, 0:heads, :]
                cos = rope_tab[:, 2 * n, pt, :].unsqueeze(1).to_broadcast([P, heads, DR])
                lo = rope_tab[:, 2 * n + 1, pt, 0:half].unsqueeze(1).to_broadcast([P, heads, half])
                hi = rope_tab[:, 2 * n + 1, pt, half:DR].unsqueeze(1).to_broadcast([P, heads, half])
                dve.tensor_tensor(t[:, 0], x, cos, ALU.mult)
                dve.tensor_tensor(t[:, 1, :, 0:half], x[:, :, half:DR], lo, ALU.mult)
                link("rope", rope_step, dve.tensor_tensor(t[:, 1, :, half:DR], x[:, :, 0:half], hi, ALU.mult))
                return dve.tensor_tensor(o, t[:, 0], t[:, 1], ALU.add)

            aT_copy(0)
            for i in range(NT):
                pt = i - FIRST[0 if i < FIRST[1] else 1]
                if i + 1 < NT:
                    aT_copy(i + 1)
                dve.wait_ge(c_tr, i + 1)
                if i >= 1:
                    dve.wait_ge(kv_mm, i)
                dve.tensor_tensor(cT[:, :, :], ps[:, 0:2, :].rearrange("p b (k t) -> p (b k) t", t=P)[:, 0:KQ + KKV, :],
                                  g_lat[:, :].unsqueeze(2).to_broadcast([P, KQ + KKV, P]), ALU.mult).then_inc(cT_done, 1)
                if i >= 1:
                    dve.wait_ge(r_tr, i)
                    dve.tensor_copy(rT[:, :, (i - 1) * P:i * P], ps[:, 7, :].rearrange("p (n t) -> p n t", n=4)).then_inc(rT_done, 1)
                dve.wait_ge(q_sq, i + 1)
                if i >= 1:
                    dve.wait_ge(q_ms, i)
                dve.tensor_reduce(stats[:, 12:16], junk[:, 0:H * DQK].rearrange("t (h w) -> t h w", h=H), AX.X, ALU.add).then_inc(q_ss, 1)
                dve.wait_ge(q_rstd, i + 1)
                if i >= 1:
                    dve.wait_ge(qn_tr, i)
                    dve.wait_ge(qr_done, i)
                r = stats[:, 20:24].rearrange("t (b h) -> t b h", b=2).unsqueeze(3)
                q = ps[:, 2:4, 0:384].rearrange("t b (h w) -> t b h w", h=2)
                dve.tensor_tensor(q_x[:, :, :].rearrange("t (b h) w -> t b h w", b=2), q[:, :, :, DN:],
                                  r.to_broadcast([P, 2, 2, DR]), ALU.mult).then_inc(qx_done, 1)
                dve.tensor_tensor(q_n[:, :, :].rearrange("t (b h) w -> t b h w", b=2), q[:, :, :, 0:DN],
                                  r.to_broadcast([P, 2, 2, DN]), ALU.mult).then_inc(qn_done, 1)
                dve.wait_ge(k_sq, i + 1)
                if i >= 1:
                    dve.wait_ge(k_rstd, i)
                dve.tensor_reduce(stats[:, 28:32], junk[:, 0:H * DN].rearrange("t (h w) -> t h w", h=H), AX.X, ALU.add).then_inc(k_ss, 1)
                dve.wait_ge(qn_done, i + 1)
                rotate(q_x[:, :, :], q_r[:, :, :], 0, pt, H, qr_done).then_inc(qr_done, 1)
                dve.wait_ge(k_rstd, i + 1)
                dve.wait_ge(v_done, i + 1)
                if i >= 1:
                    dve.wait_ge(kn_tr, i)
                r = stats[:, 40:44]
                kv = ps[:, 5:7, :].rearrange("t b (h w) -> t b h w", h=2)
                dve.tensor_tensor(k_n[:, :, :].rearrange("t (b h) w -> t b h w", b=2), kv[:, :, :, 0:DN],
                                  r.rearrange("t (b h) -> t b h", b=2).unsqueeze(3).to_broadcast([P, 2, 2, DN]),
                                  ALU.mult).then_inc(kn_done, 1)
                dve.wait_ge(qr_done, i + 1)
                dve.wait_ge(k_raw_done, i + 1)
                link("rope", rope_step, rotate(k_raw[:, :].unsqueeze(1), rope_k[:, :].unsqueeze(1), 1, pt, 1, None))
                dve.tensor_tensor(k_r[:, :, :], rope_k[:, :].unsqueeze(1).to_broadcast([P, H, DR]),
                                  r.unsqueeze(2).to_broadcast([P, H, DR]), ALU.mult).then_inc(kr_done, 1)
            dve.wait_ge(r_tr, NT)
            dve.tensor_copy(rT[:, :, (NT - 1) * P:], ps[:, 7, :].rearrange("p (n t) -> p n t", n=4)).then_inc(rT_done, 1)

            dve.wait_ge(kr_done, NT)
            for m, (s, hp, qt) in enumerate(units):
                n = SEQS[s]
                for u in range(2):
                    w = 2 * m + u
                    st = a_stat[:, w % 4]
                    dve.wait_ge(s_ready, w + 1)
                    if w >= 4:
                        dve.wait_ge(exp_done, w - 3)
                        dve.wait_ge(p_done, w - 3)
                    dve.reduce_max(st[:, 0:1], ps[:, 2 * (m % 2) + u, 0:n], AX.X).then_inc(row_max, 1)
                    dve.wait_ge(row_max, w + 1)
                    dve.tensor_scalar(st[:, 1:2], st[:, 0:1], -SCALE, None, ALU.mult).then_inc(neg_max, 1)
                if m >= 1:
                    pT_copy(dve, m - 1, 1)
                for u in range(2):
                    w = 2 * m + u
                    st = a_stat[:, w % 4]
                    dve.wait_ge(exp_done, w + 1)
                    dve.reciprocal(st[:, 3:4], st[:, 2:3]).then_inc(recip_done, 1)
                    dve.wait_ge(recip_done, w + 1)
                    dve.tensor_scalar(p_sb[:, w % 4, 0:n], p_sb[:, w % 4, 0:n], st[:, 3:4], None, ALU.mult).then_inc(p_done, 1)
                if m - 1 in last_of_head:
                    o_copy(dve, m - 1, 1)
            pT_copy(dve, len(units) - 1, 1)
            o_copy(dve, len(units) - 1, 1)

            for g in range(NG):
                dve.wait_ge(mix_mm, g + 1)
                for s in range(2):
                    dve.tensor_scalar(kT[:, g, FIRST[s] * P:FIRST[s] * P + SEQS[s]], ps[:, 4 + 2 * (g % 2) + s, 0:SEQS[s]],
                                      g_pool[:, g:g + 1], None, ALU.mult).then_inc(mix_done, 1)

            RF = route_f
            dve.wait_ge(d_mm, NG)
            dve.memset(RF[:, 128:136], -3e38).then_inc(bf_set, 1)
            dve.wait_ge(g_ffn_in, 16)

            def residual(i):
                dve.wait_ge(x_res_in, 16 * (i + 1))
                if i >= 2:
                    dve.wait_ge(h_stored, 16 * (i - 1))
                    dve.wait_ge(a2_done, i - 1)
                    dve.wait_ge(h_sq, i - 1)
                for n in range(2):
                    dve.wait_ge(o_mm, 2 * i + n + 1)
                    dve.tensor_tensor(h_sb[:, i % 2, n * 512:(n + 1) * 512], ps[:, 2 * (i % 2) + n, :], x_res[:, n * 512:(n + 1) * 512],
                                      ALU.add).then_inc(h_done, 1)

            def second_norm(i):
                dve.wait_ge(h_rstd, i + 1)
                if i >= 2:
                    dve.wait_ge(rows_stored, 16 * (i - 1))
                    dve.wait_ge(a2_tr, i - 1)
                dve.scalar_tensor_tensor(out=rows[:, i % 2, 0:D].rearrange("t (k p) -> t p k", k=KD),
                                         in0=h_sb[:, i % 2, :].rearrange("t (p k) -> t p k", k=KD), scalar=route_f[:, 402:403],
                                         in1=g_ffn[:, :].rearrange("t (p k) -> t p k", k=KD), op0=ALU.mult, op1=ALU.mult).then_inc(a2_done, 1)

            def bias_logits(i):
                dve.wait_ge(lg_mm, i + 1)
                if i >= 1:
                    dve.wait_ge(lg_tr, i)
                dve.tensor_scalar(RF[0:EG + E, 0:P], ps[0:EG + E, 6, 0:P], r_bias[:, 0:1], None, ALU.add).then_inc(lg_bias, 1)

            def route(i):
                def step(ins):
                    link("route", route_step, ins)

                dve.wait_ge(lg_tr, i + 1)
                if i >= 1:
                    dve.wait_ge(g_exp, i)
                if i == 0:
                    dve.wait_ge(bf_set, 4)
                lg = ps[:, 7, 0:EG + E]
                step(dve.tensor_copy(RF[:, 128:128 + EG], lg[:, 0:EG]))
                step(dve.max(RF[:, 136:144], RF[:, 128:136]))
                dve.tensor_scalar(RF[:, 176:177], RF[:, 136:137], -1.0, None, ALU.mult).then_inc(neg_g, 1)
                step(dve.max_index(route_u[:, 0:8], RF[:, 136:144], RF[:, 128:136]))
                step(dve.tensor_copy(RF[:, 180:181], route_u[:, 0:1]))
                step(dve.tensor_scalar(RF[:, 168:172], iota[:, 0:EG], RF[:, 180:181], -BIG, ALU.not_equal, ALU.mult))
                step(dve.tensor_tensor(RF[:, 192:192 + E].rearrange("t (g e) -> t g e", g=EG),
                                       lg[:, EG:EG + E].rearrange("t (g e) -> t g e", g=EG),
                                       RF[:, 168:172].unsqueeze(2).to_broadcast([P, EG, EPG]), ALU.add))
                step(dve.max(RF[:, 144:152], RF[:, 192:192 + E]))
                dve.tensor_tensor(RF[:, 178:179], RF[:, 145:146], RF[:, 144:145], ALU.subtract).then_inc(e_diff, 1)
                step(dve.max_index(route_u[:, 8:16], RF[:, 144:152], RF[:, 192:192 + E]))
                step(dve.tensor_copy(RF[:, 182:184], route_u[:, 8:10]))
                if i >= 1:
                    dve.wait_ge(rank_mm, i)
                    dve.wait_ge(pos_done, i)
                dve.tensor_scalar(RF[:, 224:224 + E], iota, RF[:, 182:183], None, ALU.is_equal)
                step(dve.tensor_scalar(RF[:, 256:256 + E], iota, RF[:, 183:184], None, ALU.is_equal))
                dve.tensor_tensor(m_sum[:, 1, :], RF[:, 224:224 + E], RF[:, 256:256 + E], ALU.add).then_inc(mask_done, 1)
                dve.wait_ge(e_exp, i + 1)
                dve.wait_ge(g_exp, i + 1)
                step(dve.tensor_scalar(RF[:, 184:185], RF[:, 179:180], 1.0, RF[:, 177:178], ALU.add, ALU.mult))
                step(dve.reciprocal(RF[:, 185:186], RF[:, 184:185]))
                step(dve.tensor_tensor(RF[:, 186:187], RF[:, 185:186], RF[:, 179:180], ALU.mult))
                step(dve.tensor_scalar(RF[:, 288:288 + E], RF[:, 256:256 + E], RF[:, 186:187], None, ALU.mult))
                dve.scalar_tensor_tensor(out=rows[:, i % 2, D:ROW], in0=RF[:, 224:224 + E], scalar=RF[:, 185:186],
                                         in1=RF[:, 288:288 + E], op0=ALU.mult, op1=ALU.add).then_inc(gates_done, 1)

            def positions(i):
                def step(ins):
                    link("route", route_step, ins)

                dve.wait_ge(rank_mm, i + 1)
                dve.wait_ge(mask_done, i + 1)
                step(dve.tensor_copy(RF[:, 320:320 + E], ps[:, 6, 128:128 + E]))
                for c in range(2):
                    oh = RF[:, 224 + E * c:224 + E * c + E]
                    step(dve.tensor_tensor_reduce(out=RF[:, 352:352 + E], in0=oh, in1=RF[:, 320:320 + E], scale=1.0, scalar=0.0,
                                                  op0=ALU.mult, op1=ALU.add, accum_out=RF[:, 384 + c:385 + c]))
                    step(dve.tensor_tensor_reduce(out=RF[:, 352:352 + E], in0=oh, in1=ebase, scale=1.0, scalar=0.0,
                                                  op0=ALU.mult, op1=ALU.add, accum_out=RF[:, 386 + c:387 + c]))
                ri = route_u[:, 16:18].bitcast(I32)
                rs = route_u[:, 18:20].bitcast(I32)
                step(dve.tensor_copy(ri, RF[:, 384:386]))
                step(dve.tensor_scalar(rs, ri, 6, None, ALU.arith_shift_right))
                step(dve.tensor_copy(RF[:, 388:390], rs))
                step(dve.scalar_tensor_tensor(out=RF[:, 386:388], in0=RF[:, 384:386], scalar=float(PAIRS), in1=RF[:, 386:388],
                                              op0=ALU.mult, op1=ALU.add))
                step(dve.scalar_tensor_tensor(out=RF[:, 390:392], in0=RF[:, 388:390], scalar=float(BLOCK - LANE * PAIRS),
                                              in1=RF[:, 386:388], op0=ALU.mult, op1=ALU.add))
                step(dve.tensor_copy(idx_pos[:, i, :], RF[:, 390:392]))
                dve.tensor_tensor(m_sum[:, 0, :], m_sum[:, 0, :], m_sum[:, 1, :], ALU.add).then_inc(pos_done, 1)

            for i in range(NT):
                residual(i)
                if i >= 2:
                    positions(i - 2)
                second_norm(i)
                if i >= 1:
                    bias_logits(i - 1)
                    route(i - 1)
            positions(NT - 2)
            bias_logits(NT - 1)
            route(NT - 1)
            positions(NT - 1)

            dve.wait_ge(total_mm, 1)
            c = RF[0:1, 224:224 + E]
            link("route", route_step, dve.tensor_copy(c, ps[0:1, 7, 0:E]))
            cp = c.rearrange("t (l j) -> t l j", l=2)
            link("route", route_step, dve.tensor_tensor(RF[0:1, 256:256 + PAIRS], cp[:, 0, :], cp[:, 1, :], ALU.max))
            link("route", route_step, dve.tensor_scalar(RF[0:1, 288:288 + PAIRS], RF[0:1, 256:256 + PAIRS], -1.0, 0.0, ALU.add, ALU.max))
            link("route", route_step, dve.tensor_copy(counts_i[0:1, 0, :], RF[0:1, 288:288 + PAIRS]))
            dve.tensor_scalar(counts_i[0:1, 3, :], counts_i[0:1, 0, :], 6, None, ALU.arith_shift_right).then_inc(counts_done, 1)

            dve.wait_ge(counts_done, 1)

            def x_copy(q, n):
                dve.wait_ge(q.x_tr, n + 1)
                bank = 1 if q is main else 7
                dve.tensor_copy(xT[:, q.o, 4:8, :], ps[:, bank, :].rearrange("p (k t) -> p k t", k=4)).then_inc(q.x_dve, 1)

            def gates(q, src, j, n, g):
                for lane in range(2):
                    r = slice(lane * LANE, (lane + 1) * LANE)
                    dve.tensor_copy(gate[r, g:g + 1], src[r, bass.ds(j + D + PAIRS * lane, 1)]).then_inc(q.gate_done, 1)

            def hidden(q, n, g):
                dve.wait_ge(q.silu_done, n + 1)
                dve.wait_ge(q.gate_done, 2 * (n + 1))
                dve.scalar_tensor_tensor(out=hid[:, q.o, :, :].rearrange("t k p -> t p k"),
                                         in0=s_act[:, q.o, :].rearrange("t (p k) -> t p k", k=2), scalar=gate[:, g:g + 1],
                                         in1=ps[:, 2, FH:2 * FH].rearrange("t (p k) -> t p k", k=2),
                                         op0=ALU.mult, op1=ALU.mult).then_inc(q.hid_done, 1)

            def hT_copy(q, n):
                dve.wait_ge(q.h_tr, n + 1)
                dve.tensor_copy(hT[:, q.o, :, :], ps[:, 3, 0:FH].rearrange("p (k t) -> p k t", k=2)).then_inc(q.hT_done, 1)

            def y_copy(q, n, buf):
                dve.wait_ge(q.y_mm, n + 1)
                y_free(dve, q, n)
                dve.tensor_copy(y_sb[:, buf, 512:1024], ps[:, 5, :]).then_inc(q.y_dve, 1)

            more_passes = passes_counter(dve)

            def pair(j, i, b, last):
                hidden(main, j, b)
                if not last:
                    dve.wait_ge((main.gathered0, main.gathered1)[1 - b], 16 * (i + 1 + b))
                    gates(main, g_rows[:, 1 - b, :], j + 1, j + 1, 1 - b)
                    x_copy(main, j + 1)
                hT_copy(main, j)
                y_copy(main, j, b)

                def again(n, p):
                    dve.wait_ge(over.gathered0, 16 * (n + 1))
                    gates(over, more_rows[:, :], j, n, 2)
                    x_copy(over, n)
                    hidden(over, n, 2)
                    hT_copy(over, n)
                    y_copy(over, n, 2)

                more_passes(j, again)

            dve.wait_ge(main.gathered0, 16)
            gates(main, g_rows[:, 0, :], 0, 0, 0)
            x_copy(main, 0)
            run_pairs(dve, pair)

        @block.gpsimd
        def _(pool):
            pool.memset(neg_half[:, :], -0.5).then_inc(neg_half_set, 1)
            pool.wait_ge(neg_half_set, 1)

            S = stats

            def x_part(i):
                pool.wait_ge(x_sq, i + 1)
                pool.tensor_scalar(S[:, 1:2], S[:, 0:1], 1.0 / D, EPS, ALU.mult, ALU.add).then_inc(x_ms, 1)
                pool.wait_ge(x_ms, i + 1)
                if i >= 1:
                    pool.wait_ge(xn_done, i)
                pool.tensor_tensor(S[:, 2:3], S[:, 1:2], neg_half[:, 0:1], ALU.pow).then_inc(x_rstd, 1)

            x_part(0)
            for i in range(NT):
                if i + 1 < NT:
                    x_part(i + 1)
                pool.wait_ge(c_sq, 3 * (i + 1))
                pool.tensor_scalar(S[:, 10:11], S[:, 4:5], 1.0 / RQ, EPS, ALU.mult, ALU.add).then_inc(c_ms, 1)
                pool.tensor_scalar(S[:, 11:12], S[:, 5:6], 1.0 / RKV, EPS, ALU.mult, ALU.add).then_inc(c_ms, 1)
                pool.wait_ge(c_ms, 2 * (i + 1))
                if i >= 1:
                    pool.wait_ge(cn_done, 2 * i)
                pool.tensor_tensor(S[:, 8:10], S[:, 10:12], neg_half[:, 0:2], ALU.pow).then_inc(c_rstd, 1)
                pool.wait_ge(q_ss, i + 1)
                pool.tensor_scalar(S[:, 16:20], S[:, 12:16], 1.0 / DQK, EPS, ALU.mult, ALU.add).then_inc(q_ms, 1)
                pool.wait_ge(q_ms, i + 1)
                if i >= 1:
                    pool.wait_ge(qn_done, i)
                pool.tensor_tensor(S[:, 20:24], S[:, 16:20], neg_half[:, 0:4], ALU.pow).then_inc(q_rstd, 1)
                pool.wait_ge(k_ss, i + 1)
                pool.tensor_scalar(S[:, 32:36], S[:, 28:32], S[:, 6:7], 1.0 / DQK, ALU.add, ALU.mult).then_inc(k_ms, 1)
                pool.wait_ge(k_ms, i + 1)
                pool.tensor_scalar(S[:, 36:40], S[:, 32:36], EPS, None, ALU.add).then_inc(k_eps, 1)
                pool.wait_ge(k_eps, i + 1)
                if i >= 1:
                    pool.wait_ge(kr_done, i)
                pool.tensor_tensor(S[:, 40:44], S[:, 36:40], neg_half[:, 0:4], ALU.pow).then_inc(k_rstd, 1)

            pool.wait_ge(setup_dram, 48)

            def fill_slots(i):
                pool.wait_ge(pos_done, i + 1)
                for c in range(2):
                    pool.indirect_dma_start(
                        out=slot_table, out_offset=bass.IndirectOffsetOnAxis(ap=idx_pos[:, i, c:c + 1], axis=0),
                        in_=tok_ids[:, i:i + 1], in_offset=None).then_inc(slots_stored, 16)

            for i in range(NT):
                pool.wait_ge(h_sq, i + 1)
                pool.tensor_scalar(route_f[:, 401:402], route_f[:, 400:401], 1.0 / D, EPS, ALU.mult, ALU.add).then_inc(h_ms, 1)
                pool.wait_ge(h_ms, i + 1)
                if i >= 1:
                    pool.wait_ge(a2_done, i)
                pool.tensor_tensor(route_f[:, 402:403], route_f[:, 401:402], neg_half[:, 0:1], ALU.pow).then_inc(h_rstd, 1)
                if i >= 2:
                    fill_slots(i - 2)
            fill_slots(NT - 2)
            fill_slots(NT - 1)

            pool.wait_ge(idx_in, 16)
            pool.wait_ge(rows_stored, 16 * NT)
            pool.wait_ge(h_stored, 16 * NT)
            pool.wait_ge(counts_done, 1)

            def gather(dst, idx, done):
                pool.indirect_dma_start(out=dst, out_offset=None, in_=table,
                                        in_offset=bass.IndirectOffsetOnAxis(ap=idx, axis=0)).then_inc(done, 16)

            def ready(*waits):
                for signal, value in waits:
                    pool.wait_ge(signal, value)
                pool.sem_inc(dma_go, 1)

            def set_idx(col, j):
                pool.tensor_copy(idx_now[:, col:col + 1], idx_all[:, bass.ds(j, 1)]).then_inc(idx_set, 1)

            def gather_pair(j, b, count):
                set_idx(b, j)
                ready((idx_set, count))
                gather(g_rows[:, b, :], idx_now[:, b:b + 1], (main.gathered0, main.gathered1)[b])

            def add_rows(q, n, buf, idx):
                pool.indirect_dma_start(out=out, out_offset=bass.IndirectOffsetOnAxis(ap=idx, axis=0),
                                        in_=y_sb[:, buf, :], in_offset=None, compute_op=ALU.add).then_inc(q.added, 16)

            more_passes = passes_counter(pool)

            def pair(j, i, b, last):
                ahead = not (isinstance(j, int) and j >= PAIRS - 2)
                if ahead:
                    pool.wait_ge(main.x_tr, j + 1)
                    pool.wait_ge(main.gate_done, 2 * (j + 1))
                    gather_pair(j + 2, b, 2 * j + 3)
                set_idx(2 + b, j)
                waits = [(idx_set, add_count(j)), (main.y_act, j + 1), (main.y_dve, j + 1)]
                if not (isinstance(j, int) and j == 0):
                    waits.append((main.added, 16 * j))
                ready(*waits)
                add_rows(main, j, b, idx_now[:, 2 + b:3 + b])

                def again(n, p):
                    src = slot_table.rearrange("(a s j) c -> a s (j c)", s=2 * LANE, j=PAIRS)
                    with nc.allow_non_contiguous_dma(reason="128 indices"):
                        pool.dma_start(idx_now[:, 4:5], src[bass.ds(p, 1), :, bass.ds(j, 1)].rearrange("a s c -> (a s) c")).then_inc(over_idx_in, 16)
                    ready((over_idx_in, 16 * (n + 1)))
                    gather(more_rows[:, :], idx_now[:, 4:5], over.gathered0)
                    ready((over.y_act, n + 1), (over.y_dve, n + 1), (main.added, 16 * (j + 1)))
                    add_rows(over, n, 2, idx_now[:, 4:5])
                    pool.wait_ge(over.added, 16 * (n + 1))

                more_passes(j, again)

            def add_count(j):
                if isinstance(j, int) and j >= PAIRS - 2:
                    return PAIRS + j + 1
                return 2 * j + 4

            gather_pair(0, 0, 1)
            gather_pair(1, 1, 2)
            run_pairs(pool, pair)
            pool.wait_ge(main.added, 16 * PAIRS)


_INS = ["x_prompt", "x_sample", "g_attn_norm", "w_in", "g_q_lat", "g_kv_lat", "w_uq", "w_ukv", "g_q_head", "g_k_head",
        "w_pool", "pool_scale", "w_out", "g_ffn_norm", "w_group_router", "b_group_router", "w_expert_router",
        "b_expert_router", "w_gate", "w_up", "w_down"]


def kernel(**inputs):
    import concourse.bacc as _bacc
    from concourse.bass_utils import run_bass_kernel_spmd as _run

    nc = _bacc.Bacc("TRN2", target_bir_lowering=False, num_devices=1)
    arrays, args = {}, {}
    named = {name: inputs[name] for name in _INS}
    named.update(host_constants())
    for name, x in named.items():
        x = np.ascontiguousarray(x)
        arrays[f"in_{name}"] = x
        args[name] = nc.dram_tensor(f"in_{name}", x.shape, mybir.dt.from_np(x.dtype), kind="ExternalInput").ap()
    out = nc.dram_tensor("out", [T + P, D], F32, kind="ExternalOutput").ap()
    build(nc, args, out)
    r = _run(nc, [arrays], core_ids=[0])
    y = np.asarray(r.results[0]["out"])
    return y[0:SEQS[0]].reshape(1, SEQS[0], D), y[SEQS[0]:T].reshape(1, SEQS[1], D)
```

```python
from contextlib import ExitStack

import numpy as np

import concourse.bass as bass
from concourse import mybir
from concourse.alu_op_type import AluOpType as ALU

F32 = mybir.dt.float32
F32R = mybir.dt.float32r
BF16 = mybir.dt.bfloat16
I32 = mybir.dt.int32
U32 = mybir.dt.uint32
ACT = mybir.ActivationFunctionType
AX = mybir.AxisListType

P = 128
D = 1024
KD = D // P
SEQS = (512, 256)
T = sum(SEQS)
NT = T // P
FIRST = (0, SEQS[0] // P)
TILES = tuple(s // P for s in SEQS)
H = 4
DN, DR, DV = 128, 64, 128
DQK = DN + DR
RQ, RKV = 384, 256
KQ, KKV = RQ // P, RKV // P
NU = 512
NG, GC = 4, 128
IN_W = RQ + RKV + DR + NU
WINDOWS = (2, 4, 8, 16)
HALO = max(WINDOWS) // 2
BANDW = P + 2 * HALO
EG, EPG = 4, 8
E = EG * EPG
FH = 256
LANE = 64
PAIRS = E // 2
PASSES = T // LANE
BLOCK = 2 * LANE * PAIRS
ROW = D + E
EPS = 1e-6
SCALE = float(DQK) ** -0.5
BIG = 1e30

C_ID, C_LTRI, C_COS, C_SIN = 0, P, 2 * P, 2 * P + 4 * DR
C_IOTA = C_SIN + 4 * DR
C_EBASE = C_IOTA + E
C_W = C_EBASE + E


def host_constants():
    c = np.zeros((P, C_W), np.float32)
    c[:, C_ID:C_ID + P] = np.eye(P)
    c[:, C_LTRI:C_LTRI + P] = np.triu(np.ones((P, P)), 1)
    inv = (1.0 / (np.float32(10000.0) ** (np.arange(0, DR, 2, dtype=np.float32) / np.float32(DR)))).astype(np.float32)
    pos = np.arange(max(SEQS), dtype=np.float32)
    ang = (pos[:, None] * inv[None, :]).astype(np.float32)
    cos = np.concatenate([np.cos(ang)] * 2, -1).reshape(-1, P, DR)
    sin = np.concatenate([-np.sin(ang), np.sin(ang)], -1).reshape(-1, P, DR)
    c[:, C_COS:C_COS + 4 * DR] = cos.transpose(1, 0, 2).reshape(P, -1)
    c[:, C_SIN:C_SIN + 4 * DR] = sin.transpose(1, 0, 2).reshape(P, -1)
    e = np.arange(E)
    c[:, C_IOTA:C_IOTA + E] = e
    c[:, C_EBASE:C_EBASE + E] = (e // PAIRS) * (LANE * PAIRS) + e % PAIRS
    band = np.zeros((P, NG, 3, BANDW), np.float32)
    s = 3 * P
    for g, w in enumerate(WINDOWS):
        full = np.zeros((s, s), np.float64)
        for t in range(s):
            lo, hi = max(t - w // 2, 0), min(t + w - w // 2, s)
            full[lo:hi, t] = 1.0 / (hi - lo)
            full[t, t] -= 1.0
        for kind in range(3):
            for col in range(BANDW):
                t = kind * P - HALO + col
                if 0 <= t < s:
                    band[:, g, kind, col] = full[kind * P:(kind + 1) * P, t]
    tokens = (np.arange(P)[:, None] + P * np.arange(NT)[None, :]).astype(np.int32)
    slots = np.broadcast_to((T + np.arange(2 * LANE))[None, :, None], (PASSES, 2 * LANE, PAIRS))
    slots = np.ascontiguousarray(slots.reshape(-1, 1).astype(np.int32))
    zeros = np.zeros((P, ROW), np.float32)
    return {"consts": c, "band": band.reshape(P, -1), "tokens": tokens, "slots": slots, "zeros": zeros}


def build(nc, a, out):
    table = nc.dram_tensor("token_rows", [T + P, ROW], F32, kind="Internal").ap()
    slot_table = nc.dram_tensor("slot_tokens", [PASSES * BLOCK, 1], I32, kind="Internal").ap()

    ctx = ExitStack()
    with ctx:
        def sem(name):
            return ctx.enter_context(nc.semaphore(name))

        def region(size, *groups):
            got = []
            for group in groups:
                with ExitStack() as one:
                    used = 0
                    for name, shape, dt in group:
                        got.append(one.enter_context(nc.sbuf_tensor(name, shape, dt)))
                        used += (int(np.prod(shape[1:])) * (2 if dt == BF16 else 4) + 31) // 32 * 32
                    assert used <= size, (group[0][0], used, size)
            hold = group[0][0] + "_region"
            ctx.enter_context(nc.sbuf_tensor(hold, [P, size // 4], F32))
            return got

        (consts, bf_consts, g_attn, g_lat, g_nope, g_pool, tok_ids, neg_half, idx_pos, counts_i,
         m_sum, w_router) = region(
            6 * 1024,
            [("consts_sb", [P, C_W], F32), ("bf_consts", [P, 2, P], BF16), ("g_attn", [P, KD], F32),
             ("g_lat", [P, KQ + KKV], F32), ("g_nope", [P, 2], F32), ("g_pool", [P, NG], F32),
             ("tok_ids", [P, NT], I32), ("neg_half", [P, 8], F32),
             ("idx_pos", [P, NT, 2], I32), ("counts_i", [1, 4, PAIRS], I32), ("m_sum", [P, 2, E], BF16),
             ("w_router", [P, KD, EG + E], F32)])
        W_BYTES = 2 * (2 * KD * FH + 2 * D) * 4
        (w0, w_in_lo, w_uq_lo, q_x) = region(
            W_BYTES,
            [("expert_w0", [P, 2, 3, 2 * D], F32)],
            [("w_in_lo", [P, KD, IN_W], F32R), ("w_uq_lo", [P, KQ, H * DQK], F32R), ("q_x", [P, H, DR], F32)])
        (qT, kT, w_in_hi, w_in_raw0, w_uq_raw, _, w_out, w2, xT, s_act, hid, hT) = region(
            2 * H * T * 4 + KD * IN_W * 4,
            [("qT", [P, H, T], F32), ("kT", [P, H, T], F32), ("w_in_hi", [P, KD, IN_W], F32R)],
            [("w_in_raw0", [P, KD, RQ], F32), ("w_uq_raw", [P, KQ, H * DQK], F32)],
            [("under_w_out", [P, 2 * H * T], F32), ("w_out_sb", [P, KD, D], F32)],
            [("expert_w2", [P, 2, 3, 2 * D], F32), ("xT", [P, 2, KD, P], F32), ("s_act", [P, 2, FH], F32),
             ("hid", [P, 2, 2, P], F32), ("hT", [P, 2, 2, P], F32)])
        (rT, v_sb, u_sb, w_in_raw2, aT0, _, w_in_raw1, x_res, h_sb, rows, a2T, g_ffn, route_f, route_u, h_junk, r_bias,
         g_rows, more_rows, y_sb, idx_all, idx_more, idx_now, gate) = region(
            3 * H * T * 4,
            [("rT", [P, 4, T], F32), ("v_sb", [P, NT, H * DV], F32), ("u_sb", [P, NT, NU], F32)],
            [("w_in_raw2", [P, KD, NU], F32), ("aT0", [P, KD, P], F32), ("under_raw1", [P, D], F32),
             ("w_in_raw1", [P, KD, RKV + DR], F32)],
            [("x_res", [P, D], F32), ("h_sb", [P, 2, D], F32), ("rows", [P, 2, ROW], F32),
             ("a2T", [P, KD, P], F32), ("g_ffn", [P, D], F32), ("route_f", [P, 420], F32),
             ("route_u", [P, 24], U32), ("h_junk", [P, D], F32), ("r_bias", [P, EG + E], F32)],
            [("g_rows", [P, 3, ROW], F32), ("more_rows", [P, ROW], F32), ("y_sb", [P, 4, D], F32),
             ("idx_all", [P, PAIRS + 1], I32), ("idx_more", [P, PAIRS], I32), ("idx_now", [P, 7], I32), ("gate", [P, 4], F32)])
        (w_uq_hi, w_ukv, x_sb, xn, aT_hi, aT_lo, cn, cT_hi, cT_lo, cT_kv, junk, q_n, q_r, k_n, k_raw, k_r, rope_t, rope_k, rope_tab, stats,
         p_sb, pT, dT, band, w_pool, a_stat, w1) = region(
            56512,
            [("w_uq_hi", [P, KQ, H * DQK], F32R), ("w_ukv_sb", [P, KKV, H * (DN + DV)], F32),
             ("x_sb", [P, D], F32), ("xn", [P, KD, P], F32), ("aT_hi", [P, KD, P], F32R),
             ("aT_lo", [P, KD, P], F32R), ("cn", [P, KQ + KKV, P], F32), ("cT_hi", [P, KQ, P], F32R),
             ("cT_lo", [P, KQ, P], F32R), ("cT_kv", [P, KKV, P], F32), ("junk", [P, H * DQK], F32),
             ("q_n", [P, H, DN], F32), ("q_r", [P, H, DR], F32),
             ("k_n", [P, H, DN], F32), ("k_raw", [P, DR], F32), ("k_r", [P, H, DR], F32),
             ("rope_t", [P, 2, H, DR], F32), ("rope_k", [P, DR], F32), ("rope_tab", [P, 4, 4, DR], F32),
             ("stats", [P, 48], F32)],
            [("p_sb", [P, 4, 512], F32), ("pT", [P, 2, 4, 512], F32), ("dT", [P, 2, T], F32),
             ("band_sb", [P, NG, 3, BANDW], F32), ("w_pool_sb", [P, NG, GC], F32), ("a_stat", [P, 4, 4], F32)],
            [("expert_w1", [P, 2, 3, 2 * D], F32)])
        weights = (w0, w1, w2)
        w_in_raw = (w_in_raw0, w_in_raw1, w_in_raw2)
        W_CUTS = (0, RQ, RQ + RKV + DR, IN_W)
        g_rope = q_x

        ps = ctx.enter_context(nc.psum_tensor("ps", [P, 8, 512], F32))

        ident = consts[:, C_ID:C_ID + P]
        iota = consts[:, C_IOTA:C_IOTA + E]
        ebase = consts[:, C_EBASE:C_EBASE + E]
        ones_bf, ltri_bf = bf_consts[:, 0, :], bf_consts[:, 1, :]

        consts_in, g_attn_in, gains_in, setup_dram = (sem(n) for n in ("consts_in", "g_attn_in", "gains_in", "setup_dram"))
        x_in = sem("x_in")
        w_in_in = [sem(f"w_in_in{n}") for n in range(3)]
        w_up_in, w_out_in, pool_in = sem("w_up_in"), sem("w_out_in"), sem("pool_in")
        x_res_in, g_ffn_in = sem("x_res_in"), sem("g_ffn_in")
        part_in = [[sem(f"weights{b}_part{n}_in") for n in range(6)] for b in range(3)]
        neg_half_set, tables_set, bf_set = sem("neg_half_set"), sem("tables_set"), sem("bf_set")
        x_sq, x_ms, x_rstd, xn_done = sem("x_sq"), sem("x_ms"), sem("x_rstd"), sem("xn_done")
        x_tr, aT_full, aT_hi_done, aT_done = (sem(n) for n in ("x_tr", "aT_full", "aT_hi_done", "aT_done"))
        w_hi_done, w_lo_done = sem("w_hi_done"), sem("w_lo_done")
        cT_full, cT_hi_done = sem("cT_full"), sem("cT_hi_done")
        p1_done, p2_done, p3_done = sem("p1_done"), sem("p2_done"), sem("p3_done")
        c_sq, c_ms, c_rstd, cn_done, k_raw_done = sem("c_sq"), sem("c_ms"), sem("c_rstd"), sem("cn_done"), sem("k_raw_done")
        c_tr, cT_done, u_done = sem("c_tr"), sem("cT_done"), sem("u_done")
        q_mm, kv_mm, q_sq, q_ss, q_ms, q_rstd = (sem(n) for n in ("q_mm", "kv_mm", "q_sq", "q_ss", "q_ms", "q_rstd"))
        k_sq, k_ss, k_ms, k_eps, k_rstd, v_done = (sem(n) for n in ("k_sq", "k_ss", "k_ms", "k_eps", "k_rstd", "v_done"))
        qn_done, qx_done, kn_done, rope_step, qr_done, kr_done = (
            sem(n) for n in ("qn_done", "qx_done", "kn_done", "rope_step", "qr_done", "kr_done"))
        qn_tr, kn_tr, r_tr, qT_done, kT_done, rT_done = (
            sem(n) for n in ("qn_tr", "kn_tr", "r_tr", "qT_done", "kT_done", "rT_done"))
        s_ready, row_max, neg_max, exp_done, recip_done, p_done, p_tr = (
            sem(n) for n in ("s_ready", "row_max", "neg_max", "exp_done", "recip_done", "p_done", "p_tr"))
        pT_act, pT_dve = sem("pT_act"), sem("pT_dve")
        pv_done, o_act, o_dve = sem("pv_done"), sem("o_act"), sem("o_dve")
        d_mm, dT_done, mix_mm, mix_done = sem("d_mm"), sem("dT_done"), sem("mix_mm"), sem("mix_done")
        o_mm, h_done, h_sq, h_ms, h_rstd, a2_done = (sem(n) for n in ("o_mm", "h_done", "h_sq", "h_ms", "h_rstd", "a2_done"))
        a2_tr, a2T_done, lg_mm, lg_bias = (sem(n) for n in ("a2_tr", "a2T_done", "lg_mm", "lg_bias"))
        route_step, g_exp, e_exp, neg_g, e_diff = (sem(n) for n in ("route_step", "g_exp", "e_exp", "neg_g", "e_diff"))
        mask_done, rank_mm, pos_done, gates_done = (sem(n) for n in ("mask_done", "rank_mm", "pos_done", "gates_done"))
        h_stored, rows_stored, slots_stored = sem("h_stored"), sem("rows_stored"), sem("slots_stored")
        total_mm, counts_done = sem("total_mm"), sem("counts_done")
        idx_in, idx_set = sem("idx_in"), sem("idx_set")

        class PassSignals:

            def __init__(self, prefix, o):
                self.o = o
                self.gathered = [sem(f"{prefix}gathered{b}") for b in range(3 if o == 0 else 1)]
                self.x_tr, self.x_act, self.x_dve = sem(prefix + "x_tr"), sem(prefix + "x_act"), sem(prefix + "x_dve")
                self.gu_mm, self.silu_done = sem(prefix + "gu_mm"), sem(prefix + "silu_done")
                self.gate_done, self.hid_done = sem(prefix + "gate_done"), sem(prefix + "hid_done")
                self.h_tr, self.hT_done, self.y_mm = sem(prefix + "h_tr"), sem(prefix + "hT_done"), sem(prefix + "y_mm")
                self.y_act, self.y_dve, self.added = sem(prefix + "y_act"), sem(prefix + "y_dve"), sem(prefix + "added")

        main, over = PassSignals("main_", 0), PassSignals("more_", 1)
        pair_done = sem("pair_done")
        dma_go = sem("dma_go")
        over_idx_in, more_set = sem("more_idx_in"), sem("more_idx_set")

        def w_gu(b, lane, k):
            return weights[b][:, lane, 0:2, k * FH:(k + 1) * FH]

        def w_dn(b, lane, k, n):
            return weights[b][:, lane, 2, k * D + n * 512:k * D + (n + 1) * 512]

        units = [(s, hp, qt) for s in range(2) for hp in range(2) for qt in range(TILES[s])]
        last_of_head = [m for m, (s, hp, qt) in enumerate(units) if qt == TILES[s] - 1]

        def x_dram(i):
            s = 0 if i < FIRST[1] else 1
            r = (i - FIRST[s]) * P
            return a["x_prompt" if s == 0 else "x_sample"][0, r:r + P, :]

        def load_pair(sp, j, b, i, parts=range(6)):
            for n in parts:
                lane, what = (n // 2, n % 2) if n < 4 else (n - 4, 2)
                if n >= 3:
                    sp.wait_ge(part_in[b][n - 3], 16 * (i + 1))
                name, k = ("w_gate", "w_up", "w_down")[what], 2 if what == 2 else KD
                src = a[name][0, bass.ds(PAIRS * lane + j, 1)].rearrange("e (p k) f -> p (e k f)", k=k)
                sp.dma_start(weights[b][:, lane, what, :], src).then_inc(part_in[b][n], 16)

        def pe_y_free(pe, j):
            if isinstance(j, int) and j == 0:
                return
            pe.wait_ge(main.y_act, j)
            pe.wait_ge(main.y_dve, j)

        def run_pairs(eng, pair):
            for b in range(3):
                pair(b, 0, b, False)
            with eng.Fori(1, PAIRS // 3) as i:
                for b in range(3):
                    pair(3 * i + b, i, b, False)
            pair(PAIRS - 1, PAIRS // 3, 0, True)

        def passes_counter(eng):
            before = eng.alloc_register("more_before")
            eng.reg_mov(before, 0)

            def run(j, again):
                todo = eng.value_load(counts_i[0:1, 3, bass.ds(j, 1)], min_val=0, max_val=PASSES - 1)
                with eng.If(todo > 0):
                    with eng.Fori(1, todo + 1) as p:
                        n = eng.snap(before)
                        again(n, p)
                        eng.reg_add(before, before, 1)
            return run

        def y_free(eng, q, n):
            if q is over:
                if not (isinstance(n, int) and n == 0):
                    eng.wait_ge(over.added, 16 * n)
            elif not (isinstance(n, int) and n < 3):
                eng.wait_ge(main.added, 16 * (n - 2))

        def pT_copy(eng, m, u):
            s, hp, qt = units[m]
            eng.wait_ge(p_tr, 2 * m + u + 1)
            g = sum(1 for x in last_of_head if x < m)
            if g >= 1:
                eng.wait_ge(pv_done, 2 * g)
            dst = pT[:, u, 0:TILES[s], qt * P:(qt + 1) * P]
            src = ps[:, 4 + u, 0:SEQS[s]].rearrange("p (c t) -> p c t", c=TILES[s])
            if u == 0:
                eng.activation(dst, src, ACT.Copy).then_inc(pT_act, 1)
            else:
                eng.tensor_copy(dst, src).then_inc(pT_dve, 1)

        def o_copy(eng, m, u):
            s, hp, qt = units[m]
            eng.wait_ge(pv_done, 2 * last_of_head.index(m) + u + 1)
            dst = qT[:, 2 * hp + u, FIRST[s] * P:FIRST[s] * P + SEQS[s]]
            if u == 0:
                eng.activation(dst, ps[:, 6, 0:SEQS[s]], ACT.Copy).then_inc(o_act, 1)
            else:
                eng.tensor_copy(dst, ps[:, 7, 0:SEQS[s]]).then_inc(o_dve, 1)

        N_GAINS = 14
        block = ctx.enter_context(nc.Block())

        @block.sync
        def _(sp):
            sp.dma_start(x_sb[:, :], x_dram(0)).then_inc(x_in, 16)
            sp.dma_start(consts[:, :], a["consts"]).then_inc(consts_in, 16)
            with nc.allow_non_contiguous_dma(reason="128 short rows"):
                sp.dma_start(g_attn[:, :], a["g_attn_norm"][0].rearrange("(p k) -> p k", k=KD)).then_inc(g_attn_in, 16)
            w_in_d = a["w_in"][0].rearrange("(p k) n -> p k n", k=KD)
            
            def load_w_in(n):
                sp.dma_start(w_in_raw[n][:, :, :], w_in_d[:, :, W_CUTS[n]:W_CUTS[n + 1]]).then_inc(w_in_in[n], 16)

            load_w_in(0)
            gains = [
                (g_lat[:, 0:KQ], a["g_q_lat"][0].rearrange("(p k) -> p k", k=KQ)),
                (g_lat[:, KQ:], a["g_kv_lat"][0].rearrange("(p k) -> p k", k=KKV)),
                (g_nope[:, 0:1], a["g_q_head"][0, 0:DN].rearrange("(p k) -> p k", k=1)),
                (g_nope[:, 1:2], a["g_k_head"][0, 0:DN].rearrange("(p k) -> p k", k=1)),
                (g_pool[:, :], a["pool_scale"][0].rearrange("(g p) -> p g", p=P)),
                (tok_ids[:, :], a["tokens"]),
                (w_router[:, :, 0:EG], a["w_group_router"][0].rearrange("(p k) n -> p k n", k=KD)),
                (w_router[:, :, EG:], a["w_expert_router"][0].rearrange("(p k) n -> p k n", k=KD)),
            ]
            half = DR // 2
            for n, name in enumerate(("g_q_head", "g_k_head")):
                g = a[name][0:1, DN:DQK]
                gains += [(g_rope[:, 2 * n, :], g.partition_broadcast(P)),
                          (g_rope[:, 2 * n + 1, 0:half], g[:, half:DR].partition_broadcast(P)),
                          (g_rope[:, 2 * n + 1, half:DR], g[:, 0:half].partition_broadcast(P))]
            with nc.allow_non_contiguous_dma(reason="a few hundred short rows"):
                for dst, src in gains:
                    sp.dma_start(dst, src).then_inc(gains_in, 16)
            assert len(gains) == N_GAINS
            load_w_in(1)
            sp.wait_ge(xn_done, 1)
            sp.dma_start(x_sb[:, :], x_dram(1)).then_inc(x_in, 16)
            load_w_in(2)
            sp.dma_start(w_uq_raw[:, :, :], a["w_uq"][0].rearrange("(p k) n -> p k n", k=KQ)).then_inc(w_up_in, 16)
            sp.dma_start(w_ukv[:, :, :], a["w_ukv"][0].rearrange("(p k) n -> p k n", k=KKV)).then_inc(w_up_in, 16)
            sp.dma_start(slot_table.rearrange("(a b) c -> a (b c)", a=P),
                         a["slots"].rearrange("(a b) c -> a (b c)", a=P)).then_inc(setup_dram, 16)
            sp.dma_start(table[T:T + P, :], a["zeros"]).then_inc(setup_dram, 16)
            sp.dma_start(out[T:T + P, :], a["zeros"][:, 0:D]).then_inc(setup_dram, 16)
            for i in range(2, NT):
                sp.wait_ge(xn_done, i)
                sp.dma_start(x_sb[:, :], x_dram(i)).then_inc(x_in, 16)
            sp.wait_ge(p3_done, NT)
            sp.dma_start(w_out[:, :, :], a["w_out"][0].rearrange("(k p) n -> p k n", p=P)).then_inc(w_out_in, 16)
            sp.wait_ge(kv_mm, NT)
            sp.wait_ge(r_tr, NT)
            sp.wait_ge(qT_done, NT)
            sp.wait_ge(kT_done, NT)
            sp.wait_ge(rT_done, NT)
            sp.wait_ge(v_done, NT)
            sp.dma_start(band[:, :, :, :], a["band"].rearrange("p (g k c) -> p g k c", g=NG, k=3)).then_inc(pool_in, 16)
            sp.dma_start(w_pool[:, :, :], a["w_pool"][0].rearrange("g c d -> c g d")).then_inc(pool_in, 16)
            sp.wait_ge(q_mm, NT)
            sp.wait_ge(qr_done, NT)
            load_pair(sp, 0, 0, 0)
            sp.wait_ge(d_mm, NG)
            sp.dma_start(x_res[:, :], x_dram(0)).then_inc(x_res_in, 16)
            sp.dma_start(g_ffn[:, :], a["g_ffn_norm"].partition_broadcast(P)).then_inc(g_ffn_in, 16)
            sp.dma_start(r_bias[:, 0:EG], a["b_group_router"].partition_broadcast(P)).then_inc(g_ffn_in, 16)
            sp.dma_start(r_bias[:, EG:], a["b_expert_router"].partition_broadcast(P)).then_inc(g_ffn_in, 16)
            sp.wait_ge(mix_mm, NG)
            sp.wait_ge(dT_done, 2 * NG)
            load_pair(sp, 1, 1, 0)
            for i in range(NT):
                sp.wait_ge(h_done, 2 * (i + 1))
                sp.dma_start(out[i * P:(i + 1) * P, :], h_sb[:, i % 2, :]).then_inc(h_stored, 16)
                if i + 1 < NT:
                    sp.dma_start(x_res[:, :], x_dram(i + 1)).then_inc(x_res_in, 16)
                else:
                    load_pair(sp, 2, 2, 0, range(2))
                sp.wait_ge(gates_done, i + 1)
                sp.dma_start(table[i * P:(i + 1) * P, :], rows[:, i % 2, :]).then_inc(rows_stored, 16)
            sp.wait_ge(slots_stored, 2 * NT * 16)
            sp.wait_ge(counts_done, 1)
            sp.dma_start(idx_all[:, 0:PAIRS], slot_table[0:BLOCK, :].rearrange("(s j) c -> s (j c)", j=PAIRS)).then_inc(idx_in, 16)
            sp.dma_start(idx_more[:, :], slot_table[BLOCK:2 * BLOCK, :].rearrange("(s j) c -> s (j c)", j=PAIRS)).then_inc(idx_in, 16)
            with nc.allow_non_contiguous_dma(reason="128 indices"):
                sp.dma_start(idx_all[:, PAIRS:], a["slots"][0:BLOCK, :].rearrange("(s j) c -> s (j c)", j=PAIRS)[:, 0:1]).then_inc(idx_in, 16)

            sp.wait_ge(main.gathered[0], 16)
            load_pair(sp, 2, 2, 0, range(2, 6))

            def refill(j, i, b):
                sp.wait_ge(main.y_mm, j - 2)
                sp.wait_ge(pair_done, j - 2)
                load_pair(sp, j, b, i)

            with sp.Fori(1, PAIRS // 3) as i:
                for b in range(3):
                    refill(3 * i + b, i, b)
            refill(PAIRS - 1, PAIRS // 3, 0)

        @block.tensor
        def _(pe):
            def x_transposes(i):
                pe.wait_ge(xn_done, i + 1)
                if i >= 1:
                    pe.wait_ge(aT_full, 2 * i)
                if i == 0:
                    pe.wait_ge(consts_in, 16)
                for k in range(KD):
                    mm = pe.transpose(ps[:, k // 4, (k % 4) * P:(k % 4 + 1) * P], xn[:, k, :], ident)
                    if k % 4 == 3:
                        mm.then_inc(x_tr, 1)

            def split_product(dst, chunks, l_hi, l_lo, r_hi, r_lo):
                for k in range(chunks):
                    pe.matmul(dst, l_hi(k), r_hi(k), start=(k == 0), stop=False)
                    pe.matmul(dst, l_hi(k), r_lo(k), start=False, stop=False)
                    mm = pe.matmul(dst, l_lo(k), r_hi(k), start=False, stop=(k == chunks - 1))
                return mm

            def project(i, n, bank, done):
                lo, hi = W_CUTS[n], W_CUTS[n + 1]
                dst = ps[:, bank, 0:hi - lo]
                if i == 0:
                    pe.wait_ge(w_in_in[n], 16)
                    for k in range(KD):
                        mm = pe.matmul(dst, aT0[:, k, :], w_in_raw[n][:, k, :], start=(k == 0), stop=(k == KD - 1))
                else:
                    pe.wait_ge(w_lo_done, n + 1)
                    mm = split_product(dst, KD, lambda k: aT_hi[:, k, :], lambda k: aT_lo[:, k, :],
                                       lambda k: w_in_hi[:, k, lo:hi], lambda k: w_in_lo[:, k, lo:hi])
                mm.then_inc(done, 1)

            def head_transposes(i, src, ready, done):
                pe.wait_ge(ready, i + 1)
                for h in range(H):
                    mm = pe.transpose(ps[:, 7, h * P:(h + 1) * P], src[:, h, :], ident)
                mm.then_inc(done, 1)

            def rope_transposes(i):
                pe.wait_ge(qr_done, i + 1)
                pe.wait_ge(kr_done, i + 1)
                pe.wait_ge(kT_done, i + 1)
                for n, src in enumerate((q_r, k_r)):
                    flat = src[:, :, :].rearrange("t h r -> t (h r)")
                    for hp in range(2):
                        mm = pe.transpose(ps[:, 7, (2 * n + hp) * P:(2 * n + hp + 1) * P], flat[:, hp * P:(hp + 1) * P], ident)
                mm.then_inc(r_tr, 1)

            x_transposes(0)
            for i in range(NT):
                if i == 0:
                    pe.wait_ge(aT_full, 2)
                else:
                    pe.wait_ge(aT_done, i)
                    pe.wait_ge(q_sq, i)
                    pe.wait_ge(qn_done, i)
                project(i, 0, 2, p1_done)
                if i >= 1:
                    if i >= 2:
                        pe.wait_ge(rT_done, i - 1)
                    head_transposes(i - 1, q_n, qn_done, qn_tr)
                project(i, 1, 3, p2_done)
                if i >= 1:
                    pe.wait_ge(qT_done, i)
                    head_transposes(i - 1, k_n, kn_done, kn_tr)
                    pe.wait_ge(u_done, i)
                project(i, 2, 4, p3_done)
                pe.wait_ge(cn_done, 2 * (i + 1))
                pe.wait_ge(k_raw_done, i + 1)
                for k in range(KQ + KKV):
                    bank, col = (2, k) if k < KQ else (3, k - KQ)
                    mm = pe.transpose(ps[:, bank, col * P:(col + 1) * P], cn[:, k, :], ident)
                mm.then_inc(c_tr, 1)
                if i + 1 < NT:
                    x_transposes(i + 1)
                if i >= 1:
                    rope_transposes(i - 1)
                pe.wait_ge(cT_done, i + 1)
                pe.wait_ge(w_up_in, 32)
                if i >= 1:
                    pe.wait_ge(w_lo_done, 4)
                for n in range(2):
                    c = slice(n * 384, (n + 1) * 384)
                    if i == 0:
                        for k in range(KQ):
                            mm = pe.matmul(ps[:, 2 + n, 0:384], cn[:, k, :], w_uq_raw[:, k, c], start=(k == 0), stop=(k == KQ - 1))
                    else:
                        mm = split_product(ps[:, 2 + n, 0:384], KQ, lambda k: cT_hi[:, k, :], lambda k: cT_lo[:, k, :],
                                           lambda k: w_uq_hi[:, k, c], lambda k: w_uq_lo[:, k, c])
                mm.then_inc(q_mm, 1)
                if i >= 1:
                    pe.wait_ge(k_sq, i)
                    pe.wait_ge(kn_done, i)
                    pe.wait_ge(v_done, i)
                for n in range(2):
                    for k in range(KKV):
                        mm = pe.matmul(ps[:, 5 + n, :], cT_kv[:, k, :], w_ukv[:, k, n * 512:(n + 1) * 512],
                                       start=(k == 0), stop=(k == KKV - 1))
                mm.then_inc(kv_mm, 1)
            pe.wait_ge(rT_done, NT - 1)
            head_transposes(NT - 1, q_n, qn_done, qn_tr)
            pe.wait_ge(qT_done, NT)
            head_transposes(NT - 1, k_n, kn_done, kn_tr)
            rope_transposes(NT - 1)

            pe.wait_ge(rT_done, NT)
            pe.wait_ge(kT_done, NT)
            pe.wait_ge(v_done, NT)
            pe.wait_ge(k_sq, NT)
            pe.wait_ge(kn_done, NT)
            pe.wait_ge(qn_done, NT)
            pe.wait_ge(u_done, NT)

            def scores(m):
                s, hp, qt = units[m]
                keys = slice(FIRST[s] * P, (FIRST[s] + TILES[s]) * P)
                q = slice((FIRST[s] + qt) * P, (FIRST[s] + qt + 1) * P)
                if m >= 2:
                    pe.wait_ge(exp_done, 2 * (m - 1))
                bank = 2 * (m % 2)
                n = SEQS[s]
                for u in range(2):
                    h = 2 * hp + u
                    pe.matmul(ps[:, bank + u, 0:n], qT[:, h, q], kT[:, h, keys], start=True, stop=False)
                for u in range(2):
                    r = slice(u * DR, (u + 1) * DR)
                    pe.matmul(ps[:, bank + u, 0:n], rT[r, hp, q], rT[r, 2 + hp, keys], start=False, stop=True).then_inc(s_ready, 1)

            def p_transposes(m):
                s, hp, qt = units[m]
                if m >= 1:
                    pe.wait_ge(pT_act, m)
                    pe.wait_ge(pT_dve, m)
                for u in range(2):
                    pe.wait_ge(p_done, 2 * m + u + 1)
                    for c in range(TILES[s]):
                        mm = pe.transpose(ps[:, 4 + u, c * P:(c + 1) * P], p_sb[:, (2 * m + u) % 4, c * P:(c + 1) * P], ident)
                    mm.then_inc(p_tr, 1)

            def attend(m):
                s, hp, qt = units[m]
                g = last_of_head.index(m)
                pe.wait_ge(pT_act, m + 1)
                pe.wait_ge(pT_dve, m + 1)
                if g >= 1:
                    pe.wait_ge(o_act, g)
                    pe.wait_ge(o_dve, g)
                for u in range(2):
                    h = 2 * hp + u
                    for c in range(TILES[s]):
                        mm = pe.matmul(ps[:, 6 + u, 0:SEQS[s]], v_sb[:, FIRST[s] + c, h * DV:(h + 1) * DV],
                                       pT[:, u, c, 0:SEQS[s]], start=(c == 0), stop=(c == TILES[s] - 1))
                    mm.then_inc(pv_done, 1)

            scores(0)
            for m in range(len(units)):
                if m + 1 < len(units):
                    scores(m + 1)
                p_transposes(m)
                if m in last_of_head:
                    attend(m)

            pe.wait_ge(pool_in, 32)

            def windows(g):
                if g >= 2:
                    pe.wait_ge(dT_done, 2 * (g - 1))
                for s in range(2):
                    bank = 2 * (g % 2) + s
                    for t in range(TILES[s]):
                        kind = 0 if t == 0 else 2 if t == TILES[s] - 1 else 1
                        lo, hi = max(t * P - HALO, 0), min((t + 1) * P + HALO, SEQS[s])
                        c = lo - (t * P - HALO)
                        mm = pe.matmul(ps[:, bank, lo:hi], u_sb[:, FIRST[s] + t, g * GC:(g + 1) * GC],
                                       band[:, g, kind, c:c + hi - lo], start=(t == 0), stop=(t == TILES[s] - 1),
                                       skip_group_check=True)
                mm.then_inc(d_mm, 1)

            def mix(g):
                pe.wait_ge(dT_done, 2 * (g + 1))
                if g == 0:
                    pe.wait_ge(o_act, len(last_of_head))
                    pe.wait_ge(o_dve, len(last_of_head))
                if g >= 2:
                    pe.wait_ge(mix_done, 2 * (g - 1))
                for s in range(2):
                    mm = pe.matmul(ps[:, 4 + 2 * (g % 2) + s, 0:SEQS[s]], w_pool[:, g, :],
                                   dT[:, g % 2, FIRST[s] * P:FIRST[s] * P + SEQS[s]], start=True, stop=True)
                mm.then_inc(mix_mm, 1)

            windows(0)
            for g in range(NG):
                if g + 1 < NG:
                    windows(g + 1)
                mix(g)

            pe.wait_ge(mix_done, 2 * NG)
            pe.wait_ge(w_out_in, 16)
            pe.wait_ge(bf_set, 2)

            def out_half(i, n):
                if i >= 2:
                    pe.wait_ge(h_done, 2 * (i - 1))
                for c in range(KD):
                    src = qT if c < H else kT
                    mm = pe.matmul(ps[:, 2 * (i % 2) + n, :], src[:, c % H, i * P:(i + 1) * P],
                                   w_out[:, c, n * 512:(n + 1) * 512], start=(c == 0), stop=(c == KD - 1))
                mm.then_inc(o_mm, 1)

            def row_transposes(i):
                pe.wait_ge(a2_done, i + 1)
                if i >= 1:
                    pe.wait_ge(a2T_done, 2 * i)
                for k in range(KD):
                    mm = pe.transpose(ps[:, 4 + k // 4, (k % 4) * P:(k % 4 + 1) * P], rows[:, i % 2, k * P:(k + 1) * P], ident)
                mm.then_inc(a2_tr, 1)

            def logits(i):
                pe.wait_ge(a2T_done, 2 * (i + 1))
                if i >= 1:
                    pe.wait_ge(lg_bias, i)
                for k in range(KD):
                    mm = pe.matmul(ps[:, 7, 0:EG + E], a2T[:, k, :], w_router[:, k, :], start=(k == 0), stop=(k == KD - 1))
                mm.then_inc(lg_mm, 1)

            def ranks(i):
                pe.wait_ge(mask_done, i + 1)
                if i >= 1:
                    pe.wait_ge(pos_done, i)
                pe.matmul(ps[:, 6, 128:128 + E], ones_bf, m_sum[:, 0, :], start=True, stop=False)
                pe.matmul(ps[:, 6, 128:128 + E], ltri_bf, m_sum[:, 1, :], start=False, stop=True).then_inc(rank_mm, 1)

            for i in range(NT):
                out_half(i, 0)
                if i >= 1:
                    row_transposes(i - 1)
                if i >= 2:
                    ranks(i - 2)
                out_half(i, 1)
                if i >= 1:
                    logits(i - 1)
            row_transposes(NT - 1)
            ranks(NT - 2)
            logits(NT - 1)
            ranks(NT - 1)
            pe.wait_ge(pos_done, NT)
            pe.matmul(ps[:, 7, 0:E], ones_bf, m_sum[:, 0, :], start=True, stop=True).then_inc(total_mm, 1)

            pe.wait_ge(counts_done, 1)

            def gather_transposes(q, src, landed, uses):
                pe.wait_ge(landed, 16 * uses)
                banks = 0 if q is main else 6
                for k in range(KD):
                    mm = pe.transpose(ps[:, banks + k // 4, (k % 4) * P:(k % 4 + 1) * P], src[:, k * P:(k + 1) * P], ident)
                mm.then_inc(q.x_tr, 1)

            def gate_up(q, b, n):
                pe.wait_ge(q.x_act, n + 1)
                pe.wait_ge(q.x_dve, n + 1)
                for k in range(KD):
                    for lane in range(2):
                        r = slice(lane * LANE, (lane + 1) * LANE)
                        mm = pe.matmul(ps[r, 2, :].rearrange("p (g f) -> p g f", g=2), xT[:, q.o, k, r], w_gu(b, lane, k),
                                       start=(k == 0), stop=(k == KD - 1))
                mm.then_inc(q.gu_mm, 1)

            def hidden_transposes(q, n):
                pe.wait_ge(q.hid_done, n + 1)
                for k in range(2):
                    mm = pe.transpose(ps[:, 3, k * P:(k + 1) * P], hid[:, q.o, k, :], ident)
                mm.then_inc(q.h_tr, 1)

            def down(q, b, n):
                pe.wait_ge(q.hT_done, n + 1)
                for half in range(2):
                    for k in range(2):
                        for lane in range(2):
                            r = slice(lane * LANE, (lane + 1) * LANE)
                            mm = pe.matmul(ps[r, 4 + half, :], hT[:, q.o, k, r], w_dn(b, lane, k, half),
                                           start=(k == 0), stop=(k == 1))
                mm.then_inc(q.y_mm, 1)

            more_passes = passes_counter(pe)

            def pair(j, i, b, last):
                for n in range(4):
                    pe.wait_ge(part_in[b][n], 16 * (i + 1))
                gate_up(main, b, j)
                if not last:
                    nb = (b + 1) % 3
                    gather_transposes(main, g_rows[:, nb, :], main.gathered[nb], i + 1 if b < 2 else i + 2)
                hidden_transposes(main, j)
                for n in range(4, 6):
                    pe.wait_ge(part_in[b][n], 16 * (i + 1))
                pe_y_free(pe, j)
                down(main, b, j)

                def again(n, p):
                    gather_transposes(over, more_rows[:, :], over.gathered[0], n + 1)
                    gate_up(over, b, n)
                    hidden_transposes(over, n)
                    pe.wait_ge(main.y_act, j + 1)
                    pe.wait_ge(main.y_dve, j + 1)
                    down(over, b, n)
                    pe.wait_ge(over.y_act, n + 1)
                    pe.wait_ge(over.y_dve, n + 1)

                more_passes(j, again)
                pe.nop().then_inc(pair_done, 1)

            gather_transposes(main, g_rows[:, 0, :], main.gathered[0], 1)
            run_pairs(pe, pair)

        @block.scalar
        def _(act):
            def norm_x(i):
                act.wait_ge(x_in, 16 * (i + 1))
                if i == 1:
                    act.wait_ge(x_tr, 2)
                elif i > 1:
                    act.wait_ge(aT_done, i - 1)
                act.activation(xn[:, :, :].rearrange("t k p -> t (k p)"), x_sb[:, :], ACT.Square,
                               accum_out=stats[:, 0:1]).then_inc(x_sq, 1)
                act.wait_ge(x_rstd, i + 1)
                act.activation(xn[:, :, :].rearrange("t k p -> t p k"), x_sb[:, :].rearrange("t (p k) -> t p k", k=KD),
                               ACT.Copy, scale=stats[:, 2:3]).then_inc(xn_done, 1)

            def heads_out(i, col, dst, tr, done):
                act.wait_ge(tr, i + 1)
                act.activation(dst[:, :, i * P:(i + 1) * P], ps[:, 7, :].rearrange("p (h t) -> p h t", h=H), ACT.Copy,
                               scale=g_nope[:, col:col + 1]).then_inc(done, 1)

            def round_weights(n):
                if n < 3:
                    act.wait_ge(w_in_in[n], 16)
                    src, dst = w_in_raw[n][:, :, :], w_in_hi[:, :, W_CUTS[n]:W_CUTS[n + 1]]
                else:
                    act.wait_ge(w_up_in, 32)
                    src, dst = w_uq_raw[:, :, :], w_uq_hi[:, :, :]
                act.activation(dst, src, ACT.Copy).then_inc(w_hi_done, 1)

            norm_x(0)
            round_weights(0)
            for i in range(NT):
                if i == 1:
                    act.wait_ge(gains_in, 16 * N_GAINS)
                if i + 1 < NT:
                    norm_x(i + 1)
                act.wait_ge(p1_done, i + 1)
                if i >= 1:
                    act.wait_ge(k_ss, i)
                    act.wait_ge(c_rstd, i)
                act.activation(junk[:, 0:RQ], ps[:, 2, 0:RQ], ACT.Square, accum_out=stats[:, 4:5]).then_inc(c_sq, 1)
                if i >= 1:
                    heads_out(i - 1, 0, qT, qn_tr, qT_done)
                if i == 0:
                    round_weights(1)
                act.wait_ge(p2_done, i + 1)
                act.wait_ge(c_sq, 3 * i + 1)
                act.activation(junk[:, 0:RKV], ps[:, 3, 0:RKV], ACT.Square, accum_out=stats[:, 5:6]).then_inc(c_sq, 1)
                act.wait_ge(c_sq, 3 * i + 2)
                if i >= 1:
                    act.wait_ge(k_ms, i)
                    act.wait_ge(kr_done, i)
                act.activation(junk[:, 0:DR], ps[:, 3, RKV:RKV + DR], ACT.Square, accum_out=stats[:, 6:7]).then_inc(c_sq, 1)
                act.activation(k_raw[:, :], ps[:, 3, RKV:RKV + DR], ACT.Copy).then_inc(k_raw_done, 1)
                if i == 1:
                    act.wait_ge(w_lo_done, 4)
                if i >= 1:
                    heads_out(i - 1, 1, kT, kn_tr, kT_done)
                act.wait_ge(c_rstd, i + 1)
                if i >= 1:
                    act.wait_ge(cT_done, i)
                    act.wait_ge(q_mm, i)
                act.activation(cn[:, 0:KQ, :].rearrange("t k p -> t p k"), ps[:, 2, 0:RQ].rearrange("t (p k) -> t p k", k=KQ),
                               ACT.Copy, scale=stats[:, 8:9]).then_inc(cn_done, 1)
                act.activation(cn[:, KQ:, :].rearrange("t k p -> t p k"), ps[:, 3, 0:RKV].rearrange("t (p k) -> t p k", k=KKV),
                               ACT.Copy, scale=stats[:, 9:10]).then_inc(cn_done, 1)
                if i == 0:
                    round_weights(2)
                    act.wait_ge(w_lo_done, 2)
                act.wait_ge(p3_done, i + 1)
                act.activation(u_sb[:, i, :], ps[:, 4, :], ACT.Copy).then_inc(u_done, 1)
                act.wait_ge(q_mm, i + 1)
                act.wait_ge(c_sq, 3 * i + 3)
                act.activation(junk[:, 0:H * DQK].rearrange("t (b c) -> t b c", b=2), ps[:, 2:4, 0:384], ACT.Square).then_inc(q_sq, 1)
                act.wait_ge(kv_mm, i + 1)
                act.wait_ge(q_ss, i + 1)
                kv = ps[:, 5:7, :].rearrange("t b (h w) -> t b h w", h=2)
                act.activation(junk[:, 0:H * DN].rearrange("t (b h w) -> t b h w", b=2, h=2), kv[:, :, :, 0:DN], ACT.Square).then_inc(k_sq, 1)
                if i == 0:
                    act.wait_ge(w_lo_done, 3)
                act.activation(v_sb[:, i, :].rearrange("t (b h w) -> t b h w", b=2, h=2), kv[:, :, :, DN:], ACT.Copy).then_inc(v_done, 1)
                if i == 0:
                    round_weights(3)
            heads_out(NT - 1, 0, qT, qn_tr, qT_done)
            heads_out(NT - 1, 1, kT, kn_tr, kT_done)

            act.wait_ge(r_tr, NT)
            act.wait_ge(rT_done, NT)
            for m, (s, hp, qt) in enumerate(units):
                n = SEQS[s]
                for u in range(2):
                    w = 2 * m + u
                    act.wait_ge(neg_max, w + 1)
                    if w >= 4:
                        act.wait_ge(p_tr, w - 3)
                    act.activation(p_sb[:, w % 4, 0:n], ps[:, 2 * (m % 2) + u, 0:n], ACT.Exp, bias=a_stat[:, w % 4, 1:2],
                                   scale=SCALE, accum_out=a_stat[:, w % 4, 2:3]).then_inc(exp_done, 1)
                if m >= 1:
                    pT_copy(act, m - 1, 0)
                if m - 1 in last_of_head:
                    o_copy(act, m - 1, 0)
            pT_copy(act, len(units) - 1, 0)
            o_copy(act, len(units) - 1, 0)

            for g in range(NG):
                act.wait_ge(d_mm, g + 1)
                if g >= 2:
                    act.wait_ge(mix_mm, g - 1)
                for s in range(2):
                    act.activation(dT[:, g % 2, FIRST[s] * P:FIRST[s] * P + SEQS[s]], ps[:, 2 * (g % 2) + s, 0:SEQS[s]],
                                   ACT.Copy).then_inc(dT_done, 1)

            def route_exps(i):
                act.wait_ge(neg_g, i + 1)
                if i >= 1:
                    act.wait_ge(gates_done, i)
                act.activation(route_f[:, 160:164], route_f[:, 128:132], ACT.Exp, bias=route_f[:, 176:177],
                               accum_out=route_f[:, 177:178]).then_inc(g_exp, 1)
                act.wait_ge(e_diff, i + 1)
                act.activation(route_f[:, 179:180], route_f[:, 178:179], ACT.Exp).then_inc(e_exp, 1)

            for i in range(NT):
                act.wait_ge(h_done, 2 * (i + 1))
                if i >= 1:
                    act.wait_ge(h_rstd, i)
                act.activation(h_junk[:, :], h_sb[:, i % 2, :], ACT.Square, accum_out=route_f[:, 400:401]).then_inc(h_sq, 1)
                if i >= 1:
                    route_exps(i - 1)
                act.wait_ge(a2_tr, i + 1)
                if i >= 1:
                    act.wait_ge(lg_mm, i)
                for half in range(2):
                    act.activation(a2T[:, 4 * half:4 * half + 4, :], ps[:, 4 + half, :].rearrange("p (k t) -> p k t", k=4),
                                   ACT.Copy).then_inc(a2T_done, 1)
            route_exps(NT - 1)

            act.wait_ge(counts_done, 1)

            def x_copy(q, n):
                act.wait_ge(q.x_tr, n + 1)
                bank = 0 if q is main else 6
                act.activation(xT[:, q.o, 0:4, :], ps[:, bank, :].rearrange("p (k t) -> p k t", k=4), ACT.Copy).then_inc(q.x_act, 1)

            def silu(q, n):
                act.wait_ge(q.gu_mm, n + 1)
                act.activation(s_act[:, q.o, :], ps[:, 2, 0:FH], ACT.Silu).then_inc(q.silu_done, 1)

            def y_copy(q, n, buf):
                act.wait_ge(q.y_mm, n + 1)
                y_free(act, q, n)
                act.activation(y_sb[:, buf, 0:512], ps[:, 4, :], ACT.Copy).then_inc(q.y_act, 1)

            more_passes = passes_counter(act)

            def pair(j, i, b, last):
                silu(main, j)
                if not last:
                    x_copy(main, j + 1)
                y_copy(main, j, b)

                def again(n, p):
                    x_copy(over, n)
                    silu(over, n)
                    y_copy(over, n, 3)

                more_passes(j, again)

            x_copy(main, 0)
            run_pairs(act, pair)

        @block.vector
        def _(dve):
            steps = {"rope": 0, "route": 0}

            def link(kind, signal, ins):
                steps[kind] += 1
                ins.then_inc(signal, 1)
                dve.wait_ge(signal, steps[kind])

            dve.wait_ge(consts_in, 16)
            dve.tensor_copy(ltri_bf, consts[:, C_LTRI:C_LTRI + P]).then_inc(bf_set, 1)
            dve.memset(ones_bf, 1.0).then_inc(bf_set, 1)
            dve.memset(m_sum[:, 0, :], 0.0).then_inc(bf_set, 1)
            def aT_copy(i):
                full = aT0 if i == 0 else xn
                for half in range(2):
                    dve.wait_ge(x_tr, 2 * i + (half if i == 0 else 1) + 1)
                    dve.tensor_tensor(full[:, 4 * half:4 * half + 4, :], ps[:, half, :].rearrange("p (k t) -> p k t", k=4),
                                      g_attn[:, 4 * half:4 * half + 4].unsqueeze(2).to_broadcast([P, 4, P]),
                                      ALU.mult).then_inc(aT_full, 1)
                if i >= 1:
                    dve.wait_ge(aT_full, 2 * (i + 1))
                    dve.wait_ge(p3_done, i)
                    dve.tensor_copy(aT_hi[:, :, :], xn[:, :, :]).then_inc(aT_hi_done, 1)
                    dve.wait_ge(aT_hi_done, i)
                    dve.tensor_tensor(aT_lo[:, :, :], xn[:, :, :], aT_hi[:, :, :].bitcast(F32), ALU.subtract).then_inc(aT_done, 1)

            def cT_copy(i):
                dve.wait_ge(c_tr, i + 1)
                dve.tensor_tensor(cn[:, 0:KQ, :], ps[:, 2, 0:RQ].rearrange("p (k t) -> p k t", k=KQ),
                                  g_lat[:, 0:KQ].unsqueeze(2).to_broadcast([P, KQ, P]), ALU.mult).then_inc(cT_full, 1)
                dve.wait_ge(cT_full, i + 1)
                if i >= 1:
                    dve.wait_ge(kv_mm, i)
                    dve.tensor_copy(cT_hi[:, :, :], cn[:, 0:KQ, :]).then_inc(cT_hi_done, 1)
                kv = dve.tensor_tensor(cT_kv[:, :, :], ps[:, 3, 0:RKV].rearrange("p (k t) -> p k t", k=KKV),
                                       g_lat[:, KQ:].unsqueeze(2).to_broadcast([P, KKV, P]), ALU.mult)
                if i >= 1:
                    dve.wait_ge(cT_hi_done, i)
                    dve.tensor_tensor(cT_lo[:, :, :], cn[:, 0:KQ, :], cT_hi[:, :, :].bitcast(F32), ALU.subtract).then_inc(cT_done, 1)
                else:
                    kv.then_inc(cT_done, 1)

            def split_weights(n):
                dve.wait_ge(w_hi_done, n + 1)
                if n < 3:
                    c = slice(W_CUTS[n], W_CUTS[n + 1])
                    raw, hi, lo = w_in_raw[n][:, :, :], w_in_hi[:, :, c], w_in_lo[:, :, c]
                else:
                    raw, hi, lo = w_uq_raw[:, :, :], w_uq_hi[:, :, :], w_uq_lo[:, :, :]
                dve.tensor_tensor(lo, raw, hi.bitcast(F32), ALU.subtract).then_inc(w_lo_done, 1)

            def rotate(x, o, n, pt, heads, done):
                half = DR // 2
                t = rope_t[:, :, 0:heads, :]
                cos = rope_tab[:, 2 * n, pt, :].unsqueeze(1).to_broadcast([P, heads, DR])
                lo = rope_tab[:, 2 * n + 1, pt, 0:half].unsqueeze(1).to_broadcast([P, heads, half])
                hi = rope_tab[:, 2 * n + 1, pt, half:DR].unsqueeze(1).to_broadcast([P, heads, half])
                dve.tensor_tensor(t[:, 0], x, cos, ALU.mult)
                dve.tensor_tensor(t[:, 1, :, 0:half], x[:, :, half:DR], lo, ALU.mult)
                link("rope", rope_step, dve.tensor_tensor(t[:, 1, :, half:DR], x[:, :, 0:half], hi, ALU.mult))
                return dve.tensor_tensor(o, t[:, 0], t[:, 1], ALU.add)

            dve.wait_ge(g_attn_in, 16)
            aT_copy(0)
            dve.wait_ge(gains_in, 16 * N_GAINS)
            for n in range(4):
                tab = consts[:, (C_COS, C_SIN)[n % 2]:(C_COS, C_SIN)[n % 2] + 4 * DR].rearrange("p (t r) -> p t r", t=4)
                dve.tensor_tensor(rope_tab[:, n, :, :], tab, g_rope[:, n, :].unsqueeze(1).to_broadcast([P, 4, DR]),
                                  ALU.mult).then_inc(tables_set, 1)
            dve.wait_ge(tables_set, 4)
            split_weights(0)
            for i in range(NT):
                pt = i - FIRST[0 if i < FIRST[1] else 1]
                if i == 0:
                    split_weights(1)
                cT_copy(i)
                if i + 1 < NT:
                    aT_copy(i + 1)
                if i == 0:
                    split_weights(2)
                if i >= 1:
                    dve.wait_ge(r_tr, i)
                    dve.tensor_copy(rT[:, :, (i - 1) * P:i * P], ps[:, 7, :].rearrange("p (n t) -> p n t", n=4)).then_inc(rT_done, 1)
                dve.wait_ge(q_sq, i + 1)
                if i >= 1:
                    dve.wait_ge(q_ms, i)
                dve.tensor_reduce(stats[:, 12:16], junk[:, 0:H * DQK].rearrange("t (h w) -> t h w", h=H), AX.X, ALU.add).then_inc(q_ss, 1)
                dve.wait_ge(q_rstd, i + 1)
                if i >= 1:
                    dve.wait_ge(qn_tr, i)
                    dve.wait_ge(qr_done, i)
                r = stats[:, 20:24].rearrange("t (b h) -> t b h", b=2).unsqueeze(3)
                q = ps[:, 2:4, 0:384].rearrange("t b (h w) -> t b h w", h=2)
                dve.tensor_tensor(q_x[:, :, :].rearrange("t (b h) w -> t b h w", b=2), q[:, :, :, DN:],
                                  r.to_broadcast([P, 2, 2, DR]), ALU.mult).then_inc(qx_done, 1)
                dve.tensor_tensor(q_n[:, :, :].rearrange("t (b h) w -> t b h w", b=2), q[:, :, :, 0:DN],
                                  r.to_broadcast([P, 2, 2, DN]), ALU.mult).then_inc(qn_done, 1)
                dve.wait_ge(k_sq, i + 1)
                if i >= 1:
                    dve.wait_ge(k_rstd, i)
                dve.tensor_reduce(stats[:, 28:32], junk[:, 0:H * DN].rearrange("t (h w) -> t h w", h=H), AX.X, ALU.add).then_inc(k_ss, 1)
                dve.wait_ge(qn_done, i + 1)
                rotate(q_x[:, :, :], q_r[:, :, :], 0, pt, H, qr_done).then_inc(qr_done, 1)
                dve.wait_ge(k_rstd, i + 1)
                dve.wait_ge(v_done, i + 1)
                if i >= 1:
                    dve.wait_ge(kn_tr, i)
                r = stats[:, 40:44]
                kv = ps[:, 5:7, :].rearrange("t b (h w) -> t b h w", h=2)
                dve.tensor_tensor(k_n[:, :, :].rearrange("t (b h) w -> t b h w", b=2), kv[:, :, :, 0:DN],
                                  r.rearrange("t (b h) -> t b h", b=2).unsqueeze(3).to_broadcast([P, 2, 2, DN]),
                                  ALU.mult).then_inc(kn_done, 1)
                dve.wait_ge(qr_done, i + 1)
                dve.wait_ge(k_raw_done, i + 1)
                link("rope", rope_step, rotate(k_raw[:, :].unsqueeze(1), rope_k[:, :].unsqueeze(1), 1, pt, 1, None))
                dve.tensor_tensor(k_r[:, :, :], rope_k[:, :].unsqueeze(1).to_broadcast([P, H, DR]),
                                  r.unsqueeze(2).to_broadcast([P, H, DR]), ALU.mult).then_inc(kr_done, 1)
                if i == 0:
                    split_weights(3)
            dve.wait_ge(r_tr, NT)
            dve.tensor_copy(rT[:, :, (NT - 1) * P:], ps[:, 7, :].rearrange("p (n t) -> p n t", n=4)).then_inc(rT_done, 1)

            dve.wait_ge(kr_done, NT)
            for m, (s, hp, qt) in enumerate(units):
                n = SEQS[s]
                for u in range(2):
                    w = 2 * m + u
                    st = a_stat[:, w % 4]
                    dve.wait_ge(s_ready, w + 1)
                    if w >= 4:
                        dve.wait_ge(exp_done, w - 3)
                        dve.wait_ge(p_done, w - 3)
                    dve.reduce_max(st[:, 0:1], ps[:, 2 * (m % 2) + u, 0:n], AX.X).then_inc(row_max, 1)
                    dve.wait_ge(row_max, w + 1)
                    dve.tensor_scalar(st[:, 1:2], st[:, 0:1], -SCALE, None, ALU.mult).then_inc(neg_max, 1)
                if m >= 1:
                    pT_copy(dve, m - 1, 1)
                for u in range(2):
                    w = 2 * m + u
                    st = a_stat[:, w % 4]
                    dve.wait_ge(exp_done, w + 1)
                    dve.reciprocal(st[:, 3:4], st[:, 2:3]).then_inc(recip_done, 1)
                    dve.wait_ge(recip_done, w + 1)
                    dve.tensor_scalar(p_sb[:, w % 4, 0:n], p_sb[:, w % 4, 0:n], st[:, 3:4], None, ALU.mult).then_inc(p_done, 1)
                if m - 1 in last_of_head:
                    o_copy(dve, m - 1, 1)
            pT_copy(dve, len(units) - 1, 1)
            o_copy(dve, len(units) - 1, 1)

            for g in range(NG):
                dve.wait_ge(mix_mm, g + 1)
                for s in range(2):
                    dve.tensor_scalar(kT[:, g, FIRST[s] * P:FIRST[s] * P + SEQS[s]], ps[:, 4 + 2 * (g % 2) + s, 0:SEQS[s]],
                                      g_pool[:, g:g + 1], None, ALU.mult).then_inc(mix_done, 1)

            RF = route_f
            dve.wait_ge(d_mm, NG)
            dve.memset(RF[:, 128:136], -3e38).then_inc(bf_set, 1)
            dve.wait_ge(g_ffn_in, 48)

            def residual(i):
                dve.wait_ge(x_res_in, 16 * (i + 1))
                if i >= 2:
                    dve.wait_ge(h_stored, 16 * (i - 1))
                    dve.wait_ge(a2_done, i - 1)
                    dve.wait_ge(h_sq, i - 1)
                for n in range(2):
                    dve.wait_ge(o_mm, 2 * i + n + 1)
                    dve.tensor_tensor(h_sb[:, i % 2, n * 512:(n + 1) * 512], ps[:, 2 * (i % 2) + n, :], x_res[:, n * 512:(n + 1) * 512],
                                      ALU.add).then_inc(h_done, 1)

            def second_norm(i):
                dve.wait_ge(h_rstd, i + 1)
                if i >= 2:
                    dve.wait_ge(rows_stored, 16 * (i - 1))
                    dve.wait_ge(a2_tr, i - 1)
                dve.scalar_tensor_tensor(out=rows[:, i % 2, 0:D].rearrange("t (k p) -> t p k", k=KD),
                                         in0=h_sb[:, i % 2, :].rearrange("t (p k) -> t p k", k=KD), scalar=route_f[:, 402:403],
                                         in1=g_ffn[:, :].rearrange("t (p k) -> t p k", k=KD), op0=ALU.mult, op1=ALU.mult).then_inc(a2_done, 1)

            def route(i):
                def step(ins):
                    link("route", route_step, ins)

                dve.wait_ge(lg_mm, i + 1)
                if i >= 1:
                    dve.wait_ge(g_exp, i)
                if i == 0:
                    dve.wait_ge(bf_set, 4)
                step(dve.tensor_tensor(RF[:, 128:128 + EG], ps[:, 7, 0:EG], r_bias[:, 0:EG], ALU.add))
                dve.tensor_tensor(RF[:, 0:E], ps[:, 7, EG:EG + E], r_bias[:, EG:], ALU.add).then_inc(lg_bias, 1)
                step(dve.max(RF[:, 136:144], RF[:, 128:136]))
                dve.tensor_scalar(RF[:, 176:177], RF[:, 136:137], -1.0, None, ALU.mult).then_inc(neg_g, 1)
                step(dve.max_index(route_u[:, 0:8], RF[:, 136:144], RF[:, 128:136]))
                dve.wait_ge(lg_bias, i + 1)
                step(dve.tensor_copy(RF[:, 180:181], route_u[:, 0:1]))
                step(dve.tensor_scalar(RF[:, 168:172], iota[:, 0:EG], RF[:, 180:181], -BIG, ALU.not_equal, ALU.mult))
                step(dve.tensor_tensor(RF[:, 192:192 + E].rearrange("t (g e) -> t g e", g=EG),
                                       RF[:, 0:E].rearrange("t (g e) -> t g e", g=EG),
                                       RF[:, 168:172].unsqueeze(2).to_broadcast([P, EG, EPG]), ALU.add))
                step(dve.max(RF[:, 144:152], RF[:, 192:192 + E]))
                dve.tensor_tensor(RF[:, 178:179], RF[:, 145:146], RF[:, 144:145], ALU.subtract).then_inc(e_diff, 1)
                step(dve.max_index(route_u[:, 8:16], RF[:, 144:152], RF[:, 192:192 + E]))
                step(dve.tensor_copy(RF[:, 182:184], route_u[:, 8:10]))
                if i >= 1:
                    dve.wait_ge(rank_mm, i)
                    dve.wait_ge(pos_done, i)
                dve.tensor_scalar(RF[:, 224:224 + E], iota, RF[:, 182:183], None, ALU.is_equal)
                step(dve.tensor_scalar(RF[:, 256:256 + E], iota, RF[:, 183:184], None, ALU.is_equal))
                dve.tensor_tensor(m_sum[:, 1, :], RF[:, 224:224 + E], RF[:, 256:256 + E], ALU.add).then_inc(mask_done, 1)
                dve.wait_ge(e_exp, i + 1)
                dve.wait_ge(g_exp, i + 1)
                step(dve.tensor_scalar(RF[:, 184:185], RF[:, 179:180], 1.0, RF[:, 177:178], ALU.add, ALU.mult))
                step(dve.reciprocal(RF[:, 185:186], RF[:, 184:185]))
                step(dve.tensor_tensor(RF[:, 186:187], RF[:, 185:186], RF[:, 179:180], ALU.mult))
                step(dve.tensor_scalar(RF[:, 288:288 + E], RF[:, 256:256 + E], RF[:, 186:187], None, ALU.mult))
                dve.scalar_tensor_tensor(out=rows[:, i % 2, D:ROW], in0=RF[:, 224:224 + E], scalar=RF[:, 185:186],
                                         in1=RF[:, 288:288 + E], op0=ALU.mult, op1=ALU.add).then_inc(gates_done, 1)

            def positions(i):
                def step(ins):
                    link("route", route_step, ins)

                dve.wait_ge(rank_mm, i + 1)
                dve.wait_ge(mask_done, i + 1)
                step(dve.tensor_copy(RF[:, 320:320 + E], ps[:, 6, 128:128 + E]))
                for c in range(2):
                    oh = RF[:, 224 + E * c:224 + E * c + E]
                    step(dve.tensor_tensor_reduce(out=RF[:, 352:352 + E], in0=oh, in1=RF[:, 320:320 + E], scale=1.0, scalar=0.0,
                                                  op0=ALU.mult, op1=ALU.add, accum_out=RF[:, 384 + c:385 + c]))
                    step(dve.tensor_tensor_reduce(out=RF[:, 352:352 + E], in0=oh, in1=ebase, scale=1.0, scalar=0.0,
                                                  op0=ALU.mult, op1=ALU.add, accum_out=RF[:, 386 + c:387 + c]))
                ri = route_u[:, 16:18].bitcast(I32)
                rs = route_u[:, 18:20].bitcast(I32)
                step(dve.tensor_copy(ri, RF[:, 384:386]))
                step(dve.tensor_scalar(rs, ri, 6, None, ALU.arith_shift_right))
                step(dve.tensor_copy(RF[:, 388:390], rs))
                step(dve.scalar_tensor_tensor(out=RF[:, 386:388], in0=RF[:, 384:386], scalar=float(PAIRS), in1=RF[:, 386:388],
                                              op0=ALU.mult, op1=ALU.add))
                step(dve.scalar_tensor_tensor(out=RF[:, 390:392], in0=RF[:, 388:390], scalar=float(BLOCK - LANE * PAIRS),
                                              in1=RF[:, 386:388], op0=ALU.mult, op1=ALU.add))
                step(dve.tensor_copy(idx_pos[:, i, :], RF[:, 390:392]))
                dve.tensor_tensor(m_sum[:, 0, :], m_sum[:, 0, :], m_sum[:, 1, :], ALU.add).then_inc(pos_done, 1)

            for i in range(NT):
                residual(i)
                if i >= 2:
                    positions(i - 2)
                second_norm(i)
                if i >= 1:
                    route(i - 1)
            positions(NT - 2)
            route(NT - 1)
            positions(NT - 1)

            dve.wait_ge(total_mm, 1)
            c = RF[0:1, 224:224 + E]
            link("route", route_step, dve.tensor_copy(c, ps[0:1, 7, 0:E]))
            cp = c.rearrange("t (l j) -> t l j", l=2)
            link("route", route_step, dve.tensor_tensor(RF[0:1, 256:256 + PAIRS], cp[:, 0, :], cp[:, 1, :], ALU.max))
            link("route", route_step, dve.tensor_scalar(RF[0:1, 288:288 + PAIRS], RF[0:1, 256:256 + PAIRS], -1.0, 0.0, ALU.add, ALU.max))
            link("route", route_step, dve.tensor_copy(counts_i[0:1, 0, :], RF[0:1, 288:288 + PAIRS]))
            dve.tensor_scalar(counts_i[0:1, 3, :], counts_i[0:1, 0, :], 6, None, ALU.arith_shift_right).then_inc(counts_done, 1)

            dve.wait_ge(counts_done, 1)

            def x_copy(q, n):
                dve.wait_ge(q.x_tr, n + 1)
                bank = 1 if q is main else 7
                dve.tensor_copy(xT[:, q.o, 4:8, :], ps[:, bank, :].rearrange("p (k t) -> p k t", k=4)).then_inc(q.x_dve, 1)

            def gates(q, src, j, n, g):
                for lane in range(2):
                    r = slice(lane * LANE, (lane + 1) * LANE)
                    dve.tensor_copy(gate[r, g:g + 1], src[r, bass.ds(j + D + PAIRS * lane, 1)]).then_inc(q.gate_done, 1)

            def hidden(q, n, g):
                dve.wait_ge(q.silu_done, n + 1)
                dve.wait_ge(q.gate_done, 2 * (n + 1))
                dve.scalar_tensor_tensor(out=hid[:, q.o, :, :].rearrange("t k p -> t p k"),
                                         in0=s_act[:, q.o, :].rearrange("t (p k) -> t p k", k=2), scalar=gate[:, g:g + 1],
                                         in1=ps[:, 2, FH:2 * FH].rearrange("t (p k) -> t p k", k=2),
                                         op0=ALU.mult, op1=ALU.mult).then_inc(q.hid_done, 1)

            def hT_copy(q, n):
                dve.wait_ge(q.h_tr, n + 1)
                dve.tensor_copy(hT[:, q.o, :, :], ps[:, 3, 0:FH].rearrange("p (k t) -> p k t", k=2)).then_inc(q.hT_done, 1)

            def y_copy(q, n, buf):
                dve.wait_ge(q.y_mm, n + 1)
                y_free(dve, q, n)
                dve.tensor_copy(y_sb[:, buf, 512:1024], ps[:, 5, :]).then_inc(q.y_dve, 1)

            more_passes = passes_counter(dve)

            def pair(j, i, b, last):
                hidden(main, j, b)
                if not last:
                    nb = (b + 1) % 3
                    dve.wait_ge(main.gathered[nb], 16 * (i + 1 if b < 2 else i + 2))
                    gates(main, g_rows[:, nb, :], j + 1, j + 1, nb)
                    x_copy(main, j + 1)
                hT_copy(main, j)
                y_copy(main, j, b)

                def again(n, p):
                    dve.wait_ge(over.gathered[0], 16 * (n + 1))
                    gates(over, more_rows[:, :], j, n, 3)
                    x_copy(over, n)
                    hidden(over, n, 3)
                    hT_copy(over, n)
                    y_copy(over, n, 3)

                more_passes(j, again)

            dve.wait_ge(main.gathered[0], 16)
            gates(main, g_rows[:, 0, :], 0, 0, 0)
            x_copy(main, 0)
            run_pairs(dve, pair)

        @block.gpsimd
        def _(pool):
            pool.memset(neg_half[:, :], -0.5).then_inc(neg_half_set, 1)
            pool.wait_ge(neg_half_set, 1)

            S = stats

            def x_part(i):
                pool.wait_ge(x_sq, i + 1)
                pool.tensor_scalar(S[:, 1:2], S[:, 0:1], 1.0 / D, EPS, ALU.mult, ALU.add).then_inc(x_ms, 1)
                pool.wait_ge(x_ms, i + 1)
                if i >= 1:
                    pool.wait_ge(xn_done, i)
                pool.tensor_tensor(S[:, 2:3], S[:, 1:2], neg_half[:, 0:1], ALU.pow).then_inc(x_rstd, 1)

            x_part(0)
            for i in range(NT):
                if i + 1 < NT:
                    x_part(i + 1)
                pool.wait_ge(c_sq, 3 * (i + 1))
                pool.tensor_scalar(S[:, 10:11], S[:, 4:5], 1.0 / RQ, EPS, ALU.mult, ALU.add).then_inc(c_ms, 1)
                pool.tensor_scalar(S[:, 11:12], S[:, 5:6], 1.0 / RKV, EPS, ALU.mult, ALU.add).then_inc(c_ms, 1)
                pool.wait_ge(c_ms, 2 * (i + 1))
                if i >= 1:
                    pool.wait_ge(cn_done, 2 * i)
                pool.tensor_tensor(S[:, 8:10], S[:, 10:12], neg_half[:, 0:2], ALU.pow).then_inc(c_rstd, 1)
                pool.wait_ge(q_ss, i + 1)
                pool.tensor_scalar(S[:, 16:20], S[:, 12:16], 1.0 / DQK, EPS, ALU.mult, ALU.add).then_inc(q_ms, 1)
                pool.wait_ge(q_ms, i + 1)
                if i >= 1:
                    pool.wait_ge(qn_done, i)
                pool.tensor_tensor(S[:, 20:24], S[:, 16:20], neg_half[:, 0:4], ALU.pow).then_inc(q_rstd, 1)
                pool.wait_ge(k_ss, i + 1)
                pool.tensor_scalar(S[:, 32:36], S[:, 28:32], S[:, 6:7], 1.0 / DQK, ALU.add, ALU.mult).then_inc(k_ms, 1)
                pool.wait_ge(k_ms, i + 1)
                pool.tensor_scalar(S[:, 36:40], S[:, 32:36], EPS, None, ALU.add).then_inc(k_eps, 1)
                pool.wait_ge(k_eps, i + 1)
                if i >= 1:
                    pool.wait_ge(kr_done, i)
                pool.tensor_tensor(S[:, 40:44], S[:, 36:40], neg_half[:, 0:4], ALU.pow).then_inc(k_rstd, 1)

            pool.wait_ge(setup_dram, 48)

            def fill_slots(i):
                pool.wait_ge(pos_done, i + 1)
                for c in range(2):
                    pool.indirect_dma_start(
                        out=slot_table, out_offset=bass.IndirectOffsetOnAxis(ap=idx_pos[:, i, c:c + 1], axis=0),
                        in_=tok_ids[:, i:i + 1], in_offset=None).then_inc(slots_stored, 16)

            for i in range(NT):
                pool.wait_ge(h_sq, i + 1)
                pool.tensor_scalar(route_f[:, 401:402], route_f[:, 400:401], 1.0 / D, EPS, ALU.mult, ALU.add).then_inc(h_ms, 1)
                pool.wait_ge(h_ms, i + 1)
                if i >= 1:
                    pool.wait_ge(a2_done, i)
                pool.tensor_tensor(route_f[:, 402:403], route_f[:, 401:402], neg_half[:, 0:1], ALU.pow).then_inc(h_rstd, 1)
                if i >= 2:
                    fill_slots(i - 2)
            fill_slots(NT - 2)
            fill_slots(NT - 1)

            pool.wait_ge(idx_in, 48)
            pool.wait_ge(rows_stored, 16 * NT)
            pool.wait_ge(h_stored, 16 * NT)
            pool.wait_ge(counts_done, 1)

            def gather(dst, idx, done):
                pool.indirect_dma_start(out=dst, out_offset=None, in_=table,
                                        in_offset=bass.IndirectOffsetOnAxis(ap=idx, axis=0)).then_inc(done, 16)

            def ready(*waits):
                for signal, value in waits:
                    pool.wait_ge(signal, value)
                pool.sem_inc(dma_go, 1)

            def set_idx(col, j):
                pool.tensor_copy(idx_now[:, col:col + 1], idx_all[:, bass.ds(j, 1)]).then_inc(idx_set, 1)

            def gather_pair(j, b, count):
                set_idx(b, j)
                ready((idx_set, count))
                gather(g_rows[:, b, :], idx_now[:, b:b + 1], main.gathered[b])

            def add_rows(q, n, buf, idx):
                pool.indirect_dma_start(out=out, out_offset=bass.IndirectOffsetOnAxis(ap=idx, axis=0),
                                        in_=y_sb[:, buf, :], in_offset=None, compute_op=ALU.add).then_inc(q.added, 16)

            def more_gather(j, p):
                src = slot_table.rearrange("(a s j) c -> a s (j c)", s=2 * LANE, j=PAIRS)
                with nc.allow_non_contiguous_dma(reason="128 indices"):
                    pool.dma_start(idx_now[:, 6:7], src[bass.ds(p, 1), :, bass.ds(j, 1)].rearrange("a s c -> (a s) c")).then_inc(over_idx_in, 16)
                m = pool.snap(loaded)
                ready((over_idx_in, 16 * (m + 1)))
                pool.reg_add(loaded, loaded, 1)
                gather(more_rows[:, :], idx_now[:, 6:7], over.gathered[0])

            def first_more_gather(j):
                todo = pool.value_load(counts_i[0:1, 3, bass.ds(j, 1)], min_val=0, max_val=PASSES - 1)
                with pool.If(todo > 0):
                    pool.tensor_copy(idx_now[:, 6:7], idx_more[:, bass.ds(j, 1)]).then_inc(more_set, 1)
                    m = pool.snap(firsts)
                    ready((more_set, m + 1))
                    pool.reg_add(firsts, firsts, 1)
                    gather(more_rows[:, :], idx_now[:, 6:7], over.gathered[0])

            def more_add(j, n):
                ready((over.y_act, n + 1), (over.y_dve, n + 1), (main.added, 16 * (j + 1)))
                add_rows(over, n, 3, idx_now[:, 6:7])
                pool.wait_ge(over.added, 16 * (n + 1))

            before, loaded, firsts = (pool.alloc_register(n) for n in ("more_before", "more_loaded", "more_firsts"))
            for r in (before, loaded, firsts):
                pool.reg_mov(r, 0)

            def pair(j, i, b, last):
                if not last:
                    if not (isinstance(j, int) and j == 0):
                        pool.wait_ge(main.x_tr, j)
                        pool.wait_ge(main.gate_done, 2 * j)
                    gather_pair(j + 2, (b + 2) % 3, 2 * j + 3)
                set_idx(3 + b, j)
                waits = [(idx_set, add_count(j)), (main.y_act, j + 1), (main.y_dve, j + 1)]
                if not (isinstance(j, int) and j == 0):
                    waits.append((main.added, 16 * j))
                ready(*waits)
                add_rows(main, j, b, idx_now[:, 3 + b:4 + b])

                todo = pool.value_load(counts_i[0:1, 3, bass.ds(j, 1)], min_val=0, max_val=PASSES - 1)
                with pool.If(todo > 0):
                    with pool.If(todo > 1):
                        with pool.Fori(1, todo) as p:
                            n = pool.snap(before)
                            more_add(j, n)
                            more_gather(j, p + 1)
                            pool.reg_add(before, before, 1)
                    more_add(j, pool.snap(before))
                    pool.reg_add(before, before, 1)
                if not last:
                    first_more_gather(j + 1)

            def add_count(j):
                return 2 * PAIRS + 1 if isinstance(j, int) and j == PAIRS - 1 else 2 * j + 4

            gather_pair(0, 0, 1)
            first_more_gather(0)
            gather_pair(1, 1, 2)
            run_pairs(pool, pair)
            pool.wait_ge(main.added, 16 * PAIRS)
            pool.wait_ge(main.gathered[PAIRS % 3], 16 * (PAIRS // 3 + 1))


_INS = ["x_prompt", "x_sample", "g_attn_norm", "w_in", "g_q_lat", "g_kv_lat", "w_uq", "w_ukv", "g_q_head", "g_k_head",
        "w_pool", "pool_scale", "w_out", "g_ffn_norm", "w_group_router", "b_group_router", "w_expert_router",
        "b_expert_router", "w_gate", "w_up", "w_down"]


def kernel(**inputs):
    import concourse.bacc as _bacc
    from concourse.bass_utils import run_bass_kernel_spmd as _run

    nc = _bacc.Bacc("TRN2", target_bir_lowering=False, num_devices=1)
    arrays, args = {}, {}
    named = {name: inputs[name] for name in _INS}
    named.update(host_constants())
    for name, x in named.items():
        x = np.ascontiguousarray(x)
        arrays[f"in_{name}"] = x
        args[name] = nc.dram_tensor(f"in_{name}", x.shape, mybir.dt.from_np(x.dtype), kind="ExternalInput").ap()
    out = nc.dram_tensor("out", [T + P, D], F32, kind="ExternalOutput").ap()
    build(nc, args, out)
    r = _run(nc, [arrays], core_ids=[0])
    y = np.asarray(r.results[0]["out"])
    return y[0:SEQS[0]].reshape(1, SEQS[0], D), y[SEQS[0]:T].reshape(1, SEQS[1], D)
```

```python
from contextlib import ExitStack

import numpy as np

import concourse.bass as bass
from concourse import mybir
from concourse.alu_op_type import AluOpType as ALU

F32 = mybir.dt.float32
F32R = mybir.dt.float32r
BF16 = mybir.dt.bfloat16
I32 = mybir.dt.int32
U32 = mybir.dt.uint32
ACT = mybir.ActivationFunctionType
AX = mybir.AxisListType

P = 128
D = 1024
KD = D // P
SEQS = (512, 256)
T = sum(SEQS)
NT = T // P
FIRST = (0, SEQS[0] // P)
TILES = tuple(s // P for s in SEQS)
H = 4
DN, DR, DV = 128, 64, 128
DQK = DN + DR
RQ, RKV = 384, 256
KQ, KKV = RQ // P, RKV // P
NU = 512
NG, GC = 4, 128
IN_W = RQ + RKV + DR + NU
WINDOWS = (2, 4, 8, 16)
HALO = max(WINDOWS) // 2
BANDW = P + 2 * HALO
EG, EPG = 4, 8
E = EG * EPG
FH = 256
LANE = 64
PAIRS = E // 2
PASSES = T // LANE
BLOCK = 2 * LANE * PAIRS
ROW = D + E
EPS = 1e-6
SCALE = float(DQK) ** -0.5
BIG = 1e30

C_ID, C_LTRI, C_COS, C_SIN = 0, P, 2 * P, 2 * P + 4 * DR
C_IOTA = C_SIN + 4 * DR
C_EBASE = C_IOTA + E
C_W = C_EBASE + E


def host_constants():
    c = np.zeros((P, C_W), np.float32)
    c[:, C_ID:C_ID + P] = np.eye(P)
    c[:, C_LTRI:C_LTRI + P] = np.triu(np.ones((P, P)), 1)
    inv = (1.0 / (np.float32(10000.0) ** (np.arange(0, DR, 2, dtype=np.float32) / np.float32(DR)))).astype(np.float32)
    pos = np.arange(max(SEQS), dtype=np.float32)
    ang = (pos[:, None] * inv[None, :]).astype(np.float32)
    cos = np.concatenate([np.cos(ang)] * 2, -1).reshape(-1, P, DR)
    sin = np.concatenate([-np.sin(ang), np.sin(ang)], -1).reshape(-1, P, DR)
    c[:, C_COS:C_COS + 4 * DR] = cos.transpose(1, 0, 2).reshape(P, -1)
    c[:, C_SIN:C_SIN + 4 * DR] = sin.transpose(1, 0, 2).reshape(P, -1)
    e = np.arange(E)
    c[:, C_IOTA:C_IOTA + E] = e
    c[:, C_EBASE:C_EBASE + E] = (e // PAIRS) * (LANE * PAIRS) + e % PAIRS
    band = np.zeros((P, NG, 3, BANDW), np.float32)
    s = 3 * P
    for g, w in enumerate(WINDOWS):
        full = np.zeros((s, s), np.float64)
        for t in range(s):
            lo, hi = max(t - w // 2, 0), min(t + w - w // 2, s)
            full[lo:hi, t] = 1.0 / (hi - lo)
            full[t, t] -= 1.0
        for kind in range(3):
            for col in range(BANDW):
                t = kind * P - HALO + col
                if 0 <= t < s:
                    band[:, g, kind, col] = full[kind * P:(kind + 1) * P, t]
    tokens = (np.arange(P)[:, None] + P * np.arange(NT)[None, :]).astype(np.int32)
    slots = np.broadcast_to((T + np.arange(2 * LANE))[None, :, None], (PASSES, 2 * LANE, PAIRS))
    slots = np.ascontiguousarray(slots.reshape(-1, 1).astype(np.int32))
    zeros = np.zeros((P, ROW), np.float32)
    return {"consts": c, "band": band.reshape(P, -1), "tokens": tokens, "slots": slots, "zeros": zeros}


def build(nc, a, out):
    table = nc.dram_tensor("token_rows", [T + P, ROW], F32, kind="Internal").ap()
    slot_table = nc.dram_tensor("slot_tokens", [PASSES * BLOCK, 1], I32, kind="Internal").ap()

    ctx = ExitStack()
    with ctx:
        def sem(name):
            return ctx.enter_context(nc.semaphore(name))

        def region(size, *groups):
            got = []
            for group in groups:
                with ExitStack() as one:
                    used = 0
                    for name, shape, dt in group:
                        got.append(one.enter_context(nc.sbuf_tensor(name, shape, dt)))
                        used += (int(np.prod(shape[1:])) * (2 if dt == BF16 else 4) + 31) // 32 * 32
                    assert used <= size, (group[0][0], used, size)
            hold = group[0][0] + "_region"
            ctx.enter_context(nc.sbuf_tensor(hold, [P, size // 4], F32))
            return got

        (consts, bf_consts, g_attn, g_lat, g_nope, g_pool, tok_ids, neg_half, idx_pos, counts_i,
         m_sum, w_router) = region(
            6 * 1024,
            [("consts_sb", [P, C_W], F32), ("bf_consts", [P, 2, P], BF16), ("g_attn", [P, KD], F32),
             ("g_lat", [P, KQ + KKV], F32), ("g_nope", [P, 2], F32), ("g_pool", [P, NG], F32),
             ("tok_ids", [P, NT], I32), ("neg_half", [P, 8], F32),
             ("idx_pos", [P, NT, 2], I32), ("counts_i", [1, 4, PAIRS], I32), ("m_sum", [P, 2, E], BF16),
             ("w_router", [P, KD, EG + E], F32)])
        ATT_FLOATS = 12 * 512 + 2 * T + NG * 3 * BANDW + NG * GC + 16
        W_BYTES = 2 * (2 * KD * FH + 2 * D) * 4
        (w1, w_in_lo, w_uq_lo, q_x, w_out_lo, o_lo, w_out_raw0) = region(
            W_BYTES,
            [("expert_w1", [P, 2, 3, 2 * D], F32)],
            [("w_in_lo", [P, KD, IN_W], F32R), ("w_uq_lo", [P, KQ, H * DQK], F32R), ("q_x", [P, H, DR], F32)],
            [("w_out_lo", [P, KD, D], F32R), ("o_lo", [P, H, T], F32R), ("w_out_raw0", [P, D], F32)])
        (qT, kT, w_in_hi, w_in_raw0, w_uq_raw, o_hi, pool_hi, w_out_hi, pool_lo0, w2, xT, s_act, hid, hT) = region(
            2 * H * T * 4 + KD * IN_W * 4,
            [("qT", [P, H, T], F32), ("kT", [P, H, T], F32), ("w_in_hi", [P, KD, IN_W], F32R)],
            [("w_in_raw0", [P, KD, RQ], F32), ("w_uq_raw", [P, KQ, H * DQK], F32)],
            [("o_hi", [P, H, T], F32R), ("pool_hi", [P, NG, T], F32R), ("w_out_hi", [P, KD, D], F32R),
             ("pool_lo0", [P, 2, T], F32R)],
            [("expert_w2", [P, 2, 3, 2 * D], F32), ("xT", [P, 2, KD, P], F32), ("s_act", [P, 2, FH], F32),
             ("hid", [P, 2, 2, P], F32), ("hT", [P, 2, 2, P], F32)])
        (rT, v_sb, u_sb, w_in_raw2, aT0, _, w_in_raw1, x_res, h_sb, rows, a2T, g_ffn, route_f, route_u, route_i, h_junk, r_bias,
         g_rows, more_rows, y_sb, idx_all, idx_more, idx_now, gate) = region(
            3 * H * T * 4,
            [("rT", [P, 4, T], F32), ("v_sb", [P, NT, H * DV], F32), ("u_sb", [P, NT, NU], F32)],
            [("w_in_raw2", [P, KD, NU], F32), ("aT0", [P, KD, P], F32), ("under_raw1", [P, D], F32),
             ("w_in_raw1", [P, KD, RKV + DR], F32)],
            [("x_res", [P, D], F32), ("h_sb", [P, 2, D], F32), ("rows", [P, 2, ROW], F32),
             ("a2T", [P, KD, P], F32), ("g_ffn", [P, D], F32), ("route_f", [P, 420], F32),
             ("route_u", [P, 24], U32), ("route_i", [P, 2, E], I32), ("h_junk", [P, D], F32), ("r_bias", [P, EG + E], F32)],
            [("g_rows", [P, 3, ROW], F32), ("more_rows", [P, ROW], F32), ("y_sb", [P, 4, D], F32),
             ("idx_all", [P, PAIRS + 1], I32), ("idx_more", [P, PAIRS], I32), ("idx_now", [P, 7], I32), ("gate", [P, 4], F32)])
        (w_uq_hi, w_ukv, x_sb, xn, aT_hi, aT_lo, cn, cT_hi, cT_lo, cT_kv, junk, q_n, q_r, k_n, k_raw, k_r, rope_t, rope_k, rope_tab, stats,
         p_sb, pT, dT, band, w_pool, a_stat, w_out_raw1, w_out_raw2, _, pool_lo2, w0) = region(
            56512,
            [("w_uq_hi", [P, KQ, H * DQK], F32R), ("w_ukv_sb", [P, KKV, H * (DN + DV)], F32),
             ("x_sb", [P, D], F32), ("xn", [P, KD, P], F32), ("aT_hi", [P, KD, P], F32R),
             ("aT_lo", [P, KD, P], F32R), ("cn", [P, KQ + KKV, P], F32), ("cT_hi", [P, KQ, P], F32R),
             ("cT_lo", [P, KQ, P], F32R), ("cT_kv", [P, KKV, P], F32), ("junk", [P, H * DQK], F32),
             ("q_n", [P, H, DN], F32), ("q_r", [P, H, DR], F32),
             ("k_n", [P, H, DN], F32), ("k_raw", [P, DR], F32), ("k_r", [P, H, DR], F32),
             ("rope_t", [P, 2, H, DR], F32), ("rope_k", [P, DR], F32), ("rope_tab", [P, 4, 4, DR], F32),
             ("stats", [P, 48], F32)],
            [("p_sb", [P, 4, 512], F32), ("pT", [P, 2, 4, 512], F32), ("dT", [P, 2, T], F32),
             ("band_sb", [P, NG, 3, BANDW], F32), ("w_pool_sb", [P, NG, GC], F32), ("a_stat", [P, 4, 4], F32),
             ("w_out_raw1", [P, D], F32), ("w_out_raw2", [P, D], F32),
             ("under_pool_lo", [P, W_BYTES // 4 - ATT_FLOATS - 2 * D], F32), ("pool_lo2", [P, 2, T], F32R)],
            [("expert_w0", [P, 2, 3, 2 * D], F32)])
        w_out_raw = (w_out_raw0, w_out_raw1, w_out_raw2)
        pool_lo = (pool_lo0, pool_lo2)
        weights = (w0, w1, w2)
        w_in_raw = (w_in_raw0, w_in_raw1, w_in_raw2)
        W_CUTS = (0, RQ, RQ + RKV + DR, IN_W)
        g_rope = q_x

        ps = ctx.enter_context(nc.psum_tensor("ps", [P, 8, 512], F32))

        ident = consts[:, C_ID:C_ID + P]
        iota = consts[:, C_IOTA:C_IOTA + E]
        ebase = consts[:, C_EBASE:C_EBASE + E]
        ones_bf, ltri_bf = bf_consts[:, 0, :], bf_consts[:, 1, :]

        consts_in, g_attn_in, gains_in, setup_dram = (sem(n) for n in ("consts_in", "g_attn_in", "gains_in", "setup_dram"))
        x_in = sem("x_in")
        w_in_in = [sem(f"w_in_in{n}") for n in range(3)]
        w_up_in, pool_in = sem("w_up_in"), sem("pool_in")
        w_out_in = [sem(f"w_out_in{b}") for b in range(3)]
        w_out_hi_done, w_out_lo_done = sem("w_out_hi_done"), sem("w_out_lo_done")
        x_res_in, g_ffn_in = sem("x_res_in"), sem("g_ffn_in")
        part_in = [sem(f"weights_part{n}_in") for n in range(6)]
        neg_half_set, tables_set, bf_set = sem("neg_half_set"), sem("tables_set"), sem("bf_set")
        x_sq, x_ms, x_rstd, xn_done = sem("x_sq"), sem("x_ms"), sem("x_rstd"), sem("xn_done")
        x_tr, aT_full, aT_hi_done, aT_done = (sem(n) for n in ("x_tr", "aT_full", "aT_hi_done", "aT_done"))
        w_hi_done, w_lo_done = sem("w_hi_done"), sem("w_lo_done")
        cT_full, cT_hi_done = sem("cT_full"), sem("cT_hi_done")
        p1_done, p2_done, p3_done = sem("p1_done"), sem("p2_done"), sem("p3_done")
        c_sq, c_ms, c_rstd, cn_done, k_raw_done = sem("c_sq"), sem("c_ms"), sem("c_rstd"), sem("cn_done"), sem("k_raw_done")
        c_tr, cT_done, u_done = sem("c_tr"), sem("cT_done"), sem("u_done")
        q_mm, kv_mm, q_sq, q_ss, q_ms, q_rstd = (sem(n) for n in ("q_mm", "kv_mm", "q_sq", "q_ss", "q_ms", "q_rstd"))
        k_sq, k_ss, k_ms, k_eps, k_rstd, v_done = (sem(n) for n in ("k_sq", "k_ss", "k_ms", "k_eps", "k_rstd", "v_done"))
        qn_done, qx_done, kn_done, rope_step, qr_done, kr_done = (
            sem(n) for n in ("qn_done", "qx_done", "kn_done", "rope_step", "qr_done", "kr_done"))
        qn_tr, kn_tr, r_tr, qT_done, kT_done, rT_done = (
            sem(n) for n in ("qn_tr", "kn_tr", "r_tr", "qT_done", "kT_done", "rT_done"))
        s_ready, row_max, neg_max, exp_done, recip_done, p_done, p_tr = (
            sem(n) for n in ("s_ready", "row_max", "neg_max", "exp_done", "recip_done", "p_done", "p_tr"))
        pT_act, pT_dve = sem("pT_act"), sem("pT_dve")
        pv_done, o_act, o_dve, o_lo_done = sem("pv_done"), sem("o_act"), sem("o_dve"), sem("o_lo_done")
        d_mm, dT_done, mix_mm, mix_done = sem("d_mm"), sem("dT_done"), sem("mix_mm"), sem("mix_done")
        o_mm, h_done, h_sq, h_ms, h_rstd, a2_done = (sem(n) for n in ("o_mm", "h_done", "h_sq", "h_ms", "h_rstd", "a2_done"))
        a2_tr, a2T_done, lg_mm, lg_bias = (sem(n) for n in ("a2_tr", "a2T_done", "lg_mm", "lg_bias"))
        route_step, g_exp, e_exp, neg_g, e_diff = (sem(n) for n in ("route_step", "g_exp", "e_exp", "neg_g", "e_diff"))
        mask_done, rank_mm, pos_done, gates_done = (sem(n) for n in ("mask_done", "rank_mm", "pos_done", "gates_done"))
        h_stored, rows_stored, slots_stored = sem("h_stored"), sem("rows_stored"), sem("slots_stored")
        total_mm, counts_done = sem("total_mm"), sem("counts_done")
        idx_in, idx_rest_in, idx_set = sem("idx_in"), sem("idx_rest_in"), sem("idx_set")

        class PassSignals:

            def __init__(self, prefix, o):
                self.o = o
                self.gathered = [sem(f"{prefix}gathered{b}") for b in range(3 if o == 0 else 1)]
                self.x_tr, self.x_act, self.x_dve = sem(prefix + "x_tr"), sem(prefix + "x_act"), sem(prefix + "x_dve")
                self.gu_mm, self.silu_done = sem(prefix + "gu_mm"), sem(prefix + "silu_done")
                self.gate_done, self.hid_done = sem(prefix + "gate_done"), sem(prefix + "hid_done")
                self.h_tr, self.hT_done, self.y_mm = sem(prefix + "h_tr"), sem(prefix + "hT_done"), sem(prefix + "y_mm")
                self.y_act, self.y_dve, self.added = sem(prefix + "y_act"), sem(prefix + "y_dve"), sem(prefix + "added")

        main, over = PassSignals("main_", 0), PassSignals("more_", 1)
        refill_go, dma_go = sem("refill_go"), sem("dma_go")
        over_idx_in, more_set = sem("more_idx_in"), sem("more_idx_set")

        def w_gu(b, lane, k, g):
            return weights[b][:, lane, g, k * FH:(k + 1) * FH]

        def w_dn(b, lane, k, n):
            return weights[b][:, lane, 2, k * D + n * 512:k * D + (n + 1) * 512]

        units = [(s, hp, qt) for hp in range(2) for s in range(2) for qt in range(TILES[s])]
        last_of_head = [m for m, (s, hp, qt) in enumerate(units) if qt == TILES[s] - 1]

        def x_dram(i):
            s = 0 if i < FIRST[1] else 1
            r = (i - FIRST[s]) * P
            return a["x_prompt" if s == 0 else "x_sample"][0, r:r + P, :]

        def load_pair(sp, j, b, parts=range(6)):
            for n in parts:
                what, lane = n // 2, n % 2
                if n >= 3:
                    sp.wait_ge(part_in[n - 3], 16 * (j + 1))
                elif not (isinstance(j, int) and j == 0):
                    sp.wait_ge(part_in[n + 3], 16 * j)
                name, k = ("w_gate", "w_up", "w_down")[what], 2 if what == 2 else KD
                src = a[name][0, bass.ds(PAIRS * lane + j, 1)].rearrange("e (p k) f -> p (e k f)", k=k)
                sp.dma_start(weights[b][:, lane, what, :], src).then_inc(part_in[n], 16)

        def pe_y_free(pe, j):
            if isinstance(j, int) and j == 0:
                return
            pe.wait_ge(main.y_act, j)
            pe.wait_ge(main.y_dve, j)

        def run_pairs(eng, pair):
            for b in range(3):
                pair(b, 0, b, False)
            with eng.Fori(1, PAIRS // 3) as i:
                for b in range(3):
                    pair(3 * i + b, i, b, False)
            pair(PAIRS - 1, PAIRS // 3, 0, True)

        def passes_counter(eng):
            before = eng.alloc_register("more_before")
            eng.reg_mov(before, 0)

            def run(j, again):
                todo = eng.value_load(counts_i[0:1, 3, bass.ds(j, 1)], min_val=0, max_val=PASSES - 1)
                with eng.If(todo > 0):
                    with eng.Fori(1, todo + 1) as p:
                        n = eng.snap(before)
                        again(n, p)
                        eng.reg_add(before, before, 1)
            return run

        def y_free(eng, q, n):
            if q is over:
                if not (isinstance(n, int) and n == 0):
                    eng.wait_ge(over.added, 16 * n)
            elif not (isinstance(n, int) and n < 3):
                eng.wait_ge(main.added, 16 * (n - 2))

        def pT_copy(eng, m, u):
            s, hp, qt = units[m]
            eng.wait_ge(p_tr, 2 * m + u + 1)
            g = sum(1 for x in last_of_head if x < m)
            if g >= 1:
                eng.wait_ge(pv_done, 2 * g)
            dst = pT[:, u, 0:TILES[s], qt * P:(qt + 1) * P]
            src = ps[:, 4 + u, 0:SEQS[s]].rearrange("p (c t) -> p c t", c=TILES[s])
            if u == 0:
                eng.activation(dst, src, ACT.Copy).then_inc(pT_act, 1)
            else:
                eng.tensor_copy(dst, src).then_inc(pT_dve, 1)

        def o_place(m):
            s, hp, qt = units[m]
            return slice(FIRST[s] * P, FIRST[s] * P + SEQS[s]), SEQS[s], 2 * hp

        def o_copy(eng, m, u):
            eng.wait_ge(pv_done, 2 * last_of_head.index(m) + u + 1)
            place, n, h = o_place(m)
            if u == 0:
                eng.activation(o_hi[:, h, place], ps[:, 6, 0:n], ACT.Copy).then_inc(o_act, 1)
            else:
                eng.tensor_copy(o_hi[:, h + 1, place], ps[:, 7, 0:n]).then_inc(o_dve, 1)

        def o_split(dve, m):
            g = last_of_head.index(m)
            place, n, h = o_place(m)
            for u, high_done in ((1, o_dve), (0, o_act)):
                dve.wait_ge(high_done, g + 1)
                dve.tensor_tensor(o_lo[:, h + u, place], ps[:, 6 + u, 0:n], o_hi[:, h + u, place].bitcast(F32),
                                  ALU.subtract).then_inc(o_lo_done, 1)


        N_GAINS = 14
        block = ctx.enter_context(nc.Block())

        @block.sync
        def _(sp):
            sp.dma_start(x_sb[:, :], x_dram(0)).then_inc(x_in, 16)
            sp.dma_start(consts[:, :], a["consts"]).then_inc(consts_in, 16)
            with nc.allow_non_contiguous_dma(reason="128 short rows"):
                sp.dma_start(g_attn[:, :], a["g_attn_norm"][0].rearrange("(p k) -> p k", k=KD)).then_inc(g_attn_in, 16)
            w_in_d = a["w_in"][0].rearrange("(p k) n -> p k n", k=KD)
            
            def load_w_in(n):
                sp.dma_start(w_in_raw[n][:, :, :], w_in_d[:, :, W_CUTS[n]:W_CUTS[n + 1]]).then_inc(w_in_in[n], 16)

            load_w_in(0)
            gains = [
                (g_lat[:, 0:KQ], a["g_q_lat"][0].rearrange("(p k) -> p k", k=KQ)),
                (g_lat[:, KQ:], a["g_kv_lat"][0].rearrange("(p k) -> p k", k=KKV)),
                (g_nope[:, 0:1], a["g_q_head"][0, 0:DN].rearrange("(p k) -> p k", k=1)),
                (g_nope[:, 1:2], a["g_k_head"][0, 0:DN].rearrange("(p k) -> p k", k=1)),
                (g_pool[:, :], a["pool_scale"][0].rearrange("(g p) -> p g", p=P)),
                (tok_ids[:, :], a["tokens"]),
                (w_router[:, :, 0:EG], a["w_group_router"][0].rearrange("(p k) n -> p k n", k=KD)),
                (w_router[:, :, EG:], a["w_expert_router"][0].rearrange("(p k) n -> p k n", k=KD)),
            ]
            half = DR // 2
            for n, name in enumerate(("g_q_head", "g_k_head")):
                g = a[name][0:1, DN:DQK]
                gains += [(g_rope[:, 2 * n, :], g.partition_broadcast(P)),
                          (g_rope[:, 2 * n + 1, 0:half], g[:, half:DR].partition_broadcast(P)),
                          (g_rope[:, 2 * n + 1, half:DR], g[:, 0:half].partition_broadcast(P))]
            with nc.allow_non_contiguous_dma(reason="a few hundred short rows"):
                for dst, src in gains:
                    sp.dma_start(dst, src).then_inc(gains_in, 16)
            assert len(gains) == N_GAINS
            load_w_in(1)
            sp.wait_ge(xn_done, 1)
            sp.dma_start(x_sb[:, :], x_dram(1)).then_inc(x_in, 16)
            load_w_in(2)
            sp.dma_start(w_uq_raw[:, :, :], a["w_uq"][0].rearrange("(p k) n -> p k n", k=KQ)).then_inc(w_up_in, 16)
            sp.dma_start(w_ukv[:, :, :], a["w_ukv"][0].rearrange("(p k) n -> p k n", k=KKV)).then_inc(w_up_in, 16)
            sp.dma_start(slot_table.rearrange("(a b) c -> a (b c)", a=P),
                         a["slots"].rearrange("(a b) c -> a (b c)", a=P)).then_inc(setup_dram, 16)
            sp.dma_start(table[T:T + P, :], a["zeros"]).then_inc(setup_dram, 16)
            sp.dma_start(out[T:T + P, :], a["zeros"][:, 0:D]).then_inc(setup_dram, 16)
            for i in range(2, NT):
                sp.wait_ge(xn_done, i)
                sp.dma_start(x_sb[:, :], x_dram(i)).then_inc(x_in, 16)
            sp.wait_ge(kv_mm, NT)
            sp.wait_ge(r_tr, NT)
            sp.wait_ge(qT_done, NT)
            sp.wait_ge(kT_done, NT)
            sp.wait_ge(rT_done, NT)
            sp.wait_ge(v_done, NT)
            sp.dma_start(band[:, :, :, :], a["band"].rearrange("p (g k c) -> p g k c", g=NG, k=3)).then_inc(pool_in, 16)
            sp.dma_start(w_pool[:, :, :], a["w_pool"][0].rearrange("g c d -> c g d")).then_inc(pool_in, 16)
            sp.wait_ge(q_mm, NT)
            sp.wait_ge(qr_done, NT)
            for k in range(KD):
                if k >= 3:
                    sp.wait_ge(w_out_lo_done, k - 2)
                sp.dma_start(w_out_raw[k % 3][:, :], a["w_out"][0, k * P:(k + 1) * P, :]).then_inc(w_out_in[k % 3], 16)
            sp.wait_ge(d_mm, NG)
            sp.dma_start(x_res[:, :], x_dram(0)).then_inc(x_res_in, 16)
            sp.dma_start(g_ffn[:, :], a["g_ffn_norm"].partition_broadcast(P)).then_inc(g_ffn_in, 16)
            sp.dma_start(r_bias[:, 0:EG], a["b_group_router"].partition_broadcast(P)).then_inc(g_ffn_in, 16)
            sp.dma_start(r_bias[:, EG:], a["b_expert_router"].partition_broadcast(P)).then_inc(g_ffn_in, 16)
            sp.wait_ge(mix_mm, NG)
            sp.wait_ge(dT_done, 2 * NG)
            sp.wait_ge(w_out_lo_done, KD)
            load_pair(sp, 0, 0)

            def store_rows(i):
                sp.wait_ge(gates_done, i + 1)
                sp.dma_start(table[i * P:(i + 1) * P, :], rows[:, i % 2, :]).then_inc(rows_stored, 16)

            for i in range(NT):
                sp.wait_ge(h_done, 2 * (i + 1))
                sp.dma_start(out[i * P:(i + 1) * P, :], h_sb[:, i % 2, :]).then_inc(h_stored, 16)
                if i + 1 < NT:
                    sp.dma_start(x_res[:, :], x_dram(i + 1)).then_inc(x_res_in, 16)
                else:
                    load_pair(sp, 1, 1, range(3))
                if i >= 1:
                    store_rows(i - 1)
            load_pair(sp, 1, 1, range(3, 4))
            store_rows(NT - 1)
            sp.wait_ge(slots_stored, 2 * NT * 16)
            sp.wait_ge(counts_done, 1)
            sp.dma_start(idx_all[:, 0:PAIRS], slot_table[0:BLOCK, :].rearrange("(s j) c -> s (j c)", j=PAIRS)).then_inc(idx_in, 16)
            sp.dma_start(idx_more[:, :], slot_table[BLOCK:2 * BLOCK, :].rearrange("(s j) c -> s (j c)", j=PAIRS)).then_inc(idx_rest_in, 16)
            with nc.allow_non_contiguous_dma(reason="128 indices"):
                sp.dma_start(idx_all[:, PAIRS:], a["slots"][0:BLOCK, :].rearrange("(s j) c -> s (j c)", j=PAIRS)[:, 0:1]).then_inc(idx_rest_in, 16)

            sp.wait_ge(main.gathered[0], 16)
            load_pair(sp, 1, 1, range(4, 6))
            load_pair(sp, 2, 2)

            more = sp.alloc_register("more_total")
            sp.reg_mov(more, 0)

            def refill(j, b):
                todo = sp.value_load(counts_i[0:1, 3, bass.ds(j - 3, 1)], min_val=0, max_val=PASSES - 1)
                sp.reg_add(more, more, todo)
                passes = sp.snap(more)

                def used(kind):
                    sp.wait_ge(kind(main), j - 2)
                    sp.wait_ge(kind(over), passes)
                    sp.sem_inc(refill_go, 1)

                used(lambda q: q.gu_mm)
                load_pair(sp, j, b, range(4))
                used(lambda q: q.y_mm)
                load_pair(sp, j, b, range(4, 6))

            with sp.Fori(1, PAIRS // 3) as i:
                for b in range(3):
                    refill(3 * i + b, b)
            refill(PAIRS - 1, 0)

        @block.tensor
        def _(pe):
            def x_transposes(i):
                pe.wait_ge(xn_done, i + 1)
                if i >= 1:
                    pe.wait_ge(aT_full, 2 * i)
                if i == 0:
                    pe.wait_ge(consts_in, 16)
                for k in range(KD):
                    mm = pe.transpose(ps[:, k // 4, (k % 4) * P:(k % 4 + 1) * P], xn[:, k, :], ident)
                    if k % 4 == 3:
                        mm.then_inc(x_tr, 1)

            def split_product(dst, ks, l_hi, l_lo, r_hi, r_lo, first=True, last=True, lo_ready=None):
                for k in ks:
                    pe.matmul(dst, l_hi(k), r_hi(k), start=(first and k == ks[0]), stop=False)
                    pe.matmul(dst, l_hi(k), r_lo(k), start=False, stop=False)
                if lo_ready:
                    pe.wait_ge(*lo_ready)
                for k in ks:
                    mm = pe.matmul(dst, l_lo(k), r_hi(k), start=False, stop=(last and k == ks[-1]))
                return mm

            def project(i, n, bank, done):
                lo, hi = W_CUTS[n], W_CUTS[n + 1]
                dst = ps[:, bank, 0:hi - lo]
                if i == 0:
                    pe.wait_ge(w_in_in[n], 16)
                    for k in range(KD):
                        mm = pe.matmul(dst, aT0[:, k, :], w_in_raw[n][:, k, :], start=(k == 0), stop=(k == KD - 1))
                else:
                    pe.wait_ge(w_lo_done, n + 1)
                    mm = split_product(dst, range(KD), lambda k: aT_hi[:, k, :], lambda k: aT_lo[:, k, :],
                                       lambda k: w_in_hi[:, k, lo:hi], lambda k: w_in_lo[:, k, lo:hi])
                mm.then_inc(done, 1)

            def head_transposes(i, src, ready, done):
                pe.wait_ge(ready, i + 1)
                for h in range(H):
                    mm = pe.transpose(ps[:, 7, h * P:(h + 1) * P], src[:, h, :], ident)
                mm.then_inc(done, 1)

            def rope_transposes(i):
                pe.wait_ge(qr_done, i + 1)
                pe.wait_ge(kr_done, i + 1)
                pe.wait_ge(kT_done, i + 1)
                for n, src in enumerate((q_r, k_r)):
                    flat = src[:, :, :].rearrange("t h r -> t (h r)")
                    for hp in range(2):
                        mm = pe.transpose(ps[:, 7, (2 * n + hp) * P:(2 * n + hp + 1) * P], flat[:, hp * P:(hp + 1) * P], ident)
                mm.then_inc(r_tr, 1)

            x_transposes(0)
            for i in range(NT):
                if i == 0:
                    pe.wait_ge(aT_full, 2)
                else:
                    pe.wait_ge(aT_done, i)
                project(i, 0, 4, p1_done)
                if i >= 1:
                    if i >= 2:
                        pe.wait_ge(rT_done, i - 1)
                    head_transposes(i - 1, q_n, qn_done, qn_tr)
                if i >= 1:
                    pe.wait_ge(q_sq, i)
                    pe.wait_ge(qn_done, i)
                project(i, 1, 3, p2_done)
                if i >= 1:
                    pe.wait_ge(qT_done, i)
                    head_transposes(i - 1, k_n, kn_done, kn_tr)
                project(i, 2, 2, p3_done)
                pe.wait_ge(cn_done, 2 * (i + 1))
                pe.wait_ge(k_raw_done, i + 1)
                for k in range(KQ + KKV):
                    bank, col = (4, k) if k < KQ else (3, k - KQ)
                    mm = pe.transpose(ps[:, bank, col * P:(col + 1) * P], cn[:, k, :], ident)
                mm.then_inc(c_tr, 1)
                if i + 1 < NT:
                    x_transposes(i + 1)
                if i >= 1:
                    rope_transposes(i - 1)
                if i == 0:
                    pe.wait_ge(cT_done, 1)
                else:
                    pe.wait_ge(cT_hi_done, i)
                pe.wait_ge(u_done, i + 1)
                pe.wait_ge(w_up_in, 32)
                if i >= 1:
                    pe.wait_ge(w_lo_done, 4)
                for n in range(2):
                    c = slice(n * 384, (n + 1) * 384)
                    if i == 0:
                        for k in range(KQ):
                            mm = pe.matmul(ps[:, 2 + n, 0:384], cn[:, k, :], w_uq_raw[:, k, c], start=(k == 0), stop=(k == KQ - 1))
                    else:
                        mm = split_product(ps[:, 2 + n, 0:384], range(KQ), lambda k: cT_hi[:, k, :], lambda k: cT_lo[:, k, :],
                                           lambda k: w_uq_hi[:, k, c], lambda k: w_uq_lo[:, k, c],
                                           lo_ready=(cT_done, i + 1))
                mm.then_inc(q_mm, 1)
                if i >= 1:
                    pe.wait_ge(k_sq, i)
                    pe.wait_ge(kn_done, i)
                    pe.wait_ge(v_done, i)
                for n in range(2):
                    for k in range(KKV):
                        mm = pe.matmul(ps[:, 5 + n, :], cT_kv[:, k, :], w_ukv[:, k, n * 512:(n + 1) * 512],
                                       start=(k == 0), stop=(k == KKV - 1))
                mm.then_inc(kv_mm, 1)
            def scores(m):
                s, hp, qt = units[m]
                keys = slice(FIRST[s] * P, (FIRST[s] + TILES[s]) * P)
                q = slice((FIRST[s] + qt) * P, (FIRST[s] + qt + 1) * P)
                if m >= 2:
                    pe.wait_ge(exp_done, 2 * (m - 1))
                bank = 2 * (m % 2)
                n = SEQS[s]
                for u in range(2):
                    h = 2 * hp + u
                    pe.matmul(ps[:, bank + u, 0:n], qT[:, h, q], kT[:, h, keys], start=True, stop=False)
                for u in range(2):
                    r = slice(u * DR, (u + 1) * DR)
                    pe.matmul(ps[:, bank + u, 0:n], rT[r, hp, q], rT[r, 2 + hp, keys], start=False, stop=True).then_inc(s_ready, 1)

            pe.wait_ge(aT_full, 2 * NT)
            pe.wait_ge(rT_done, NT - 1)
            pe.wait_ge(qT_done, NT - 1)
            pe.wait_ge(kT_done, NT - 1)
            scores(0)
            head_transposes(NT - 1, q_n, qn_done, qn_tr)
            pe.wait_ge(qT_done, NT)
            head_transposes(NT - 1, k_n, kn_done, kn_tr)
            rope_transposes(NT - 1)

            pe.wait_ge(rT_done, NT)
            pe.wait_ge(kT_done, NT)
            pe.wait_ge(v_done, NT)
            pe.wait_ge(k_sq, NT)
            pe.wait_ge(kn_done, NT)
            pe.wait_ge(qn_done, NT)
            pe.wait_ge(u_done, NT)

            def p_transposes(m):
                s, hp, qt = units[m]
                if m >= 1:
                    pe.wait_ge(pT_act, m)
                    pe.wait_ge(pT_dve, m)
                for u in range(2):
                    pe.wait_ge(p_done, 2 * m + u + 1)
                    for c in range(TILES[s]):
                        mm = pe.transpose(ps[:, 4 + u, c * P:(c + 1) * P], p_sb[:, (2 * m + u) % 4, c * P:(c + 1) * P], ident)
                    mm.then_inc(p_tr, 1)

            def attend(m):
                s, hp, qt = units[m]
                g = last_of_head.index(m)
                pe.wait_ge(pT_act, m + 1)
                pe.wait_ge(pT_dve, m + 1)
                if g >= 1:
                    pe.wait_ge(o_lo_done, 2 * g)
                for u in range(2):
                    h = 2 * hp + u
                    for c in range(TILES[s]):
                        mm = pe.matmul(ps[:, 6 + u, 0:SEQS[s]], v_sb[:, FIRST[s] + c, h * DV:(h + 1) * DV],
                                       pT[:, u, c, 0:SEQS[s]], start=(c == 0), stop=(c == TILES[s] - 1))
                    mm.then_inc(pv_done, 1)

            def windows(g):
                if g >= 2:
                    pe.wait_ge(dT_done, 2 * (g - 1))
                for s in range(2):
                    bank = 2 * (g % 2) + s
                    for t in range(TILES[s]):
                        kind = 0 if t == 0 else 2 if t == TILES[s] - 1 else 1
                        lo, hi = max(t * P - HALO, 0), min((t + 1) * P + HALO, SEQS[s])
                        c = lo - (t * P - HALO)
                        mm = pe.matmul(ps[:, bank, lo:hi], u_sb[:, FIRST[s] + t, g * GC:(g + 1) * GC],
                                       band[:, g, kind, c:c + hi - lo], start=(t == 0), stop=(t == TILES[s] - 1),
                                       skip_group_check=True)
                mm.then_inc(d_mm, 1)

            def mix(g):
                pe.wait_ge(dT_done, 2 * (g + 1))
                if g == 0:
                    pe.wait_ge(o_lo_done, 2 * len(last_of_head))
                if g >= 2:
                    pe.wait_ge(mix_done, 4 * (g - 1))
                for s in range(2):
                    mm = pe.matmul(ps[:, 4 + 2 * (g % 2) + s, 0:SEQS[s]], w_pool[:, g, :],
                                   dT[:, g % 2, FIRST[s] * P:FIRST[s] * P + SEQS[s]], start=True, stop=True)
                mm.then_inc(mix_mm, 1)

            for m in range(len(units)):
                if m + 1 < len(units):
                    scores(m + 1)
                if m - 1 in last_of_head:
                    attend(m - 1)
                if m + 1 == len(units):
                    pe.wait_ge(pool_in, 32)
                    pe.wait_ge(exp_done, 2 * m)
                    windows(0)
                p_transposes(m)
            pe.wait_ge(exp_done, 2 * len(units))
            windows(1)
            attend(len(units) - 1)
            for g in range(NG):
                mix(g)
                if g + 2 < NG:
                    windows(g + 2)

            pe.wait_ge(w_out_lo_done, KD)
            pe.wait_ge(bf_set, 2)

            def out_half(i, n):
                if i >= 2:
                    pe.wait_ge(h_done, 2 * (i - 1))
                t, c = slice(i * P, (i + 1) * P), slice(n * 512, (n + 1) * 512)
                dst = ps[:, 2 * (i % 2) + n, :]
                split_product(dst, range(H), lambda k: o_hi[:, k, t], lambda k: o_lo[:, k, t],
                              lambda k: w_out_hi[:, k, c], lambda k: w_out_lo[:, k, c], last=False)
                if i == 0:
                    pe.wait_ge(mix_done, 4 * NG)
                mm = split_product(dst, range(H, KD), lambda k: pool_hi[:, k - H, t],
                                   lambda k: pool_lo[(k - H) // 2][:, (k - H) % 2, t],
                                   lambda k: w_out_hi[:, k, c], lambda k: w_out_lo[:, k, c], first=False)
                mm.then_inc(o_mm, 1)

            def row_transposes(i):
                pe.wait_ge(a2_done, i + 1)
                if i >= 1:
                    pe.wait_ge(a2T_done, 2 * i)
                for k in range(KD):
                    mm = pe.transpose(ps[:, 4 + k // 4, (k % 4) * P:(k % 4 + 1) * P], rows[:, i % 2, k * P:(k + 1) * P], ident)
                mm.then_inc(a2_tr, 1)

            def logits(i):
                pe.wait_ge(a2T_done, 2 * (i + 1))
                if i >= 1:
                    pe.wait_ge(lg_bias, i)
                for k in range(KD):
                    mm = pe.matmul(ps[:, 7, 0:EG + E], a2T[:, k, :], w_router[:, k, :], start=(k == 0), stop=(k == KD - 1))
                mm.then_inc(lg_mm, 1)

            def ranks(i):
                pe.wait_ge(mask_done, i + 1)
                if i >= 1:
                    pe.wait_ge(pos_done, i)
                pe.matmul(ps[:, 6, 128:128 + E], ones_bf, m_sum[:, 0, :], start=True, stop=False)
                pe.matmul(ps[:, 6, 128:128 + E], ltri_bf, m_sum[:, 1, :], start=False, stop=True).then_inc(rank_mm, 1)

            for i in range(NT):
                out_half(i, 0)
                if i >= 1:
                    row_transposes(i - 1)
                out_half(i, 1)
                if i >= 2:
                    ranks(i - 2)
                if i >= 1:
                    logits(i - 1)
            row_transposes(NT - 1)
            ranks(NT - 2)
            logits(NT - 1)
            ranks(NT - 1)
            pe.wait_ge(pos_done, NT)
            pe.matmul(ps[:, 7, 0:E], ones_bf, m_sum[:, 0, :], start=True, stop=True).then_inc(total_mm, 1)

            pe.wait_ge(counts_done, 1)

            def gather_transposes(q, src, landed, uses):
                pe.wait_ge(landed, 16 * uses)
                banks = 0 if q is main else 6
                for k in range(KD):
                    mm = pe.transpose(ps[:, banks + k // 4, (k % 4) * P:(k % 4 + 1) * P], src[:, k * P:(k + 1) * P], ident)
                mm.then_inc(q.x_tr, 1)

            def gate_up(q, b, n):
                pe.wait_ge(q.x_act, n + 1)
                pe.wait_ge(q.x_dve, n + 1)
                for g in range(2):
                    if q is main:
                        for lane in range(2):
                            pe.wait_ge(part_in[2 * g + lane], 16 * (n + 1))
                    for k in range(KD):
                        for lane in range(2):
                            r = slice(lane * LANE, (lane + 1) * LANE)
                            mm = pe.matmul(ps[r, 2, g * FH:(g + 1) * FH], xT[:, q.o, k, r], w_gu(b, lane, k, g),
                                           start=(k == 0), stop=(k == KD - 1))
                mm.then_inc(q.gu_mm, 1)

            def hidden_transposes(q, n):
                pe.wait_ge(q.hid_done, n + 1)
                for k in range(2):
                    mm = pe.transpose(ps[:, 3, k * P:(k + 1) * P], hid[:, q.o, k, :], ident)
                mm.then_inc(q.h_tr, 1)

            def down(q, b, n):
                pe.wait_ge(q.hT_done, n + 1)
                for half in range(2):
                    for k in range(2):
                        for lane in range(2):
                            r = slice(lane * LANE, (lane + 1) * LANE)
                            mm = pe.matmul(ps[r, 4 + half, :], hT[:, q.o, k, r], w_dn(b, lane, k, half),
                                           start=(k == 0), stop=(k == 1))
                mm.then_inc(q.y_mm, 1)

            more_passes = passes_counter(pe)

            def pair(j, i, b, last):
                gate_up(main, b, j)
                if not last:
                    nb = (b + 1) % 3
                    gather_transposes(main, g_rows[:, nb, :], main.gathered[nb], i + 1 if b < 2 else i + 2)
                hidden_transposes(main, j)
                for n in range(4, 6):
                    pe.wait_ge(part_in[n], 16 * (j + 1))
                pe_y_free(pe, j)
                down(main, b, j)

                def again(n, p):
                    gather_transposes(over, more_rows[:, :], over.gathered[0], n + 1)
                    gate_up(over, b, n)
                    hidden_transposes(over, n)
                    pe.wait_ge(main.y_act, j + 1)
                    pe.wait_ge(main.y_dve, j + 1)
                    down(over, b, n)
                    pe.wait_ge(over.y_act, n + 1)
                    pe.wait_ge(over.y_dve, n + 1)

                more_passes(j, again)

            gather_transposes(main, g_rows[:, 0, :], main.gathered[0], 1)
            run_pairs(pe, pair)

        @block.scalar
        def _(act):
            def norm_x(i):
                act.wait_ge(x_in, 16 * (i + 1))
                if i == 1:
                    act.wait_ge(x_tr, 2)
                elif i > 1:
                    act.wait_ge(aT_done, i - 1)
                act.activation(xn[:, :, :].rearrange("t k p -> t (k p)"), x_sb[:, :], ACT.Square,
                               accum_out=stats[:, 0:1]).then_inc(x_sq, 1)
                act.wait_ge(x_rstd, i + 1)
                act.activation(xn[:, :, :].rearrange("t k p -> t p k"), x_sb[:, :].rearrange("t (p k) -> t p k", k=KD),
                               ACT.Copy, scale=stats[:, 2:3]).then_inc(xn_done, 1)

            def heads_out(i, col, dst, tr, done):
                act.wait_ge(tr, i + 1)
                act.activation(dst[:, :, i * P:(i + 1) * P], ps[:, 7, :].rearrange("p (h t) -> p h t", h=H), ACT.Copy,
                               scale=g_nope[:, col:col + 1]).then_inc(done, 1)

            def round_weights(n):
                if n < 3:
                    act.wait_ge(w_in_in[n], 16)
                    src, dst = w_in_raw[n][:, :, :], w_in_hi[:, :, W_CUTS[n]:W_CUTS[n + 1]]
                else:
                    act.wait_ge(w_up_in, 32)
                    src, dst = w_uq_raw[:, :, :], w_uq_hi[:, :, :]
                act.activation(dst, src, ACT.Copy).then_inc(w_hi_done, 1)

            norm_x(0)
            round_weights(0)
            for i in range(NT):
                if i == 1:
                    act.wait_ge(gains_in, 16 * N_GAINS)
                if i + 1 < NT:
                    norm_x(i + 1)
                act.wait_ge(p1_done, i + 1)
                if i >= 1:
                    act.wait_ge(k_ss, i)
                    act.wait_ge(c_rstd, i)
                act.activation(junk[:, 0:RQ], ps[:, 4, 0:RQ], ACT.Square, accum_out=stats[:, 4:5]).then_inc(c_sq, 1)
                if i >= 1:
                    heads_out(i - 1, 0, qT, qn_tr, qT_done)
                if i == 0:
                    round_weights(1)
                act.wait_ge(p2_done, i + 1)
                act.wait_ge(c_sq, 3 * i + 1)
                act.activation(junk[:, 0:RKV], ps[:, 3, 0:RKV], ACT.Square, accum_out=stats[:, 5:6]).then_inc(c_sq, 1)
                act.wait_ge(c_sq, 3 * i + 2)
                if i >= 1:
                    act.wait_ge(k_ms, i)
                    act.wait_ge(kr_done, i)
                act.activation(junk[:, 0:DR], ps[:, 3, RKV:RKV + DR], ACT.Square, accum_out=stats[:, 6:7]).then_inc(c_sq, 1)
                act.activation(k_raw[:, :], ps[:, 3, RKV:RKV + DR], ACT.Copy).then_inc(k_raw_done, 1)
                if i == 1:
                    act.wait_ge(w_lo_done, 4)
                if i >= 1:
                    heads_out(i - 1, 1, kT, kn_tr, kT_done)
                act.wait_ge(c_rstd, i + 1)
                if i >= 1:
                    act.wait_ge(cT_done, i)
                    act.wait_ge(q_mm, i)
                act.activation(cn[:, 0:KQ, :].rearrange("t k p -> t p k"), ps[:, 4, 0:RQ].rearrange("t (p k) -> t p k", k=KQ),
                               ACT.Copy, scale=stats[:, 8:9]).then_inc(cn_done, 1)
                act.activation(cn[:, KQ:, :].rearrange("t k p -> t p k"), ps[:, 3, 0:RKV].rearrange("t (p k) -> t p k", k=KKV),
                               ACT.Copy, scale=stats[:, 9:10]).then_inc(cn_done, 1)
                if i == 0:
                    round_weights(2)
                    act.wait_ge(w_lo_done, 2)
                act.wait_ge(p3_done, i + 1)
                act.activation(u_sb[:, i, :], ps[:, 2, :], ACT.Copy).then_inc(u_done, 1)
                act.wait_ge(q_mm, i + 1)
                act.wait_ge(c_sq, 3 * i + 3)
                act.activation(junk[:, 0:H * DQK].rearrange("t (b c) -> t b c", b=2), ps[:, 2:4, 0:384], ACT.Square).then_inc(q_sq, 1)
                act.wait_ge(kv_mm, i + 1)
                act.wait_ge(q_ss, i + 1)
                kv = ps[:, 5:7, :].rearrange("t b (h w) -> t b h w", h=2)
                act.activation(junk[:, 0:H * DN].rearrange("t (b h w) -> t b h w", b=2, h=2), kv[:, :, :, 0:DN], ACT.Square).then_inc(k_sq, 1)
                if i == 0:
                    act.wait_ge(w_lo_done, 3)
                act.activation(v_sb[:, i, :].rearrange("t (b h w) -> t b h w", b=2, h=2), kv[:, :, :, DN:], ACT.Copy).then_inc(v_done, 1)
                if i == 0:
                    round_weights(3)
            heads_out(NT - 1, 0, qT, qn_tr, qT_done)
            heads_out(NT - 1, 1, kT, kn_tr, kT_done)

            act.wait_ge(r_tr, NT)
            act.wait_ge(rT_done, NT)
            for m, (s, hp, qt) in enumerate(units):
                n = SEQS[s]
                for u in range(2):
                    w = 2 * m + u
                    act.wait_ge(neg_max, w + 1)
                    if w >= 4:
                        act.wait_ge(p_tr, w - 3)
                    act.activation(p_sb[:, w % 4, 0:n], ps[:, 2 * (m % 2) + u, 0:n], ACT.Exp, bias=a_stat[:, w % 4, 1:2],
                                   scale=SCALE, accum_out=a_stat[:, w % 4, 2:3]).then_inc(exp_done, 1)
                if m >= 1:
                    pT_copy(act, m - 1, 0)
                if m - 1 in last_of_head:
                    o_copy(act, m - 1, 0)
                if 1 <= m <= KD:
                    k = m - 1
                    act.wait_ge(w_out_in[k % 3], 16 * (k // 3 + 1))
                    act.activation(w_out_hi[:, k, :], w_out_raw[k % 3][:, :], ACT.Copy).then_inc(w_out_hi_done, 1)
            pT_copy(act, len(units) - 1, 0)
            o_copy(act, len(units) - 1, 0)

            for g in range(NG):
                act.wait_ge(d_mm, g + 1)
                if g >= 2:
                    act.wait_ge(mix_mm, g - 1)
                for s in range(2):
                    act.activation(dT[:, g % 2, FIRST[s] * P:FIRST[s] * P + SEQS[s]], ps[:, 2 * (g % 2) + s, 0:SEQS[s]],
                                   ACT.Copy).then_inc(dT_done, 1)

            def route_exps(i):
                act.wait_ge(neg_g, i + 1)
                if i >= 1:
                    act.wait_ge(gates_done, i)
                act.activation(route_f[:, 160:164], route_f[:, 128:132], ACT.Exp, bias=route_f[:, 176:177],
                               accum_out=route_f[:, 177:178]).then_inc(g_exp, 1)
                act.wait_ge(e_diff, i + 1)
                act.activation(route_f[:, 179:180], route_f[:, 178:179], ACT.Exp).then_inc(e_exp, 1)

            for i in range(NT):
                act.wait_ge(h_done, 2 * (i + 1))
                if i >= 1:
                    act.wait_ge(h_rstd, i)
                act.activation(h_junk[:, :], h_sb[:, i % 2, :], ACT.Square, accum_out=route_f[:, 400:401]).then_inc(h_sq, 1)
                if i >= 1:
                    route_exps(i - 1)
                act.wait_ge(a2_tr, i + 1)
                if i >= 1:
                    act.wait_ge(lg_mm, i)
                for half in range(2):
                    act.activation(a2T[:, 4 * half:4 * half + 4, :], ps[:, 4 + half, :].rearrange("p (k t) -> p k t", k=4),
                                   ACT.Copy).then_inc(a2T_done, 1)
            route_exps(NT - 1)

            act.wait_ge(counts_done, 1)

            def x_copy(q, n):
                act.wait_ge(q.x_tr, n + 1)
                bank = 0 if q is main else 6
                act.activation(xT[:, q.o, 0:4, :], ps[:, bank, :].rearrange("p (k t) -> p k t", k=4), ACT.Copy).then_inc(q.x_act, 1)

            def silu(q, n):
                act.wait_ge(q.gu_mm, n + 1)
                act.activation(s_act[:, q.o, :], ps[:, 2, 0:FH], ACT.Silu).then_inc(q.silu_done, 1)

            def y_copy(q, n, buf):
                act.wait_ge(q.y_mm, n + 1)
                y_free(act, q, n)
                act.activation(y_sb[:, buf, 0:512], ps[:, 4, :], ACT.Copy).then_inc(q.y_act, 1)

            more_passes = passes_counter(act)

            def pair(j, i, b, last):
                silu(main, j)
                if not last:
                    x_copy(main, j + 1)
                y_copy(main, j, b)

                def again(n, p):
                    x_copy(over, n)
                    silu(over, n)
                    y_copy(over, n, 3)

                more_passes(j, again)

            x_copy(main, 0)
            run_pairs(act, pair)

        @block.vector
        def _(dve):
            steps = {"rope": 0, "route": 0}

            def link(kind, signal, ins):
                steps[kind] += 1
                ins.then_inc(signal, 1)
                dve.wait_ge(signal, steps[kind])

            dve.wait_ge(consts_in, 16)
            dve.tensor_copy(ltri_bf, consts[:, C_LTRI:C_LTRI + P]).then_inc(bf_set, 1)
            dve.memset(ones_bf, 1.0).then_inc(bf_set, 1)
            dve.memset(m_sum[:, 0, :], 0.0).then_inc(bf_set, 1)
            def aT_copy(i):
                full = aT0 if i == 0 else xn
                for half in range(2):
                    dve.wait_ge(x_tr, 2 * i + (half if i == 0 else 1) + 1)
                    dve.tensor_tensor(full[:, 4 * half:4 * half + 4, :], ps[:, half, :].rearrange("p (k t) -> p k t", k=4),
                                      g_attn[:, 4 * half:4 * half + 4].unsqueeze(2).to_broadcast([P, 4, P]),
                                      ALU.mult).then_inc(aT_full, 1)
                if i >= 1:
                    dve.wait_ge(aT_full, 2 * (i + 1))
                    dve.wait_ge(p3_done, i)
                    dve.tensor_copy(aT_hi[:, :, :], xn[:, :, :]).then_inc(aT_hi_done, 1)
                    dve.wait_ge(aT_hi_done, i)
                    dve.tensor_tensor(aT_lo[:, :, :], xn[:, :, :], aT_hi[:, :, :].bitcast(F32), ALU.subtract).then_inc(aT_done, 1)

            def cT_copy(i):
                dve.wait_ge(c_tr, i + 1)
                dve.tensor_tensor(cn[:, 0:KQ, :], ps[:, 4, 0:RQ].rearrange("p (k t) -> p k t", k=KQ),
                                  g_lat[:, 0:KQ].unsqueeze(2).to_broadcast([P, KQ, P]), ALU.mult).then_inc(cT_full, 1)
                if i >= 1:
                    dve.wait_ge(kv_mm, i)
                kv = dve.tensor_tensor(cT_kv[:, :, :], ps[:, 3, 0:RKV].rearrange("p (k t) -> p k t", k=KKV),
                                       g_lat[:, KQ:].unsqueeze(2).to_broadcast([P, KKV, P]), ALU.mult)
                if i == 0:
                    kv.then_inc(cT_done, 1)
                    return
                dve.wait_ge(cT_full, i + 1)
                dve.tensor_copy(cT_hi[:, :, :], cn[:, 0:KQ, :]).then_inc(cT_hi_done, 1)
                dve.wait_ge(cT_hi_done, i)
                dve.tensor_tensor(cT_lo[:, :, :], cn[:, 0:KQ, :], cT_hi[:, :, :].bitcast(F32), ALU.subtract).then_inc(cT_done, 1)

            def split_weights(n):
                dve.wait_ge(w_hi_done, n + 1)
                if n < 3:
                    c = slice(W_CUTS[n], W_CUTS[n + 1])
                    raw, hi, lo = w_in_raw[n][:, :, :], w_in_hi[:, :, c], w_in_lo[:, :, c]
                else:
                    raw, hi, lo = w_uq_raw[:, :, :], w_uq_hi[:, :, :], w_uq_lo[:, :, :]
                dve.tensor_tensor(lo, raw, hi.bitcast(F32), ALU.subtract).then_inc(w_lo_done, 1)

            def rotate(x, o, n, pt, heads, done):
                half = DR // 2
                t = rope_t[:, :, 0:heads, :]
                cos = rope_tab[:, 2 * n, pt, :].unsqueeze(1).to_broadcast([P, heads, DR])
                lo = rope_tab[:, 2 * n + 1, pt, 0:half].unsqueeze(1).to_broadcast([P, heads, half])
                hi = rope_tab[:, 2 * n + 1, pt, half:DR].unsqueeze(1).to_broadcast([P, heads, half])
                dve.tensor_tensor(t[:, 0], x, cos, ALU.mult)
                dve.tensor_tensor(t[:, 1, :, 0:half], x[:, :, half:DR], lo, ALU.mult)
                link("rope", rope_step, dve.tensor_tensor(t[:, 1, :, half:DR], x[:, :, 0:half], hi, ALU.mult))
                return dve.tensor_tensor(o, t[:, 0], t[:, 1], ALU.add)

            dve.wait_ge(g_attn_in, 16)
            aT_copy(0)
            dve.wait_ge(gains_in, 16 * N_GAINS)
            for n in range(4):
                tab = consts[:, (C_COS, C_SIN)[n % 2]:(C_COS, C_SIN)[n % 2] + 4 * DR].rearrange("p (t r) -> p t r", t=4)
                dve.tensor_tensor(rope_tab[:, n, :, :], tab, g_rope[:, n, :].unsqueeze(1).to_broadcast([P, 4, DR]),
                                  ALU.mult).then_inc(tables_set, 1)
            dve.wait_ge(tables_set, 4)
            split_weights(0)
            for i in range(NT):
                pt = i - FIRST[0 if i < FIRST[1] else 1]
                if i == 0:
                    split_weights(1)
                cT_copy(i)
                if i + 1 < NT:
                    aT_copy(i + 1)
                if i == 0:
                    split_weights(2)
                if i >= 1:
                    dve.wait_ge(r_tr, i)
                    dve.tensor_copy(rT[:, :, (i - 1) * P:i * P], ps[:, 7, :].rearrange("p (n t) -> p n t", n=4)).then_inc(rT_done, 1)
                dve.wait_ge(q_sq, i + 1)
                if i >= 1:
                    dve.wait_ge(q_ms, i)
                dve.tensor_reduce(stats[:, 12:16], junk[:, 0:H * DQK].rearrange("t (h w) -> t h w", h=H), AX.X, ALU.add).then_inc(q_ss, 1)
                dve.wait_ge(q_rstd, i + 1)
                if i >= 1:
                    dve.wait_ge(qn_tr, i)
                    dve.wait_ge(qr_done, i)
                r = stats[:, 20:24].rearrange("t (b h) -> t b h", b=2).unsqueeze(3)
                q = ps[:, 2:4, 0:384].rearrange("t b (h w) -> t b h w", h=2)
                dve.tensor_tensor(q_x[:, :, :].rearrange("t (b h) w -> t b h w", b=2), q[:, :, :, DN:],
                                  r.to_broadcast([P, 2, 2, DR]), ALU.mult).then_inc(qx_done, 1)
                dve.tensor_tensor(q_n[:, :, :].rearrange("t (b h) w -> t b h w", b=2), q[:, :, :, 0:DN],
                                  r.to_broadcast([P, 2, 2, DN]), ALU.mult).then_inc(qn_done, 1)
                dve.wait_ge(k_sq, i + 1)
                if i >= 1:
                    dve.wait_ge(k_rstd, i)
                dve.tensor_reduce(stats[:, 28:32], junk[:, 0:H * DN].rearrange("t (h w) -> t h w", h=H), AX.X, ALU.add).then_inc(k_ss, 1)
                dve.wait_ge(qn_done, i + 1)
                rotate(q_x[:, :, :], q_r[:, :, :], 0, pt, H, qr_done).then_inc(qr_done, 1)
                dve.wait_ge(k_rstd, i + 1)
                dve.wait_ge(v_done, i + 1)
                if i >= 1:
                    dve.wait_ge(kn_tr, i)
                r = stats[:, 40:44]
                kv = ps[:, 5:7, :].rearrange("t b (h w) -> t b h w", h=2)
                dve.tensor_tensor(k_n[:, :, :].rearrange("t (b h) w -> t b h w", b=2), kv[:, :, :, 0:DN],
                                  r.rearrange("t (b h) -> t b h", b=2).unsqueeze(3).to_broadcast([P, 2, 2, DN]),
                                  ALU.mult).then_inc(kn_done, 1)
                dve.wait_ge(qr_done, i + 1)
                dve.wait_ge(k_raw_done, i + 1)
                link("rope", rope_step, rotate(k_raw[:, :].unsqueeze(1), rope_k[:, :].unsqueeze(1), 1, pt, 1, None))
                dve.tensor_tensor(k_r[:, :, :], rope_k[:, :].unsqueeze(1).to_broadcast([P, H, DR]),
                                  r.unsqueeze(2).to_broadcast([P, H, DR]), ALU.mult).then_inc(kr_done, 1)
                if i == 0:
                    split_weights(3)
            dve.wait_ge(r_tr, NT)
            dve.tensor_copy(rT[:, :, (NT - 1) * P:], ps[:, 7, :].rearrange("p (n t) -> p n t", n=4)).then_inc(rT_done, 1)

            dve.wait_ge(kr_done, NT)
            for m, (s, hp, qt) in enumerate(units):
                n = SEQS[s]
                for u in range(2):
                    w = 2 * m + u
                    st = a_stat[:, w % 4]
                    dve.wait_ge(s_ready, w + 1)
                    if w >= 4:
                        dve.wait_ge(exp_done, w - 3)
                        dve.wait_ge(p_done, w - 3)
                    dve.reduce_max(st[:, 0:1], ps[:, 2 * (m % 2) + u, 0:n], AX.X).then_inc(row_max, 1)
                    dve.wait_ge(row_max, w + 1)
                    dve.tensor_scalar(st[:, 1:2], st[:, 0:1], -SCALE, None, ALU.mult).then_inc(neg_max, 1)
                if m >= 1:
                    pT_copy(dve, m - 1, 1)
                for u in range(2):
                    w = 2 * m + u
                    st = a_stat[:, w % 4]
                    dve.wait_ge(exp_done, w + 1)
                    dve.reciprocal(st[:, 3:4], st[:, 2:3]).then_inc(recip_done, 1)
                    dve.wait_ge(recip_done, w + 1)
                    dve.tensor_scalar(p_sb[:, w % 4, 0:n], p_sb[:, w % 4, 0:n], st[:, 3:4], None, ALU.mult).then_inc(p_done, 1)
                if m - 2 in last_of_head:
                    o_copy(dve, m - 2, 1)
                    o_split(dve, m - 2)
            pT_copy(dve, len(units) - 1, 1)
            o_copy(dve, len(units) - 1, 1)
            o_split(dve, len(units) - 1)

            for g in range(NG):
                dve.wait_ge(mix_mm, g + 1)
                for s in range(2):
                    dve.tensor_scalar(pool_hi[:, g, FIRST[s] * P:FIRST[s] * P + SEQS[s]], ps[:, 4 + 2 * (g % 2) + s, 0:SEQS[s]],
                                      g_pool[:, g:g + 1], None, ALU.mult).then_inc(mix_done, 1)
                for s in range(2):
                    place = slice(FIRST[s] * P, FIRST[s] * P + SEQS[s])
                    dve.wait_ge(mix_done, 4 * g + s + 1)
                    dve.scalar_tensor_tensor(out=pool_lo[g // 2][:, g % 2, place], in0=ps[:, 4 + 2 * (g % 2) + s, 0:SEQS[s]],
                                             scalar=g_pool[:, g:g + 1], in1=pool_hi[:, g, place].bitcast(F32),
                                             op0=ALU.mult, op1=ALU.subtract).then_inc(mix_done, 1)

            RF = route_f
            dve.wait_ge(d_mm, NG)
            dve.memset(RF[:, 128:136], -3e38).then_inc(bf_set, 1)
            dve.wait_ge(g_ffn_in, 48)

            def residual(i):
                dve.wait_ge(x_res_in, 16 * (i + 1))
                if i >= 2:
                    dve.wait_ge(h_stored, 16 * (i - 1))
                    dve.wait_ge(a2_done, i - 1)
                    dve.wait_ge(h_sq, i - 1)
                for n in range(2):
                    dve.wait_ge(o_mm, 2 * i + n + 1)
                    dve.tensor_tensor(h_sb[:, i % 2, n * 512:(n + 1) * 512], ps[:, 2 * (i % 2) + n, :], x_res[:, n * 512:(n + 1) * 512],
                                      ALU.add).then_inc(h_done, 1)

            def second_norm(i):
                dve.wait_ge(h_rstd, i + 1)
                if i >= 2:
                    dve.wait_ge(rows_stored, 16 * (i - 1))
                    dve.wait_ge(a2_tr, i - 1)
                dve.scalar_tensor_tensor(out=rows[:, i % 2, 0:D].rearrange("t (k p) -> t p k", k=KD),
                                         in0=h_sb[:, i % 2, :].rearrange("t (p k) -> t p k", k=KD), scalar=route_f[:, 402:403],
                                         in1=g_ffn[:, :].rearrange("t (p k) -> t p k", k=KD), op0=ALU.mult, op1=ALU.mult).then_inc(a2_done, 1)

            def route(i):
                def step(ins):
                    link("route", route_step, ins)

                dve.wait_ge(lg_mm, i + 1)
                if i >= 1:
                    dve.wait_ge(g_exp, i)
                if i == 0:
                    dve.wait_ge(bf_set, 4)
                step(dve.tensor_tensor(RF[:, 128:128 + EG], ps[:, 7, 0:EG], r_bias[:, 0:EG], ALU.add))
                dve.tensor_tensor(RF[:, 0:E], ps[:, 7, EG:EG + E], r_bias[:, EG:], ALU.add).then_inc(lg_bias, 1)
                step(dve.max(RF[:, 136:144], RF[:, 128:136]))
                dve.tensor_scalar(RF[:, 176:177], RF[:, 136:137], -1.0, None, ALU.mult).then_inc(neg_g, 1)
                step(dve.max_index(route_u[:, 0:8], RF[:, 136:144], RF[:, 128:136]))
                dve.wait_ge(lg_bias, i + 1)
                step(dve.tensor_copy(RF[:, 180:181], route_u[:, 0:1]))
                step(dve.tensor_scalar(RF[:, 168:172], iota[:, 0:EG], RF[:, 180:181], -BIG, ALU.not_equal, ALU.mult))
                step(dve.tensor_tensor(RF[:, 192:192 + E].rearrange("t (g e) -> t g e", g=EG),
                                       RF[:, 0:E].rearrange("t (g e) -> t g e", g=EG),
                                       RF[:, 168:172].unsqueeze(2).to_broadcast([P, EG, EPG]), ALU.add))
                step(dve.max(RF[:, 144:152], RF[:, 192:192 + E]))
                dve.tensor_tensor(RF[:, 178:179], RF[:, 145:146], RF[:, 144:145], ALU.subtract).then_inc(e_diff, 1)
                step(dve.max_index(route_u[:, 8:16], RF[:, 144:152], RF[:, 192:192 + E]))
                step(dve.tensor_copy(RF[:, 182:184], route_u[:, 8:10]))
                if i >= 1:
                    dve.wait_ge(rank_mm, i)
                    dve.wait_ge(pos_done, i)
                dve.tensor_scalar(RF[:, 224:224 + E], iota, RF[:, 182:183], None, ALU.is_equal)
                step(dve.tensor_scalar(RF[:, 256:256 + E], iota, RF[:, 183:184], None, ALU.is_equal))
                dve.tensor_tensor(m_sum[:, 1, :], RF[:, 224:224 + E], RF[:, 256:256 + E], ALU.add).then_inc(mask_done, 1)

            def route_weights(i):
                def step(ins):
                    link("route", route_step, ins)

                dve.wait_ge(e_exp, i + 1)
                dve.wait_ge(g_exp, i + 1)
                step(dve.tensor_scalar(RF[:, 184:185], RF[:, 179:180], 1.0, RF[:, 177:178], ALU.add, ALU.mult))
                step(dve.reciprocal(RF[:, 185:186], RF[:, 184:185]))
                step(dve.tensor_tensor(RF[:, 186:187], RF[:, 185:186], RF[:, 179:180], ALU.mult))
                step(dve.tensor_scalar(RF[:, 288:288 + E], RF[:, 256:256 + E], RF[:, 186:187], None, ALU.mult))
                dve.scalar_tensor_tensor(out=rows[:, i % 2, D:ROW], in0=RF[:, 224:224 + E], scalar=RF[:, 185:186],
                                         in1=RF[:, 288:288 + E], op0=ALU.mult, op1=ALU.add).then_inc(gates_done, 1)

            def positions(i):
                def step(ins):
                    link("route", route_step, ins)

                dve.wait_ge(rank_mm, i + 1)
                dve.wait_ge(mask_done, i + 1)
                rank = ps[:, 6, 128:128 + E]
                ri, rs = route_i[:, 0, :], route_i[:, 1, :]
                step(dve.tensor_copy(ri, rank))
                step(dve.tensor_scalar(rs, ri, 6, None, ALU.arith_shift_right))
                step(dve.tensor_copy(RF[:, 320:320 + E], rs))
                step(dve.scalar_tensor_tensor(out=RF[:, 352:352 + E], in0=rank, scalar=float(PAIRS), in1=ebase,
                                              op0=ALU.mult, op1=ALU.add))
                step(dve.scalar_tensor_tensor(out=RF[:, 352:352 + E], in0=RF[:, 320:320 + E], scalar=float(BLOCK - LANE * PAIRS),
                                              in1=RF[:, 352:352 + E], op0=ALU.mult, op1=ALU.add))
                for c in range(2):
                    oh = RF[:, 224 + E * c:224 + E * c + E]
                    step(dve.tensor_tensor_reduce(out=RF[:, 320:320 + E], in0=oh, in1=RF[:, 352:352 + E], scale=1.0, scalar=0.0,
                                                  op0=ALU.mult, op1=ALU.add, accum_out=RF[:, 390 + c:391 + c]))
                step(dve.tensor_copy(idx_pos[:, i, :], RF[:, 390:392]))
                dve.tensor_tensor(m_sum[:, 0, :], m_sum[:, 0, :], m_sum[:, 1, :], ALU.add).then_inc(pos_done, 1)

            for i in range(NT):
                residual(i)
                if i >= 2:
                    positions(i - 2)
                second_norm(i)
                if i >= 1:
                    route(i - 1)
                    route_weights(i - 1)
            positions(NT - 2)
            route(NT - 1)
            positions(NT - 1)
            route_weights(NT - 1)

            dve.wait_ge(total_mm, 1)
            dve.wait_ge(gates_done, NT)
            c = RF[0:1, 224:224 + E]
            link("route", route_step, dve.tensor_copy(c, ps[0:1, 7, 0:E]))
            cp = c.rearrange("t (l j) -> t l j", l=2)
            link("route", route_step, dve.tensor_tensor(RF[0:1, 256:256 + PAIRS], cp[:, 0, :], cp[:, 1, :], ALU.max))
            link("route", route_step, dve.tensor_scalar(RF[0:1, 288:288 + PAIRS], RF[0:1, 256:256 + PAIRS], -1.0, 0.0, ALU.add, ALU.max))
            link("route", route_step, dve.tensor_copy(counts_i[0:1, 0, :], RF[0:1, 288:288 + PAIRS]))
            dve.tensor_scalar(counts_i[0:1, 3, :], counts_i[0:1, 0, :], 6, None, ALU.arith_shift_right).then_inc(counts_done, 1)

            dve.wait_ge(counts_done, 1)

            def x_copy(q, n):
                dve.wait_ge(q.x_tr, n + 1)
                bank = 1 if q is main else 7
                dve.tensor_copy(xT[:, q.o, 4:8, :], ps[:, bank, :].rearrange("p (k t) -> p k t", k=4)).then_inc(q.x_dve, 1)

            def gates(q, src, j, n, g):
                for lane in range(2):
                    r = slice(lane * LANE, (lane + 1) * LANE)
                    dve.tensor_copy(gate[r, g:g + 1], src[r, bass.ds(j + D + PAIRS * lane, 1)]).then_inc(q.gate_done, 1)

            def hidden(q, n, g):
                dve.wait_ge(q.silu_done, n + 1)
                dve.wait_ge(q.gate_done, 2 * (n + 1))
                dve.scalar_tensor_tensor(out=hid[:, q.o, :, :].rearrange("t k p -> t p k"),
                                         in0=s_act[:, q.o, :].rearrange("t (p k) -> t p k", k=2), scalar=gate[:, g:g + 1],
                                         in1=ps[:, 2, FH:2 * FH].rearrange("t (p k) -> t p k", k=2),
                                         op0=ALU.mult, op1=ALU.mult).then_inc(q.hid_done, 1)

            def hT_copy(q, n):
                dve.wait_ge(q.h_tr, n + 1)
                dve.tensor_copy(hT[:, q.o, :, :], ps[:, 3, 0:FH].rearrange("p (k t) -> p k t", k=2)).then_inc(q.hT_done, 1)

            def y_copy(q, n, buf):
                dve.wait_ge(q.y_mm, n + 1)
                y_free(dve, q, n)
                dve.tensor_copy(y_sb[:, buf, 512:1024], ps[:, 5, :]).then_inc(q.y_dve, 1)

            more_passes = passes_counter(dve)

            def pair(j, i, b, last):
                hidden(main, j, b)
                if not last:
                    nb = (b + 1) % 3
                    dve.wait_ge(main.gathered[nb], 16 * (i + 1 if b < 2 else i + 2))
                    gates(main, g_rows[:, nb, :], j + 1, j + 1, nb)
                    x_copy(main, j + 1)
                hT_copy(main, j)
                y_copy(main, j, b)

                def again(n, p):
                    dve.wait_ge(over.gathered[0], 16 * (n + 1))
                    gates(over, more_rows[:, :], j, n, 3)
                    x_copy(over, n)
                    hidden(over, n, 3)
                    hT_copy(over, n)
                    y_copy(over, n, 3)

                more_passes(j, again)

            dve.wait_ge(main.gathered[0], 16)
            gates(main, g_rows[:, 0, :], 0, 0, 0)
            x_copy(main, 0)
            run_pairs(dve, pair)

        @block.gpsimd
        def _(pool):
            pool.memset(neg_half[:, :], -0.5).then_inc(neg_half_set, 1)
            pool.wait_ge(neg_half_set, 1)

            S = stats

            def x_part(i):
                pool.wait_ge(x_sq, i + 1)
                pool.tensor_scalar(S[:, 1:2], S[:, 0:1], 1.0 / D, EPS, ALU.mult, ALU.add).then_inc(x_ms, 1)
                pool.wait_ge(x_ms, i + 1)
                if i >= 1:
                    pool.wait_ge(xn_done, i)
                pool.tensor_tensor(S[:, 2:3], S[:, 1:2], neg_half[:, 0:1], ALU.pow).then_inc(x_rstd, 1)

            x_part(0)
            for i in range(NT):
                if i + 1 < NT:
                    x_part(i + 1)
                pool.wait_ge(c_sq, 3 * (i + 1))
                pool.tensor_scalar(S[:, 10:11], S[:, 4:5], 1.0 / RQ, EPS, ALU.mult, ALU.add).then_inc(c_ms, 1)
                pool.tensor_scalar(S[:, 11:12], S[:, 5:6], 1.0 / RKV, EPS, ALU.mult, ALU.add).then_inc(c_ms, 1)
                pool.wait_ge(c_ms, 2 * (i + 1))
                if i >= 1:
                    pool.wait_ge(cn_done, 2 * i)
                pool.tensor_tensor(S[:, 8:10], S[:, 10:12], neg_half[:, 0:2], ALU.pow).then_inc(c_rstd, 1)
                pool.wait_ge(q_ss, i + 1)
                pool.tensor_scalar(S[:, 16:20], S[:, 12:16], 1.0 / DQK, EPS, ALU.mult, ALU.add).then_inc(q_ms, 1)
                pool.wait_ge(q_ms, i + 1)
                if i >= 1:
                    pool.wait_ge(qn_done, i)
                pool.tensor_tensor(S[:, 20:24], S[:, 16:20], neg_half[:, 0:4], ALU.pow).then_inc(q_rstd, 1)
                pool.wait_ge(k_ss, i + 1)
                pool.tensor_scalar(S[:, 32:36], S[:, 28:32], S[:, 6:7], 1.0 / DQK, ALU.add, ALU.mult).then_inc(k_ms, 1)
                pool.wait_ge(k_ms, i + 1)
                pool.tensor_scalar(S[:, 36:40], S[:, 32:36], EPS, None, ALU.add).then_inc(k_eps, 1)
                pool.wait_ge(k_eps, i + 1)
                if i >= 1:
                    pool.wait_ge(kr_done, i)
                pool.tensor_tensor(S[:, 40:44], S[:, 36:40], neg_half[:, 0:4], ALU.pow).then_inc(k_rstd, 1)

            pool.wait_ge(qr_done, NT)
            for k in range(KD):
                pool.wait_ge(w_out_hi_done, k + 1)
                pool.tensor_tensor(w_out_lo[:, k, :], w_out_raw[k % 3][:, :], w_out_hi[:, k, :].bitcast(F32),
                                   ALU.subtract).then_inc(w_out_lo_done, 1)

            pool.wait_ge(setup_dram, 48)

            def fill_slots(i):
                pool.wait_ge(pos_done, i + 1)
                for c in range(2):
                    pool.indirect_dma_start(
                        out=slot_table, out_offset=bass.IndirectOffsetOnAxis(ap=idx_pos[:, i, c:c + 1], axis=0),
                        in_=tok_ids[:, i:i + 1], in_offset=None).then_inc(slots_stored, 16)

            for i in range(NT):
                pool.wait_ge(h_sq, i + 1)
                pool.tensor_scalar(route_f[:, 401:402], route_f[:, 400:401], 1.0 / D, EPS, ALU.mult, ALU.add).then_inc(h_ms, 1)
                pool.wait_ge(h_ms, i + 1)
                if i >= 1:
                    pool.wait_ge(a2_done, i)
                pool.tensor_tensor(route_f[:, 402:403], route_f[:, 401:402], neg_half[:, 0:1], ALU.pow).then_inc(h_rstd, 1)
                if i >= 2:
                    fill_slots(i - 2)
            fill_slots(NT - 2)
            fill_slots(NT - 1)

            pool.wait_ge(idx_in, 16)
            pool.wait_ge(rows_stored, 16 * NT)
            pool.wait_ge(h_stored, 16 * NT)
            pool.wait_ge(counts_done, 1)

            def gather(dst, idx, done):
                pool.indirect_dma_start(out=dst, out_offset=None, in_=table,
                                        in_offset=bass.IndirectOffsetOnAxis(ap=idx, axis=0)).then_inc(done, 16)

            def ready(*waits):
                for signal, value in waits:
                    pool.wait_ge(signal, value)
                pool.sem_inc(dma_go, 1)

            def set_idx(col, j):
                pool.tensor_copy(idx_now[:, col:col + 1], idx_all[:, bass.ds(j, 1)]).then_inc(idx_set, 1)

            def gather_pair(j, b, count):
                set_idx(b, j)
                ready((idx_set, count))
                gather(g_rows[:, b, :], idx_now[:, b:b + 1], main.gathered[b])

            def add_rows(q, n, buf, idx):
                pool.indirect_dma_start(out=out, out_offset=bass.IndirectOffsetOnAxis(ap=idx, axis=0),
                                        in_=y_sb[:, buf, :], in_offset=None, compute_op=ALU.add).then_inc(q.added, 16)

            def more_gather(j, p):
                src = slot_table.rearrange("(a s j) c -> a s (j c)", s=2 * LANE, j=PAIRS)
                with nc.allow_non_contiguous_dma(reason="128 indices"):
                    pool.dma_start(idx_now[:, 6:7], src[bass.ds(p, 1), :, bass.ds(j, 1)].rearrange("a s c -> (a s) c")).then_inc(over_idx_in, 16)
                m = pool.snap(loaded)
                ready((over_idx_in, 16 * (m + 1)))
                pool.reg_add(loaded, loaded, 1)
                gather(more_rows[:, :], idx_now[:, 6:7], over.gathered[0])

            def first_more_gather(j):
                todo = pool.value_load(counts_i[0:1, 3, bass.ds(j, 1)], min_val=0, max_val=PASSES - 1)
                with pool.If(todo > 0):
                    pool.tensor_copy(idx_now[:, 6:7], idx_more[:, bass.ds(j, 1)]).then_inc(more_set, 1)
                    m = pool.snap(firsts)
                    ready((more_set, m + 1))
                    pool.reg_add(firsts, firsts, 1)
                    gather(more_rows[:, :], idx_now[:, 6:7], over.gathered[0])

            def more_add(j, n):
                ready((over.y_act, n + 1), (over.y_dve, n + 1), (main.added, 16 * (j + 1)))
                add_rows(over, n, 3, idx_now[:, 6:7])
                pool.wait_ge(over.added, 16 * (n + 1))

            before, loaded, firsts = (pool.alloc_register(n) for n in ("more_before", "more_loaded", "more_firsts"))
            for r in (before, loaded, firsts):
                pool.reg_mov(r, 0)

            def pair(j, i, b, last):
                if not last:
                    if not (isinstance(j, int) and j == 0):
                        pool.wait_ge(main.x_tr, j)
                        pool.wait_ge(main.gate_done, 2 * j)
                    gather_pair(j + 2, (b + 2) % 3, 2 * j + 3)
                set_idx(3 + b, j)
                waits = [(idx_set, add_count(j)), (main.y_act, j + 1), (main.y_dve, j + 1)]
                if not (isinstance(j, int) and j == 0):
                    waits.append((main.added, 16 * j))
                ready(*waits)
                add_rows(main, j, b, idx_now[:, 3 + b:4 + b])

                todo = pool.value_load(counts_i[0:1, 3, bass.ds(j, 1)], min_val=0, max_val=PASSES - 1)
                with pool.If(todo > 0):
                    with pool.If(todo > 1):
                        with pool.Fori(1, todo) as p:
                            n = pool.snap(before)
                            more_add(j, n)
                            more_gather(j, p + 1)
                            pool.reg_add(before, before, 1)
                    more_add(j, pool.snap(before))
                    pool.reg_add(before, before, 1)
                if not last:
                    first_more_gather(j + 1)

            def add_count(j):
                return 2 * PAIRS + 1 if isinstance(j, int) and j == PAIRS - 1 else 2 * j + 4

            gather_pair(0, 0, 1)
            pool.wait_ge(idx_rest_in, 32)
            first_more_gather(0)
            gather_pair(1, 1, 2)
            run_pairs(pool, pair)
            pool.wait_ge(main.added, 16 * PAIRS)
            pool.wait_ge(main.gathered[PAIRS % 3], 16 * (PAIRS // 3 + 1))


_INS = ["x_prompt", "x_sample", "g_attn_norm", "w_in", "g_q_lat", "g_kv_lat", "w_uq", "w_ukv", "g_q_head", "g_k_head",
        "w_pool", "pool_scale", "w_out", "g_ffn_norm", "w_group_router", "b_group_router", "w_expert_router",
        "b_expert_router", "w_gate", "w_up", "w_down"]


def kernel(**inputs):
    import concourse.bacc as _bacc
    from concourse.bass_utils import run_bass_kernel_spmd as _run

    nc = _bacc.Bacc("TRN2", target_bir_lowering=False, num_devices=1)
    arrays, args = {}, {}
    named = {name: inputs[name] for name in _INS}
    named.update(host_constants())
    for name, x in named.items():
        x = np.ascontiguousarray(x)
        arrays[f"in_{name}"] = x
        args[name] = nc.dram_tensor(f"in_{name}", x.shape, mybir.dt.from_np(x.dtype), kind="ExternalInput").ap()
    out = nc.dram_tensor("out", [T + P, D], F32, kind="ExternalOutput").ap()
    build(nc, args, out)
    r = _run(nc, [arrays], core_ids=[0])
    y = np.asarray(r.results[0]["out"])
    return y[0:SEQS[0]].reshape(1, SEQS[0], D), y[SEQS[0]:T].reshape(1, SEQS[1], D)
```
